# Optimizing a Trainium2 kernel written in Bass

```python
import jax, jax.numpy as jnp
from jax import lax
import numpy as np
import math

D_MODEL = 2048
BATCH = 1
SEQ = 512
DEPTH = 1

CHUNK = 64
MIX_WIDTH = D_MODEL
ATT_WIDTH = MIX_WIDTH // 2
HG_WIDTH = MIX_WIDTH - ATT_WIDTH
ATT_HEAD_DIM = 128
ATT_HEADS = ATT_WIDTH // ATT_HEAD_DIM
ATT_LEFT_CHUNKS = 8
ATT_BAND = ATT_LEFT_CHUNKS + 1
MAX_REL = 128
HG_EXPAND = 128
HG_HEADS = HG_WIDTH // HG_EXPAND
HG_KDIM = HG_EXPAND
HG_FDIM = HG_HEADS * HG_KDIM
HG_VDIM = HG_WIDTH // HG_HEADS
IN_SPLITS = (ATT_WIDTH, ATT_WIDTH, ATT_WIDTH, ATT_WIDTH, HG_FDIM, HG_FDIM, HG_WIDTH, HG_WIDTH)
IN_COLS = sum(IN_SPLITS)
EPS = 1e-6


def _rms(x, g):
    xf = x.astype(jnp.float32)
    y = xf * lax.rsqrt(jnp.mean(xf * xf, axis=-1, keepdims=True) + EPS)
    return (y * g.astype(jnp.float32)).astype(x.dtype)

def _chunk_attention(q, k, v, q_g, k_g, rel_bias):
    B, T, H, dh = q.shape
    N = T // CHUNK
    q = _rms(q, q_g).reshape(B, N, CHUNK, H, dh)
    k = _rms(k, k_g).reshape(B, N, CHUNK, H, dh)
    v = v.reshape(B, N, CHUNK, H, dh)
    pad = ((0, 0), (ATT_LEFT_CHUNKS, 0), (0, 0), (0, 0), (0, 0))
    kp = jnp.pad(k, pad)
    vp = jnp.pad(v, pad)
    band_idx = jnp.arange(N)[:, None] + jnp.arange(ATT_BAND)[None, :]
    kb = kp[:, band_idx].reshape(B, N, ATT_BAND * CHUNK, H, dh)
    vb = vp[:, band_idx].reshape(B, N, ATT_BAND * CHUNK, H, dh)
    scores = jnp.einsum('bnqhd,bnkhd->bnhqk', q, kb).astype(jnp.float32) * (dh ** -0.5)
    qi = jnp.arange(CHUNK)
    kj = jnp.arange(ATT_BAND * CHUNK)
    dist = ATT_LEFT_CHUNKS * CHUNK + qi[:, None] - kj[None, :]
    bias_idx = jnp.clip(dist, -MAX_REL, MAX_REL) + MAX_REL
    bias = rel_bias.astype(jnp.float32)[:, bias_idx]
    valid = (jnp.arange(N)[:, None] + kj[None, :] // CHUNK) >= ATT_LEFT_CHUNKS
    scores = jnp.where(valid[None, :, None, None, :], scores + bias[None, None], -jnp.inf)
    p = jax.nn.softmax(scores, axis=-1).astype(v.dtype)
    out = jnp.einsum('bnhqk,bnkhd->bnqhd', p, vb)
    return out.reshape(B, T, H * dh)

def _hgrn2(q_raw, f_raw, i, lb, o_g):
    B, T, _ = q_raw.shape
    N = T // CHUNK
    out_dtype = i.dtype
    f32 = jnp.float32
    q = jax.nn.silu(q_raw.astype(f32))
    fr = f_raw.astype(f32)
    lb = lb.astype(f32)
    logf = jnp.log(lb + (1.0 - lb) * jax.nn.sigmoid(fr))
    k = (1.0 - lb) * jax.nn.sigmoid(-fr)
    v = i.astype(f32)

    def to_chunks(a, d):
        return a.reshape(B, N, CHUNK, HG_HEADS, d).transpose(1, 0, 3, 2, 4)

    qc, kc, lc = to_chunks(q, HG_KDIM), to_chunks(k, HG_KDIM), to_chunks(logf, HG_KDIM)
    vc = to_chunks(v, HG_VDIM)
    tril = jnp.arange(CHUNK)[:, None] >= jnp.arange(CHUNK)[None, :]

    def step(S, xs):
        qn, kn, vn, ln = xs
        b = jnp.cumsum(ln, axis=2)
        b_last = b[:, :, -1]
        inter = jnp.einsum('bhcd,bhde->bhce', qn * jnp.exp(b), S)
        diff = b[:, :, :, None, :] - b[:, :, None, :, :]
        decay = jnp.exp(jnp.where(tril[None, None, :, :, None], diff, -jnp.inf))
        A = jnp.einsum('bhtd,bhtsd,bhsd->bhts', qn, decay, kn)
        intra = jnp.einsum('bhts,bhse->bhte', A, vn)
        k_dec = kn * jnp.exp(b_last[:, :, None, :] - b)
        S_new = jnp.exp(b_last)[..., None] * S + jnp.einsum('bhsd,bhse->bhde', k_dec, vn)
        return S_new, inter + intra

    S0 = jnp.zeros((B, HG_HEADS, HG_KDIM, HG_VDIM), f32)
    _, o = lax.scan(step, S0, (qc, kc, vc, lc))
    o = o.transpose(1, 0, 3, 2, 4).reshape(B, T, HG_HEADS, HG_VDIM)
    o = _rms(o, o_g)
    return o.reshape(B, T, HG_WIDTH).astype(out_dtype)

def first_inputs(seed: int = 0) -> dict:
    key = jax.random.key(seed)
    ks = jax.random.split(key, 16)
    D = D_MODEL
    f32 = jnp.float32
    nrm = lambda k, s: jax.random.normal(k, s, f32)
    return {
        "x": nrm(ks[0], (BATCH, SEQ, D)),
        "c": nrm(ks[1], (BATCH, D)),
        "norm_g": 1.0 + 0.1 * nrm(ks[2], (DEPTH, D)),
        "w_ada": nrm(ks[3], (DEPTH, D, 3 * D)) * D ** -0.5,
        "b_ada": 0.01 * nrm(ks[4], (DEPTH, 3 * D)),
        "w_in": nrm(ks[5], (DEPTH, D, IN_COLS)) * D ** -0.5,
        "q_norm_g": 1.0 + 0.1 * nrm(ks[6], (DEPTH, ATT_HEAD_DIM)),
        "k_norm_g": 1.0 + 0.1 * nrm(ks[7], (DEPTH, ATT_HEAD_DIM)),
        "rel_bias": 0.5 * nrm(ks[8], (DEPTH, ATT_HEADS, 2 * MAX_REL + 1)),
        "lower_bounds": nrm(ks[9], (DEPTH + 1, HG_FDIM)),
        "hg_norm_g": 1.0 + 0.1 * nrm(ks[10], (DEPTH, HG_VDIM)),
        "w_out": nrm(ks[11], (DEPTH, MIX_WIDTH, D)) * MIX_WIDTH ** -0.5,
    }

def first_block(x, c, norm_g, w_ada, b_ada, w_in, q_norm_g, k_norm_g, rel_bias,
              lower_bounds, hg_norm_g, w_out):
    B, T, D = x.shape
    lbs = jnp.cumsum(jax.nn.softmax(lower_bounds.astype(jnp.float32), axis=0), axis=0)
    offsets = np.cumsum(IN_SPLITS)[:-1].tolist()
    c_act = jax.nn.silu(c)
    for l in range(DEPTH):
        mod = c_act @ w_ada[l] + b_ada[l]
        shift, scale, gate = jnp.split(mod, 3, axis=-1)
        h = _rms(x, norm_g[l]) * (1.0 + scale[:, None, :]) + shift[:, None, :]
        proj = h @ w_in[l]
        a_q, a_k, a_v, a_z, g_q, g_f, g_i, g_z = jnp.split(proj, offsets, axis=-1)
        hs = (B, T, ATT_HEADS, ATT_HEAD_DIM)
        att = _chunk_attention(a_q.reshape(hs), a_k.reshape(hs), a_v.reshape(hs),
                               q_norm_g[l], k_norm_g[l], rel_bias[l])
        att = att * jax.nn.silu(a_z)
        hg = _hgrn2(g_q, g_f, g_i, lbs[l], hg_norm_g[l]) * jax.nn.silu(g_z)
        y = jnp.concatenate([att, hg], axis=-1) @ w_out[l]
        x = x + gate[:, None, :] * y
    return x


MEM_LEN = 256
A_HEADS = 6
A_HEAD_DIM = 128
A_KV_RANK = 256
IDX_HEADS = 16
IDX_DIM = 64
TOPK_MAX = 256
Q_BLOCK = 128
B_HEADS = 12
B_KV_HEADS = 2
B_HEAD_DIM = 64
WINDOW = 128
BAND_BLOCK = 128
C_HEADS = 4
C_HEAD_DIM = 128
NUM_BUCKETS = 32
MAX_DISTANCE = 128

A_WIDTH = A_HEADS * A_HEAD_DIM
B_WIDTH = B_HEADS * B_HEAD_DIM
B_KV_WIDTH = B_KV_HEADS * B_HEAD_DIM
C_WIDTH = C_HEADS * C_HEAD_DIM
N_BRANCH = 3
IN_SIZES = (A_WIDTH, A_KV_RANK, IDX_HEADS * IDX_DIM, IDX_DIM, IDX_HEADS, A_WIDTH,
            B_WIDTH, B_KV_WIDTH, B_KV_WIDTH, B_WIDTH,
            C_WIDTH, C_WIDTH,
            N_BRANCH * D_MODEL)
IN_COLS_2 = sum(IN_SIZES)


def rmsnorm(x, g):
    xf = x.astype(jnp.float32)
    y = xf * lax.rsqrt(jnp.mean(xf * xf, axis=-1, keepdims=True) + EPS)
    return (y * g.astype(jnp.float32)).astype(x.dtype)

def layernorm(x, g, b):
    xf = x.astype(jnp.float32)
    mu = jnp.mean(xf, axis=-1, keepdims=True)
    var = jnp.mean(jnp.square(xf - mu), axis=-1, keepdims=True)
    y = (xf - mu) * lax.rsqrt(var + EPS)
    return (y * g.astype(jnp.float32) + b.astype(jnp.float32)).astype(x.dtype)

def split_cols(y, sizes):
    cuts = np.cumsum(np.array(sizes))[:-1].tolist()
    return jnp.split(y, cuts, axis=-1)

def t5_bucket(dist):
    n = jnp.maximum(dist, 0)
    max_exact = NUM_BUCKETS // 2
    nf = jnp.maximum(n, 1).astype(jnp.float32)
    large = max_exact + (jnp.log(nf / max_exact) / math.log(MAX_DISTANCE / max_exact)
                         * (NUM_BUCKETS - max_exact)).astype(jnp.int32)
    large = jnp.minimum(large, NUM_BUCKETS - 1)
    return jnp.where(n < max_exact, n, large)

def dsa_attention(q, k, v, iq, ik, iw, bias_tab, topk):
    bsz, seq, nh, dh = q.shape
    nb = seq // Q_BLOCK
    key_pos = jnp.arange(seq, dtype=jnp.int32)

    def to_blocks(t):
        return jnp.moveaxis(t.reshape((bsz, nb, Q_BLOCK) + t.shape[2:]), 1, 0)

    def block_fn(args):
        qb, iqb, iwb, t0 = args
        tpos = t0 + jnp.arange(Q_BLOCK, dtype=jnp.int32)
        rel = jax.nn.relu(jnp.einsum('bthd,bsd->bths', iqb, ik))
        score = jnp.einsum('bths,bth->bts', rel, iwb).astype(jnp.float32)
        causal = key_pos[None, :] <= tpos[:, None]
        score = jnp.where(causal[None], score, -jnp.inf)
        _, idx = lax.top_k(score, topk)
        kg = jax.vmap(lambda kk, ii: kk[ii])(k, idx)
        vg = jax.vmap(lambda vv, ii: vv[ii])(v, idx)
        logits = jnp.einsum('bthd,btkhd->bthk', qb, kg).astype(jnp.float32) * (dh ** -0.5)
        dist = tpos[None, :, None] - idx
        bias = jnp.transpose(bias_tab[t5_bucket(dist)], (0, 1, 3, 2)).astype(jnp.float32)
        logits = jnp.where((dist >= 0)[:, :, None, :], logits + bias, -jnp.inf)
        p = jax.nn.softmax(logits, axis=-1).astype(vg.dtype)
        return jnp.einsum('bthk,btkhd->bthd', p, vg)

    t0s = jnp.arange(nb, dtype=jnp.int32) * Q_BLOCK
    out = lax.map(block_fn, (to_blocks(q), to_blocks(iq), to_blocks(iw), t0s))
    return jnp.moveaxis(out, 0, 1).reshape(bsz, seq, nh * dh)

def sliding_window_attention(q, k, v, sinks, bias_tab):
    bsz, seq, hq, dh = q.shape
    hkv = k.shape[2]
    g = hq // hkv
    blk = BAND_BLOCK
    nb = seq // blk
    qb = q.reshape(bsz, nb, blk, hkv, g, dh)

    def band(t):
        tb = t.reshape(bsz, nb, blk, hkv, dh)
        prev = jnp.concatenate([jnp.zeros_like(tb[:, :1]), tb[:, :-1]], axis=1)
        return jnp.concatenate([prev, tb], axis=2)

    kband, vband = band(k), band(v)
    logits = jnp.einsum('bnqhgd,bnkhd->bnhgqk', qb, kband).astype(jnp.float32) * (dh ** -0.5)
    qi = jnp.arange(blk, dtype=jnp.int32)[:, None]
    kj = jnp.arange(2 * blk, dtype=jnp.int32)[None, :]
    dist = blk + qi - kj
    bias = jnp.transpose(bias_tab[t5_bucket(dist)], (2, 0, 1)).reshape(hkv, g, blk, 2 * blk)
    key_pos = jnp.arange(nb, dtype=jnp.int32)[:, None, None] * blk + kj[None] - blk
    valid = (dist >= 0) & (dist < WINDOW) & (key_pos >= 0)
    logits = jnp.where(valid[None, :, None, None], logits + bias.astype(jnp.float32), -jnp.inf)
    sink = jnp.broadcast_to(sinks.astype(jnp.float32).reshape(hkv, g, 1, 1), logits.shape[:-1] + (1,))
    p = jax.nn.softmax(jnp.concatenate([logits, sink], axis=-1), axis=-1)[..., :-1]
    out = jnp.einsum('bnhgqk,bnkhd->bnqhgd', p.astype(v.dtype), vband)
    return out.reshape(bsz, seq, hq * dh)

def memory_attention(q, k, v):
    bsz, seq, nh, dh = q.shape
    logits = jnp.einsum('bthd,bmhd->bhtm', q, k).astype(jnp.float32) * (dh ** -0.5)
    p = jax.nn.softmax(logits, axis=-1).astype(v.dtype)
    return jnp.einsum('bhtm,bmhd->bthd', p, v).reshape(bsz, seq, nh * dh)

def second_inputs(seed: int = 0) -> dict:
    key = jax.random.key(seed)
    ks = jax.random.split(key, 24)
    f32 = jnp.float32

    def w(k, shape, fan_in):
        return jax.random.normal(k, shape, f32) * (fan_in ** -0.5)

    def gain(k, shape):
        return 1.0 + 0.05 * jax.random.normal(k, shape, f32)

    return {
        "x": jax.random.normal(ks[0], (BATCH, SEQ, D_MODEL), f32),
        "mem": jax.random.normal(ks[1], (BATCH, MEM_LEN, D_MODEL), f32),
        "norm_g": gain(ks[2], (DEPTH, D_MODEL)),
        "w_in": w(ks[3], (DEPTH, D_MODEL, IN_COLS_2), D_MODEL),
        "kv_norm_g": gain(ks[4], (DEPTH, A_KV_RANK)),
        "w_kv_up": w(ks[5], (DEPTH, A_KV_RANK, 2 * A_WIDTH), A_KV_RANK),
        "idx_k_ln_g": gain(ks[6], (DEPTH, IDX_DIM)),
        "idx_k_ln_b": 0.02 * jax.random.normal(ks[7], (DEPTH, IDX_DIM), f32),
        "q_norm_a": gain(ks[8], (DEPTH, A_HEAD_DIM)),
        "k_norm_a": gain(ks[9], (DEPTH, A_HEAD_DIM)),
        "q_norm_b": gain(ks[10], (DEPTH, B_HEAD_DIM)),
        "k_norm_b": gain(ks[11], (DEPTH, B_HEAD_DIM)),
        "sinks_b": 0.5 * jax.random.normal(ks[12], (DEPTH, B_HEADS), f32),
        "mem_norm_g": gain(ks[13], (DEPTH, D_MODEL)),
        "w_mem_kv": w(ks[14], (DEPTH, D_MODEL, 2 * C_WIDTH), D_MODEL),
        "q_norm_c": gain(ks[15], (DEPTH, C_HEAD_DIM)),
        "k_norm_c": gain(ks[16], (DEPTH, C_HEAD_DIM)),
        "w_up_a": w(ks[17], (DEPTH, A_WIDTH, D_MODEL), A_WIDTH),
        "w_up_b": w(ks[18], (DEPTH, B_WIDTH, D_MODEL), B_WIDTH),
        "w_up_c": w(ks[19], (DEPTH, C_WIDTH, D_MODEL), C_WIDTH),
        "gate_bias": 0.02 * jax.random.normal(ks[20], (DEPTH, N_BRANCH * D_MODEL), f32),
        "w_o": w(ks[21], (DEPTH, D_MODEL, D_MODEL), D_MODEL),
        "rel_bias": 0.5 * jax.random.normal(ks[22], (NUM_BUCKETS, A_HEADS + B_HEADS), f32),
    }

def second_block(x, mem, norm_g, w_in, kv_norm_g, w_kv_up, idx_k_ln_g, idx_k_ln_b,
              q_norm_a, k_norm_a, q_norm_b, k_norm_b, sinks_b, mem_norm_g, w_mem_kv,
              q_norm_c, k_norm_c, w_up_a, w_up_b, w_up_c, gate_bias, w_o, rel_bias):
    bsz, seq, _ = x.shape
    mlen = mem.shape[1]
    topk = min(TOPK_MAX, seq // 4)
    bias_a = rel_bias[:, :A_HEADS]
    bias_b = rel_bias[:, A_HEADS:]
    for l in range(DEPTH):
        h = rmsnorm(x, norm_g[l])
        (a_q, a_ckv, i_q, i_k, i_w, a_gate,
         b_q, b_k, b_v, b_gate,
         c_q, c_gate, mix_gate) = split_cols(h @ w_in[l], IN_SIZES)

        ckv = rmsnorm(a_ckv, kv_norm_g[l])
        a_k, a_v = jnp.split(ckv @ w_kv_up[l], 2, axis=-1)
        qa = rmsnorm(a_q.reshape(bsz, seq, A_HEADS, A_HEAD_DIM), q_norm_a[l])
        ka = rmsnorm(a_k.reshape(bsz, seq, A_HEADS, A_HEAD_DIM), k_norm_a[l])
        va = a_v.reshape(bsz, seq, A_HEADS, A_HEAD_DIM)
        iq = i_q.reshape(bsz, seq, IDX_HEADS, IDX_DIM)
        ik = layernorm(i_k, idx_k_ln_g[l], idx_k_ln_b[l])
        iw = i_w * (IDX_HEADS ** -0.5) * (IDX_DIM ** -0.5)
        oa = dsa_attention(qa, ka, va, iq, ik, iw, bias_a, topk) * jax.nn.silu(a_gate)

        qb = rmsnorm(b_q.reshape(bsz, seq, B_HEADS, B_HEAD_DIM), q_norm_b[l])
        kb = rmsnorm(b_k.reshape(bsz, seq, B_KV_HEADS, B_HEAD_DIM), k_norm_b[l])
        vb = b_v.reshape(bsz, seq, B_KV_HEADS, B_HEAD_DIM)
        ob = sliding_window_attention(qb, kb, vb, sinks_b[l], bias_b) * jax.nn.silu(b_gate)

        m_k, m_v = jnp.split(rmsnorm(mem, mem_norm_g[l]) @ w_mem_kv[l], 2, axis=-1)
        qc = rmsnorm(c_q.reshape(bsz, seq, C_HEADS, C_HEAD_DIM), q_norm_c[l])
        kc = rmsnorm(m_k.reshape(bsz, mlen, C_HEADS, C_HEAD_DIM), k_norm_c[l])
        vc = m_v.reshape(bsz, mlen, C_HEADS, C_HEAD_DIM)
        oc = memory_attention(qc, kc, vc) * jax.nn.silu(c_gate)

        g_a, g_b, g_c = jnp.split(jax.nn.sigmoid(mix_gate + gate_bias[l]), N_BRANCH, axis=-1)
        merged = g_a * (oa @ w_up_a[l]) + g_b * (ob @ w_up_b[l]) + g_c * (oc @ w_up_c[l])
        x = x + merged @ w_o[l]
    return x


def setup_inputs(seed=0):
    out = dict(first_inputs(seed))
    for name, value in second_inputs(seed + 1).items():
        if name != "x":
            out[name + "_2"] = value
    return out


def reference(
    x, c, norm_g, w_ada, b_ada, w_in, q_norm_g, k_norm_g, rel_bias, lower_bounds, hg_norm_g,
    w_out, mem_2, norm_g_2, w_in_2, kv_norm_g_2, w_kv_up_2, idx_k_ln_g_2, idx_k_ln_b_2,
    q_norm_a_2, k_norm_a_2, q_norm_b_2, k_norm_b_2, sinks_b_2, mem_norm_g_2, w_mem_kv_2,
    q_norm_c_2, k_norm_c_2, w_up_a_2, w_up_b_2, w_up_c_2, gate_bias_2, w_o_2, rel_bias_2,
):
    x = first_block(
        x, c, norm_g, w_ada, b_ada, w_in, q_norm_g, k_norm_g, rel_bias, lower_bounds, hg_norm_g,
        w_out,
    )
    return second_block(
        x, mem_2, norm_g_2, w_in_2, kv_norm_g_2, w_kv_up_2, idx_k_ln_g_2, idx_k_ln_b_2,
        q_norm_a_2, k_norm_a_2, q_norm_b_2, k_norm_b_2, sinks_b_2, mem_norm_g_2, w_mem_kv_2,
        q_norm_c_2, k_norm_c_2, w_up_a_2, w_up_b_2, w_up_c_2, gate_bias_2, w_o_2, rel_bias_2,
    )


_drawn_inputs = setup_inputs


def setup_inputs(seed=0):
    import zlib

    import numpy as np

    out = dict(_drawn_inputs(seed))
    spreads = {}
    factors = {'b_ada': 5.398,
     'q_norm_g': 8.0,
     'k_norm_g': 8.0,
     'rel_bias': 2.688,
     'lower_bounds': 2.795,
     'norm_g_2': 4.366,
     'kv_norm_g_2': 8.0,
     'idx_k_ln_g_2': 8.0,
     'idx_k_ln_b_2': 8.0,
     'q_norm_a_2': 8.0,
     'k_norm_a_2': 8.0,
     'q_norm_b_2': 8.0,
     'k_norm_b_2': 8.0,
     'sinks_b_2': 200.0,
     'mem_norm_g_2': 8.0,
     'q_norm_c_2': 8.0,
     'k_norm_c_2': 8.0,
     'gate_bias_2': 8.0}
    for name, (base, spread) in spreads.items():
        noise = np.random.default_rng([zlib.crc32(name.encode()), seed]).standard_normal(out[name].shape)
        drawn = base * np.exp(spread * noise) if base else spread * noise
        out[name] = __import__('jax').numpy.asarray(drawn.astype(out[name].dtype))
    for name, factor in factors.items():
        out[name] = (out[name] * factor).astype(out[name].dtype)
    return out
```

```python
from contextlib import ExitStack

import numpy as np

import concourse.bass as bass
from concourse import mybir

F32 = mybir.dt.float32
F32R = mybir.dt.float32r
U8 = mybir.dt.uint8
I32 = mybir.dt.int32
ALU = mybir.AluOpType
ACT = mybir.ActivationFunctionType
AX = mybir.AxisListType.X

P = 128
T = 512
NT = 4
D = 2048
KT = 16
EPS = 1e-6
NEG = -1e30
TOPK = 128
SC128 = float(np.float32(128.0 ** -0.5))
SC64 = 0.125

CST = {}


def _columns():
    at = 0
    for name, n in (("ident", 128), ("ones", 128), ("ones64", 128), ("causal", 128), ("norm_g", 16), ("b_ada", 48),
                    ("q_g", 1), ("k_g", 1), ("hg_g", 1), ("lb", 16), ("norm_g2", 16), ("kv_g", 2), ("ik_g", 1),
                    ("ik_b", 1), ("qa", 1), ("ka", 1), ("qb", 1), ("kb", 1), ("qc", 1), ("kc", 1), ("mem_g", 16),
                    ("gate_b", 48), ("sinks", 12), ("c", 16)):
        CST[name] = (at, n)
        at += n
    return at


NCST = _columns()


class Queue:

    def __init__(self, engine, sem):
        self.e, self.sem, self.n, self.met = engine, sem, 0, {}

    def wait(self, *marks):
        for sem, v in (m for m in marks if m is not None):
            if self.met.get(sem.name, 0) < v:
                self.met[sem.name] = v
                self.e.wait_ge(sem, v)

    def do(self, fn, *marks):
        self.wait(*marks)
        self.n += 1
        fn(self.e).then_inc(self.sem, 1)
        return (self.sem, self.n)

    def quiet(self, fn, *marks):
        self.wait(*marks)
        fn(self.e)

    def dma(self, dst, src, sem):
        self.e.dma_start(dst, src).then_inc(sem, 16)


class Chan:

    def __init__(self, sem):
        self.sem, self.n = sem, 0


class Buf:

    def __init__(self, ap, sem=None):
        self.ap, self.free, self.busy, self.chan = ap, (), False, sem

    def give(self, *marks):
        self.busy = False
        self.free = marks


def program(nc, io):
    with ExitStack() as ctx:
        def sb(name, shape, dt=F32):
            return ctx.enter_context(nc.sbuf_tensor(name, shape, dt))[:, :]

        def sem(name):
            return ctx.enter_context(nc.semaphore(name))

        def chan(name):
            return Chan(sem(name))

        H = [sb("Hhi", [P, KT * T], F32R), sb("Hlo", [P, KT * T], F32R)]
        Y = sb("Y", [P, KT * T])
        TA = sb("TA", [P, 9216])
        NRAW, NSPL = 3, 3
        wraw = [Buf(sb(f"wraw{i}", [P, 1024]), chan(f"s_wraw{i}")) for i in range(NRAW)]
        whi = [sb(f"whi{i}", [P, 1024], F32R) for i in range(NSPL)]
        wlo = [sb(f"wlo{i}", [P, 1024], F32R) for i in range(NSPL)]
        O2 = [sb("Ohi", [P, 6 * T], F32R), sb("Olo", [P, 6 * T], F32R)]
        CK = [sb("CKhi", [P, 2 * T], F32R), sb("CKlo", [P, 2 * T], F32R)]
        cst = sb("cst", [P, NCST])
        mk = sb("mk", [P, 8 * P], U8)
        small = sb("small", [P, 64])
        par = sb("par", [P, 112])
        iww = sb("iww", [P, 256])
        iwr = [sb("iwhi", [P, 256], F32R), sb("iwlo", [P, 256], F32R)]
        iwt = sb("iwt", [P, 64])

        bank = [Buf(ctx.enter_context(nc.psum_tensor(f"bank{i}", [P, 512], F32))[:, :]) for i in range(8)]
        PJ = bank[0:2]
        bST, bS0, bS1, bT, bO, bV = bank[2:8]

        pe, dve, act, pool, sp = (Queue(e, sem(n)) for e, n in (
            (nc.tensor, "s_pe"), (nc.vector, "s_dve"), (nc.scalar, "s_act"), (nc.gpsimd, "s_pool"), (nc.sync, "s_sp")))
        s_cst = [sem(f"s_cst{i}") for i in range(4)]

        def C(name, i=0, n=None):
            at, w = CST[name]
            return cst[:, at + i:at + (w if n is None else i + n)]

        urgent, behind = [], []

        def pump():
            for line in (urgent, behind):
                if line:
                    try:
                        next(line[0])
                    except StopIteration:
                        line.pop(0)

        def drain():
            while urgent or behind:
                pump()

        def take(b):
            while b.busy:
                assert urgent or behind
                pump()
            b.busy = True
            return b

        def get(b):
            while b.busy:
                yield
            b.busy = True

        def load(q, b, dst, src, *marks):
            b.chan.n += 16
            q.wait(*marks)
            q.dma(dst, src, b.chan.sem)
            return (b.chan.sem, b.chan.n)

        for i, (dst, src) in enumerate(((cst, io["cst"]), (TA[:, 8192:9216].bitcast(I32), io["masks"]), (iww, io["w_iw"]))):
            sp.dma(dst, src, s_cst[i])
        m_cst, m_mk, m_iww = [(s_cst[i], 16) for i in range(3)]
        ident, ones, ones64 = C("ident"), C("ones"), C("ones64")

        m_mk = dve.do(lambda e: e.tensor_copy(mk, TA[:, 8192:9216].bitcast(I32)), m_mk)
        m_eps = dve.do(lambda e: e.memset(par[:, 92:93], EPS))
        eps = par[:, 92:93]

        items = []

        def plan(name, first, count, cols=1024):
            for i in range(first, first + count):
                items.append((io[name][i, :, 0:cols], cols, (name, i)))

        class Ring:
            i = n_split = n_dma = 0
            done = {}
            spl_free = [() for _ in range(NSPL)]

            def dma(self):
                j = self.n_dma
                b = wraw[j % NRAW]
                src, w, _ = items[j]
                b.mark = load(sp, b, b.ap[:, 0:w], src, *b.free)
                self.n_dma += 1

            def split(self):
                j = self.n_split
                b, s = wraw[j % NRAW], j % NSPL
                w = items[j][1]
                hi = act.do(lambda e: e.activation(whi[s][:, 0:w], b.ap[:, 0:w], ACT.Copy), b.mark, *self.spl_free[s])
                lo = pool.do(lambda e: e.tensor_tensor(wlo[s][:, 0:w], b.ap[:, 0:w], whi[s][:, 0:w].bitcast(F32),
                                                       ALU.subtract), hi)
                b.free = (hi, lo)
                self.done[j] = lo
                self.n_split += 1

            def take(self, key):
                i = self.i
                assert items[i][2] == key, (items[i][2], key)
                while self.n_dma < min(len(items), NRAW):
                    self.dma()
                while self.n_split < min(len(items), i + NSPL):
                    self.split()
                    if self.n_dma < len(items):
                        self.dma()
                self.i += 1
                return whi[i % NSPL], wlo[i % NSPL], self.done[i], i % NSPL

        ring = Ring()

        class Acts:

            def __init__(self, hi, lo, n, w):
                self.hi = [hi[:, k * w:(k + 1) * w] for k in range(n)]
                self.lo = [lo[:, k * w:(k + 1) * w] for k in range(n)]
                self.ready = [None] * n
                self.used = ()
                self.w = w

            def put(self, k, src, mark, on_dve=False):
                hi = act.do(lambda e: e.activation(self.hi[k], src, ACT.Copy), mark, *self.used)
                q = dve if on_dve else pool
                self.ready[k] = q.do(lambda e: e.tensor_tensor(self.lo[k], src, self.hi[k].bitcast(F32), ALU.subtract), hi)
                return self.ready[k]

        turn = [0]

        def product(x, slots, kts, at=0):
            b = take(PJ[turn[0] % 2])
            turn[0] += 1
            out = b.ap[:, 0:x.w]
            last = len(kts) - 1
            n = 0
            for key, count, off in slots:
                if key is not None:
                    product.cur = ring.take(key)
                hi, lo, there, s = product.cur
                for j in range(count):
                    k = kts[n]
                    wh = hi[:, off + j * P:off + (j + 1) * P]
                    wl = lo[:, off + j * P:off + (j + 1) * P]
                    pe.wait(there, x.ready[k], *(b.free if n == 0 else ()))
                    pe.quiet(lambda e, wh=wh, k=k, n=n: e.matmul(out, wh, x.hi[k], start=(n == 0), stop=False))
                    pe.quiet(lambda e, wh=wh, k=k: e.matmul(out, wh, x.lo[k], start=False, stop=False))
                    end = n == last
                    f = lambda e, wl=wl, k=k, end=end: e.matmul(out, wl, x.hi[k], start=False, stop=end)
                    if end or j == count - 1:
                        m = pe.do(f)
                    else:
                        pe.quiet(f)
                    n += 1
                    if n % 4 == 0 and n <= last:
                        pump()
                ring.spl_free[s] = (m,)
            x.last = m
            pump()
            return b, m

        def full(x, name, nb):
            return product(x, [((name, 2 * nb), 8, 0), ((name, 2 * nb + 1), 8, 0)], list(range(KT)))

        def evac(b, m, dst, w=T, q=None, bias=None):
            if bias is not None:
                r = dve.do(lambda e: e.tensor_scalar(dst.ap[:, 0:w], b.ap[:, 0:w], bias, None, ALU.add), m, *dst.free)
            elif q is dve:
                r = dve.do(lambda e: e.tensor_copy(dst.ap[:, 0:w], b.ap[:, 0:w]), m, *dst.free)
            else:
                r = act.do(lambda e: e.activation(dst.ap[:, 0:w], b.ap[:, 0:w], ACT.Copy), m, *dst.free)
            b.give(r)
            return r

        class Work:

            def __init__(self, mem, t1, t2, sems):
                def piece(i, n=T):
                    return mem[:, i:i + n]
                self.Q = [Buf(piece(T * i), sems[i]) for i in range(2)]
                self.K = [Buf(piece(T * (2 + i)), sems[2 + i]) for i in range(2)]
                self.V = [Buf(piece(T * (4 + i)), sems[4 + i]) for i in range(2)]
                self.Z = [Buf(piece(T * (6 + i))) for i in range(2)]
                self.S = [Buf(piece(T * (8 + i))) for i in range(2)]
                self.PT = [Buf(piece(T * (10 + i))) for i in range(2)]
                self.ST = [Buf(piece(T * (12 + i)), sems[6 + i]) for i in range(2)]
                self.SQ, self.R = Buf(piece(T * 14)), Buf(piece(T * 15))
                self.t1, self.t2 = Buf(t1), Buf(t2)

            def all(self):
                return [*self.Q, *self.K, *self.V, *self.Z, *self.S, *self.PT, *self.ST, self.SQ, self.R]

        w_sems = [chan(f"s_w{i}") for i in range(8)]
        W1 = Work(TA, TA[:, 8192:8704], TA[:, 8704:9216], w_sems)
        W2 = Work(Y, TA[:, 8192:8704], TA[:, 8704:9216], w_sems)

        def rsq(W, w, n, src, mark):
            R = W.R.ap[:, 0:w]
            m = act.do(lambda e: e.activation(R, src, ACT.Ln, scale=1.0 / n, bias=eps), mark, m_eps, *W.R.free)
            return act.do(lambda e: e.activation(R, R, ACT.Exp, scale=-0.5), m), m

        def norm(W, raws, marks, over, n, gains, w=T, out=None):
            yield from get(bST)
            for i, (raw, mark) in enumerate(zip(raws, marks)):
                yield from get(W.SQ)
                m = act.do(lambda e: e.activation(W.SQ.ap[:, 0:w], raw, ACT.Square), mark, *W.SQ.free)
                yield
                m = pe.do(lambda e: e.matmul(bST.ap[:, 0:w], over, W.SQ.ap[:, 0:w], start=(i == 0), stop=(i == len(raws) - 1)),
                          m, m_cst, *bST.free)
                W.SQ.give(m)
            yield from get(W.R)
            r, ln = rsq(W, w, n, bST.ap[:, 0:w], m)
            bST.give(ln)
            for i, (raw, g) in enumerate(zip(raws, gains)):
                marks[i] = dve.do(lambda e: e.scalar_tensor_tensor(out=raw, in0=raw, scalar=g, in1=W.R.ap[:, 0:w],
                                                                   op0=ALU.mult, op1=ALU.mult), r)
            W.R.give(marks[-1])

        def sigma(W, x, mark, signs):
            yield from get(W.t1)
            t1, t2 = W.t1.ap[:, 0:x.shape[1]], W.t2.ap[:, 0:x.shape[1]]
            m = act.do(lambda e: e.activation(t1, x, ACT.Abs), mark, *W.t1.free)
            m = act.do(lambda e: e.activation(t1, t1, ACT.Exp, scale=-1.0), m)
            m = act.do(lambda e: e.activation(t1, t1, ACT.Ln, bias=1.0), m)
            for sign, use in signs:
                yield from get(W.t2)
                if sign > 0:
                    a = dve.do(lambda e: e.scalar_tensor_tensor(out=t2, in0=x, scalar=0.0, in1=t1, op0=ALU.min,
                                                                op1=ALU.subtract), m, *W.t2.free)
                    a = act.do(lambda e: e.activation(t2, t2, ACT.Exp), a)
                else:
                    a = dve.do(lambda e: e.scalar_tensor_tensor(out=t2, in0=x, scalar=0.0, in1=t1, op0=ALU.max,
                                                                op1=ALU.add), m, *W.t2.free)
                    a = act.do(lambda e: e.activation(t2, t2, ACT.Exp, scale=-1.0), a)
                W.t2.give(use(t2, a))
                last = a
            W.t1.give(last, a)

        def silu(W, x, mark, out):
            def use(s, m):
                out[0] = pool.do(lambda e: e.tensor_tensor(x, x, s, ALU.mult), m)
                return out[0]
            yield from sigma(W, x, mark, [(1, use)])

        def turned(W, b, mark, out, n=NT):
            yield from get(bV)
            for i in range(n):
                m = pe.do(lambda e, i=i: e.transpose(bV.ap[:, i * P:(i + 1) * P], b.ap[:, i * P:(i + 1) * P], ident),
                          mark, m_cst, *bV.free)
            out[0] = dve.do(lambda e: e.tensor_copy(b.ap[:, 0:n * P], bV.ap[:, 0:n * P]), m)
            bV.give(out[0])
            yield

        col = [0]

        def scol():
            col[0] = (col[0] + 1) % 64
            return small[:, col[0]:col[0] + 1]

        def softmax_rows(W, sbuf, n, scale, strip, marks, extra=None, sink=None):
            bk, S = sbuf
            src, s = bk.ap[:, 0:n], S.ap[:, 0:n]
            if strip is not None:
                m = dve.do(lambda e: e.scalar_tensor_tensor(out=s, in0=src, scalar=scale, in1=strip, op0=ALU.mult,
                                                            op1=ALU.add), *marks, *S.free)
            else:
                m = dve.do(lambda e: e.tensor_scalar(s, src, scale, None, ALU.mult), *marks, *S.free)
            bk.give(m)
            if extra is not None:
                m = dve.do(lambda e: e.tensor_tensor(s, s, extra, ALU.add), m)
            nm, l, rl = scol(), scol(), scol()
            m = dve.do(lambda e: e.tensor_reduce(nm, s, AX, ALU.max, negate=True), m)
            if sink is not None:
                m = dve.do(lambda e: e.tensor_scalar(nm, nm, sink[1], None, ALU.min), m)
                es = scol()
                x = act.do(lambda e: e.activation(es, sink[0], ACT.Exp, bias=nm), m)
            m = act.do(lambda e: e.activation(s, s, ACT.Exp, bias=nm, accum_out=l), m)
            if sink is not None:
                m = dve.do(lambda e: e.tensor_tensor(l, l, es, ALU.add), m, x)
            m = dve.do(lambda e: e.reciprocal(rl, l), m)
            return dve.do(lambda e: e.tensor_scalar(s, s, rl, None, ALU.mult), m)

        def attention(W, Qb, Kb, Vb, marks, heads, blocks, nkeys, finish):
            yield from get(bO)
            first = [True]
            for rows, vcols, orows, scale, strip, extra, sink in heads:
                def scores(i):
                    n = P * len(blocks[i])
                    bk, S = [bS0, bS1][i % 2], W.S[i % 2]
                    yield from get(bk)
                    yield from get(S)
                    k0 = blocks[i][0] * P
                    m = pe.do(lambda e: e.matmul(bk.ap[:, 0:n], Qb.ap[rows, i * P:(i + 1) * P], Kb.ap[rows, k0:k0 + n],
                                                 start=True, stop=True), *marks, *bk.free)
                    st = strip(i) if strip else (None, None)
                    ex = extra(i) if extra else (None, None)
                    probs[i] = softmax_rows(W, (bk, S), n, scale, st[0], [m, st[1], ex[1]], ex[0], sink)
                    last[0] = probs[i]

                def turn_probs(i):
                    bl = blocks[i]
                    yield from get(bT)
                    yield from get(W.PT[i % 2])
                    S, PT = W.S[i % 2], W.PT[i % 2]
                    for j in range(len(bl)):
                        f = lambda e, j=j: e.transpose(bT.ap[:, j * P:(j + 1) * P], S.ap[:, j * P:(j + 1) * P], ident)
                        m = pe.do(f, probs[i], *bT.free)
                    S.give(m)
                    ptm[i] = act.do(lambda e: e.activation(PT.ap[:, 0:P * len(bl)], bT.ap[:, 0:P * len(bl)], ACT.Copy),
                                    m, *PT.free)
                    bT.give(ptm[i])

                def values(i):
                    bl, PT = blocks[i], W.PT[i % 2]
                    for j, kb in enumerate(bl):
                        f = lambda e, j=j, kb=kb: e.matmul(
                            bO.ap[orows, i * P:(i + 1) * P], Vb.ap[:, kb * P + vcols.start:kb * P + vcols.stop],
                            PT.ap[:, j * P:(j + 1) * P], start=(j == 0), stop=(j == len(bl) - 1))
                        m = pe.do(f, ptm[i], *marks, *(bO.free if first[0] else ()))
                        first[0] = False
                    PT.give(m)
                    return m

                probs, ptm, last = {}, {}, [None]
                yield from scores(0)
                yield
                for i in range(NT):
                    if i + 1 < NT:
                        yield from scores(i + 1)
                    yield from turn_probs(i)
                    yield
                    m = values(i)
                first[0] = False
            yield from finish(m, last[0])

        x1s, mks, kvs = io["x1s"], io["mgs"], io["kvs"]

        for h in range(4):
            plan("w_mem", 2 * h, 2)
            plan("w_mem", 2 * (4 + h), 2)
        for h in range(8):
            for part in range(4):
                plan("w_in", 2 * (8 * part + h), 2)
        for h in range(8):
            for part in (5, 4, 6, 7):
                plan("w_in", 2 * (8 * part + h), 2)
        for nb in range(16):
            plan("w_out", 2 * nb, 2)
        IQ, IK, CKV, CQ, CG, BK, BV, BQ, BG, AQ, AG, MA, MB, MC = 0, 8, 9, 11, 15, 19, 20, 21, 27, 33, 39, 45, 61, 77
        plan("w_in2", 2 * IK, 2)
        for j in range(8):
            plan("w_in2", 2 * (IQ + j), 2)
        for h in range(4):
            plan("w_in2", 2 * (CQ + h), 2)
            plan("w_in2", 2 * (CG + h), 2)
        plan("w_in2", 2 * BK, 2)
        plan("w_in2", 2 * BV, 2)
        for j in range(6):
            plan("w_in2", 2 * (BQ + j), 2)
            plan("w_in2", 2 * (BG + j), 2)
        for nb in range(16):
            plan("w_in2", 2 * (MC + nb), 2)
            plan("w_upc", nb, 1, 512)
        plan("w_in2", 2 * CKV, 2)
        plan("w_in2", 2 * CKV + 2, 2)
        for h in range(6):
            if h % 2 == 0:
                plan("w_kv", h // 2, 1)
                plan("w_in2", 2 * (AQ + h), 2)
                plan("w_in2", 2 * (AG + h), 2)
                plan("w_in2", 2 * (AQ + h + 1), 2)
                plan("w_in2", 2 * (AG + h + 1), 2)
        for nb in range(16):
            plan("w_in2", 2 * (MB + nb), 2)
            plan("w_upb", nb, 1, 768)
        for nb in range(16):
            plan("w_in2", 2 * (MA + nb), 2)
            plan("w_upa", nb, 1, 768)
        for nb in range(16):
            plan("w_o", 2 * nb, 2)

        s_mem, s_x = [sem(f"s_mem{i}") for i in range(4)], [sem(f"s_x{i}") for i in range(4)]
        for i in range(4):
            sp.dma(Y[:, i * 1024:(i + 1) * 1024], io["memT"][:, i * 1024:(i + 1) * 1024], s_mem[i])
        act.wait(m_cst)
        dve.wait(m_cst)

        def small_sigmoid(x, out, tmp, mark=None):
            m = act.do(lambda e: e.activation(tmp, x, ACT.Abs), mark)
            m = act.do(lambda e: e.activation(tmp, tmp, ACT.Exp, scale=-1.0), m)
            m = act.do(lambda e: e.activation(tmp, tmp, ACT.Ln, bias=1.0), m)
            m = dve.do(lambda e: e.scalar_tensor_tensor(out=out, in0=x, scalar=0.0, in1=tmp, op0=ALU.min,
                                                        op1=ALU.subtract), m)
            return act.do(lambda e: e.activation(out, out, ACT.Exp), m)

        m = small_sigmoid(C("c"), par[:, 64:80], small[:, 0:16])
        m_c = dve.do(lambda e: e.tensor_tensor(par[:, 64:80], par[:, 64:80], C("c"), ALU.mult), m)
        m = dve.do(lambda e: e.tensor_tensor(small[:, 24:32], C("lb", 0, 8), C("lb", 8, 8), ALU.subtract))
        m = small_sigmoid(small[:, 24:32], par[:, 56:64], small[:, 32:40], m)
        m_lb = dve.do(lambda e: e.tensor_scalar(par[:, 48:56], par[:, 56:64], -1.0, 1.0, ALU.mult, ALU.add), m)
        m_ns = dve.do(lambda e: e.tensor_scalar(par[:, 80:92], C("sinks"), -1.0, None, ALU.mult))

        ada = io["w_ada"].rearrange("(p j) n -> p j n", j=16)

        def ada_parts(cols, acc, slots, out_col, mark):
            m = None
            for cc in range(cols[0], cols[1]):
                a = acc[:, (cc - cols[0]) * 1024:(cc - cols[0] + 1) * 1024]
                for j in range(16):
                    s = slots[(cc * 16 + j) % len(slots)]
                    d = load(sp, s, s.ap, ada[:, j, cc * 1024:(cc + 1) * 1024], *s.free)
                    cj = par[:, 64 + j:65 + j]
                    if j == 0:
                        m = dve.do(lambda e: e.tensor_scalar(a, s.ap, cj, None, ALU.mult), d, m_c, *mark)
                    else:
                        m = dve.do(lambda e: e.scalar_tensor_tensor(out=a, in0=s.ap, scalar=cj, in1=a, op0=ALU.mult,
                                                                    op1=ALU.add), d, m)
                    s.free = (m,)
                    if j % 2:
                        yield
            yield from get(bO)
            n = 8 * (cols[1] - cols[0])
            for i in range(n):
                f = lambda e, i=i: e.matmul(bO.ap[:, i:i + 1], acc[:, i * P:(i + 1) * P], ones[:, 0:1], start=True, stop=True)
                r = pe.do(f, m, m_cst, *bO.free)
            c0 = cols[0] * 8
            r = dve.do(lambda e: e.tensor_tensor(par[:, out_col:out_col + n], bO.ap[:, 0:n], C("b_ada", c0, n), ALU.add), r)
            bO.give(r)
            ada_parts.mark = r

        a_sems = [chan(f"s_ada{i}") for i in range(4)]
        for i in range(4):
            for_now = TA[:, 4096 + 1024 * i:5120 + 1024 * i]
            a_sems[i] = Buf(for_now, a_sems[i])

        WM = Work(Y, None, None, w_sems)
        mem = Acts(H[1][:, 0:4096], H[1][:, 4096:8192], KT, 256)
        sq, rr = Y[:, 4096:8192], Y[:, 4096:4352]
        for k in range(KT):
            m = act.do(lambda e, k=k: e.activation(sq[:, k * 256:(k + 1) * 256], Y[:, k * 256:(k + 1) * 256], ACT.Square),
                       (s_mem[k // 4], 16))
            m = pe.do(lambda e, k=k: e.matmul(bST.ap[:, 0:256], ones, sq[:, k * 256:(k + 1) * 256], start=(k == 0),
                                              stop=(k == KT - 1)), m, m_cst)
        m = act.do(lambda e: e.activation(rr, bST.ap[:, 0:256], ACT.Ln, scale=1.0 / D, bias=eps), m, m_eps)
        bST.give(m)
        m_r = act.do(lambda e: e.activation(rr, rr, ACT.Exp, scale=-0.5), m)
        for k in range(KT):
            t = Y[:, k * 256:(k + 1) * 256]
            m = dve.do(lambda e, k=k, t=t: e.scalar_tensor_tensor(out=t, in0=t, scalar=C("mem_g", k, 1), in1=rr,
                                                                  op0=ALU.mult, op1=ALU.mult), m_r)
            mem_raw = mem.put(k, t, m, on_dve=k % 2 == 1)
        raws_free = mem.ready[KT - 1], mem.ready[KT - 2]

        WM = W1m = Work(Y, None, None, w_sems)
        mk_bufs = [Buf(Y[:, 4096 + 256 * i:4352 + 256 * i], s) for i, s in enumerate(w_sems[0:6])]
        WM.SQ, WM.R = Buf(Y[:, 5632:5888]), Buf(Y[:, 5888:6144])
        for b in (*mk_bufs, WM.SQ, WM.R):
            b.free = (m,)
        m_kv = {}

        def mem_post(h, kind, b, mark):
            mm = [mark]
            if kind == 0:
                yield from norm(WM, [b.ap], mm, ones, 128, [C("kc")], w=256)
            else:
                yield from turned(WM, b, mark, mm, n=2)
            m_kv[h, kind] = load(sp, b, kvs[2 * h + kind], b.ap, mm[0])
            b.give(m_kv[h, kind])
            yield

        behind.append(ada_parts((0, 4), TA[:, 0:4096], a_sems, 0, ()))
        for h in range(4):
            for kind in range(2):
                bk, m = full(mem, "w_mem", h + 4 * kind)
                b = take(mk_bufs[(2 * h + kind) % 6])
                r = evac(bk, m, b, w=256)
                urgent.append(mem_post(h, kind, b, r))
        while urgent:
            pump()
        mem_used = (m, *[m_kv[k] for k in m_kv], WM.R.free[0], WM.SQ.free[0])

        for i in range(4):
            sp.wait(*mem_used, *raws_free)
            sp.dma(Y[:, i * 2048:(i + 1) * 2048], io["xT"][:, i * 2048:(i + 1) * 2048], s_x[i])
        xq = [TA[:, 8192:8704]]
        m_sq = None
        for k in range(KT):
            m = act.do(lambda e, k=k: e.activation(xq[0], Y[:, k * T:(k + 1) * T], ACT.Square), (s_x[k // 4], 16), m_sq, m_mk)
            m_sq = pe.do(lambda e, k=k: e.matmul(bST.ap, ones, xq[0], start=(k == 0), stop=(k == KT - 1)), m, *bST.free)
            pump()
        m = act.do(lambda e: e.activation(xq[0], bST.ap, ACT.Ln, scale=1.0 / D, bias=eps), m_sq)
        bST.give(m)
        m_r = act.do(lambda e: e.activation(xq[0], xq[0], ACT.Exp, scale=-0.5), m)
        xm = []
        for k in range(KT):
            t = Y[:, k * T:(k + 1) * T]
            xm.append(dve.do(lambda e, t=t: e.tensor_tensor(t, t, xq[0], ALU.mult), m_r))
            pump()
        drain()
        m = dve.do(lambda e: e.tensor_scalar(par[:, 16:32], par[:, 16:32], 1.0, None, ALU.add), ada_parts.mark)
        m = dve.do(lambda e: e.tensor_tensor(par[:, 16:32], par[:, 16:32], C("norm_g"), ALU.mult), m)
        hx = Acts(H[0], H[1], KT, T)
        hx.used = mem_used
        for k in range(KT):
            t = Y[:, k * T:(k + 1) * T]
            r = dve.do(lambda e, k=k, t=t: e.tensor_scalar(t, t, par[:, 16 + k:17 + k], par[:, k:k + 1], ALU.mult, ALU.add), m)
            hx.put(k, t, r, on_dve=k % 3 == 1)
        hx_src = (*hx.ready, )

        for b in W1.all() + [W1.t1, W1.t2]:
            b.free = (ada_parts.mark, m)
        g_slots = [Buf(Y[:, 4096 + 1024 * i:5120 + 1024 * i], a_sems[i].chan) for i in range(2)]
        for i in range(2):
            g_slots[i].free = hx_src
        behind.append(ada_parts((4, 6), Y[:, 6144:8192], g_slots, 32, hx_src))
        yb = [Buf(Y[:, k * T:(k + 1) * T]) for k in range(KT)]
        y_m = [None] * KT
        causal1 = [list(range(i + 1)) for i in range(NT)]
        all_rows = slice(0, 128)

        def head_post(W, kind, b, mark, out, gain=None, over=None, n=128):
            mm = [mark]
            if kind == "norm":
                yield from norm(W, [b.ap], mm, over or ones, n, [gain])
            elif kind == "turn":
                yield from turned(W, b, mark, mm)
            else:
                yield from silu(W, b.ap, mark, mm)
            out.append(mm[0])

        def take_head(W, name, x, nb, b, kind, out, **kw):
            bk, m = full(x, name, nb)
            r = evac(bk, m, take(b))
            urgent.append(head_post(W, kind, b, r, out, **kw))

        def att_head(h, Qb, Kb, Vb, Zb, ms):
            W = W1
            while len(ms) < 4:
                yield
            yield from get(W.ST[h % 2])
            sbuf = W.ST[h % 2]
            d = load(sp, sbuf, sbuf.ap, io["strip1"][h], *sbuf.free)

            def finish(m, last):
                for b in (Qb, Kb):
                    b.give(last, m)
                sbuf.give(last)
                Vb.give(m)
                y_m[h] = dve.do(lambda e: e.tensor_tensor(yb[h].ap, bO.ap, Zb.ap, ALU.mult), m, *hx_src)
                bO.give(y_m[h])
                Zb.give(y_m[h])
                yield

            yield from attention(W, Qb, Kb, Vb, ms, [(all_rows, slice(0, 128), all_rows, SC128,
                                 lambda i: (sbuf.ap[:, 384 - 128 * i:512], d), None, None)], causal1, None, finish)

        for h in range(8):
            W, ms = W1, []
            bufs = W.Q[h % 2], W.K[h % 2], W.V[h % 2], W.Z[h % 2]
            take_head(W, "w_in", hx, h, bufs[0], "norm", ms, gain=C("q_g"))
            take_head(W, "w_in", hx, 8 + h, bufs[1], "norm", ms, gain=C("k_g"))
            take_head(W, "w_in", hx, 16 + h, bufs[2], "turn", ms)
            take_head(W, "w_in", hx, 24 + h, bufs[3], "silu", ms)
            behind.append(att_head(h, *bufs, ms))

        AD, OF1, OF2 = TA[:, 4096:4608], TA[:, 4608:4864], TA[:, 4864:5376]
        TOT = TA[:, 5376:5888]
        a_buf = Buf(None)

        def hg_prep(h, kind, b, mark, out, F):
            W = W1
            if kind == "f":
                res = {}

                def pos(s, m):
                    res["f"] = dve.do(lambda e: e.tensor_scalar(F.ap, s, par[:, 48 + h:49 + h], par[:, 56 + h:57 + h],
                                                                ALU.mult, ALU.add), m, m_lb, *F.free)
                    return res["f"]

                def neg(s, m):
                    res["k"] = dve.do(lambda e: e.tensor_scalar(b.ap, s, par[:, 48 + h:49 + h], None, ALU.mult), m)
                    return res["k"]
                yield from sigma(W, b.ap, mark, [(1, pos), (-1, neg)])
                out += [res["f"], res["k"]]
            elif kind == "turn":
                mm = [None]
                yield from turned(W, b, mark, mm)
                out.append(mm[0])
            else:
                mm = [None]
                yield from silu(W, b.ap, mark, mm)
                out.append(mm[0])

        def hg_head(h, Qb, Kb, Vb, Zb, Fb, ms):
            W = W1
            while len(ms) < 5:
                yield
            yield from get(a_buf)
            for b in (*W.S, *W.PT):
                yield from get(b)
            q, k = Qb.ap, Kb.ap
            lvl = 0
            up = ms
            a_free = a_buf.free if a_buf.free else ()
            z = ()
            if h == 0:
                z = (dve.do(lambda e: e.memset(AD, 0.0), *[x for b in (*W.S, *W.PT) for x in b.free]),)
            tot_m = None
            done = []
            for step, m in enumerate([0, 1, 2, 4, 8, 16, 32, 64]):
                bk = (bS0, bS1)[step % 2]
                yield from get(bk)
                for i in range(NT):
                    f = lambda e, i=i: e.matmul(bk.ap[:, i * P:(i + 1) * P], k[:, i * P:(i + 1) * P],
                                                q[:, i * P:(i + 1) * P], start=True, stop=True)
                    r = pe.do(f, *up, *bk.free)
                msk = mk[:, step * P:(step + 1) * P].unsqueeze(1).to_broadcast([P, NT, P])
                c = dve.do(lambda e, bk=bk, msk=msk: e.copy_predicated(AD.rearrange("p (i t) -> p i t", i=NT), msk,
                                                       bk.ap.rearrange("p (i t) -> p i t", i=NT)), r, m_mk, *z, *a_free)
                bk.give(c)
                a_free = z = ()
                done = [c]
                if m == 0:
                    u = dve.do(lambda e: e.tensor_tensor(q, q, Fb.ap, ALU.mult), r, *up)
                    up = [u]
                    tot = Fb.ap
                    continue_tot = None
                    yield
                    continue
                qv = q.rearrange("p (b two m) -> p b two m", two=2, m=m)
                kv = k.rearrange("p (b two m) -> p b two m", two=2, m=m)
                tv = tot.rearrange("p (b two) -> p b two", two=2)
                nb = T // (2 * m)
                tl = tv[:, :, 0:1].to_broadcast([P, nb, m])
                tr = tv[:, :, 1:2].to_broadcast([P, nb, m])
                u1 = dve.do(lambda e, qv=qv, tl=tl: e.tensor_tensor(qv[:, :, 1, :], qv[:, :, 1, :], tl, ALU.mult), r, tot_m)
                u2 = dve.do(lambda e, kv=kv, tr=tr: e.tensor_tensor(kv[:, :, 0, :], kv[:, :, 0, :], tr, ALU.mult), r, tot_m)
                new = TOT[:, T - 2 * nb:T - nb]
                tot_m = dve.do(lambda e, tv=tv, new=new: e.tensor_tensor(new, tv[:, :, 0], tv[:, :, 1], ALU.mult), tot_m)
                tot = new
                up = [u1, u2]
                yield
            yield from get(bS0)
            for i in range(2):
                f = lambda e, i=i: e.matmul(bS0.ap[:, i * P:(i + 1) * P], k[:, 2 * i * P:(2 * i + 1) * P],
                                            q[:, (2 * i + 1) * P:(2 * i + 2) * P], start=True, stop=True)
                r = pe.do(f, *up, *bS0.free)
            c1 = act.do(lambda e: e.activation(OF1, bS0.ap[:, 0:256], ACT.Copy), r, *a_buf.free)
            bS0.give(c1)
            qv = q.rearrange("p (b two m) -> p b two m", two=2, m=P)
            kv = k.rearrange("p (b two m) -> p b two m", two=2, m=P)
            tv = tot.rearrange("p (b two) -> p b two", two=2)
            u1 = dve.do(lambda e: e.tensor_tensor(qv[:, :, 1, :], qv[:, :, 1, :], tv[:, :, 0:1].to_broadcast([P, 2, P]),
                                                  ALU.mult), r, tot_m)
            u2 = dve.do(lambda e: e.tensor_tensor(kv[:, :, 0, :], kv[:, :, 0, :], tv[:, :, 1:2].to_broadcast([P, 2, P]),
                                                  ALU.mult), r, tot_m)
            Fb.give(u2)
            yield
            yield from get(bS1)
            for i in range(2):
                f = lambda e, i=i: e.matmul(bS1.ap[:, i * 256:(i + 1) * 256], k[:, i * P:(i + 1) * P], q[:, 256:512],
                                            start=True, stop=True)
                r = pe.do(f, u1, u2, *bS1.free)
            c2 = act.do(lambda e: e.activation(OF2, bS1.ap, ACT.Copy), r)
            bS1.give(c2)
            Qb.give(r)
            Kb.give(r)
            yield
            yield from get(bO)
            v = lambda i: Vb.ap[:, i * P:(i + 1) * P]
            pairs = [[(0, AD[:, 0:128])],
                     [(1, AD[:, 128:256]), (0, OF1[:, 0:128])],
                     [(2, AD[:, 256:384]), (0, OF2[:, 0:128]), (1, OF2[:, 256:384])],
                     [(3, AD[:, 384:512]), (2, OF1[:, 128:256]), (0, OF2[:, 128:256]), (1, OF2[:, 384:512])]]
            for i, ps in enumerate(pairs):
                for j, (kb, a) in enumerate(ps):
                    f = lambda e, i=i, j=j, kb=kb, a=a, n=len(ps): e.matmul(bO.ap[:, i * P:(i + 1) * P], v(kb), a,
                                                                            start=(j == 0), stop=(j == n - 1))
                    r = pe.do(f, *done, c1, c2, *ms, *bO.free)
            a_buf.give(r)
            for b in (*W.S, *W.PT):
                b.give(r, tot_m)
            Vb.give(r)
            yield from get(W.SQ)
            m = act.do(lambda e: e.activation(W.SQ.ap, bO.ap, ACT.Square), r, *W.SQ.free)
            yield
            yield from get(bST)
            m = pe.do(lambda e: e.matmul(bST.ap, ones, W.SQ.ap, start=True, stop=True), m, *bST.free)
            W.SQ.give(m)
            yield from get(W.R)
            r, ln = rsq(W, T, 128, bST.ap, m)
            bST.give(ln)
            y = yb[8 + h].ap
            m = dve.do(lambda e: e.scalar_tensor_tensor(out=y, in0=bO.ap, scalar=C("hg_g"), in1=W.R.ap, op0=ALU.mult,
                                                        op1=ALU.mult), r, ada_parts.mark)
            bO.give(m)
            W.R.give(m)
            y_m[8 + h] = dve.do(lambda e: e.tensor_tensor(y, y, Zb.ap, ALU.mult), m)
            Zb.give(y_m[8 + h])
            yield

        for h in range(8):
            W, ms = W1, []
            bufs = W.Q[h % 2], W.K[h % 2], W.V[h % 2], W.Z[h % 2], W.ST[h % 2]
            for part, b, kind in ((5, bufs[1], "f"), (4, bufs[0], "silu"), (6, bufs[2], "turn"), (7, bufs[3], "silu")):
                bk, m = full(hx, "w_in", 8 * part + h)
                if kind == "f":
                    take(bufs[4])
                r = evac(bk, m, take(b))
                urgent.append(hg_prep(h, kind, b, r, ms, bufs[4]))
            behind.append(hg_head(h, *bufs, ms))
        last_in = m
        drain()

        yx = Acts(H[0], H[1], KT, T)
        yx.used = (last_in,)
        for k in range(KT):
            yx.put(k, yb[k].ap, y_m[k], on_dve=k % 3 == 1)
        xb = [Buf(TA[:, i * T:(i + 1) * T], w_sems[i]) for i in range(3)]
        for b in xb:
            b.free = tuple(x for o in W1.all() for x in o.free)
        x1_m, x1_st = [None] * KT, [None] * KT
        s_x1 = [sem(f"s_x1_{i}") for i in range(KT)]
        sqt = Buf(TA[:, 3 * T:4 * T])
        sqt.free = xb[0].free
        for nb in range(KT):
            b = xb[nb % 3]
            d = load(sp, b, b.ap, io["xT"][:, nb * T:(nb + 1) * T], *b.free)
            bk, m = full(yx, "w_out", nb)
            t = yb[nb].ap
            r = dve.do(lambda e, nb=nb, t=t, bk=bk, b=b: e.scalar_tensor_tensor(
                out=t, in0=bk.ap, scalar=par[:, 32 + nb:33 + nb], in1=b.ap, op0=ALU.mult, op1=ALU.add), m, d, *yx.ready)
            bk.give(r)
            b.free = (r,)
            x1_m[nb] = r
            sp.wait(r)
            sp.dma(x1s[nb], t, s_x1[nb])
            x1_st[nb] = (s_x1[nb], 16)
            r = act.do(lambda e, t=t: e.activation(sqt.ap, t, ACT.Square), r, *sqt.free)
            r = pe.do(lambda e, nb=nb: e.matmul(bST.ap, ones, sqt.ap, start=(nb == 0), stop=(nb == KT - 1)), r, *bST.free)
            sqt.free = (r,)
        last_out = m

        def finish_norm(name, src_marks, dst, used):
            rb = TA[:, 4 * T:5 * T]
            m = act.do(lambda e: e.activation(rb, bST.ap, ACT.Ln, scale=1.0 / D, bias=eps), r, *sqt.free)
            bST.give(m)
            m = act.do(lambda e: e.activation(rb, rb, ACT.Exp, scale=-0.5), m)
            hb = [Buf(TA[:, (5 + i) * T:(6 + i) * T]) for i in range(4)]
            dst.used = used
            for k in range(KT):
                b = hb[k % 4]
                x = dve.do(lambda e, k=k, b=b: e.scalar_tensor_tensor(
                    out=b.ap, in0=yb[k].ap, scalar=C(name, k, 1), in1=rb, op0=ALU.mult, op1=ALU.mult),
                    m, src_marks[k], *b.free)
                b.free = (dst.put(k, b.ap, x, on_dve=k % 3 == 1),)
            return x

        h2 = Acts(H[0], H[1], KT, T)
        h2_done = finish_norm("norm_g2", x1_m, h2, (last_out,))

        W = W2
        x1_free = (h2_done, *x1_st)
        for b in W2.all():
            b.free = x1_free
        W2.t1.free = W2.t2.free = (*h2.ready[-4:],)
        ost = [Buf(TA[:, i * T:(i + 1) * T]) for i in range(6)]
        sc = TA[:, 3072:4224]
        gx = [Buf(TA[:, 4224 + i * T:4224 + (i + 1) * T]) for i in range(2)]
        ub = [Buf(TA[:, 5248 + i * T:5248 + (i + 1) * T], chan(f"s_u{i}")) for i in range(2)]
        lb_ = [Buf(TA[:, 6272 + i * T:6272 + (i + 1) * T], chan(f"s_l{i}")) for i in range(2)]
        rt = Buf(TA[:, 7296:7808])
        for b in (*ost, *gx, *ub, *lb_, rt):
            b.free = (*h2.ready,)
        OFF = {1: 0, 2: 256, 3: 640}

        ik = W.K[0]
        bk, m = full(h2, "w_in2", IK)
        r_ik = evac(bk, m, take(ik))
        ik_m, iw_m = [], []

        def ik_post():
            yield from get(bST)
            m = pe.do(lambda e: e.matmul(bST.ap, ones64, ik.ap, start=True, stop=True), r_ik, *bST.free)
            m = dve.do(lambda e: e.scalar_tensor_tensor(out=ik.ap, in0=bST.ap, scalar=-1.0 / 64, in1=ik.ap, op0=ALU.mult,
                                                        op1=ALU.add), m)
            bST.give(m)
            mm = [m]
            yield from norm(W, [ik.ap], mm, ones64, 64, [C("ik_g")])
            ik_m.append(dve.do(lambda e: e.tensor_scalar(ik.ap, ik.ap, C("ik_b"), None, ALU.add), mm[0]))

        urgent.append(ik_post())

        a = act.do(lambda e: e.activation(iwr[0], iww, ACT.Copy), m_iww)
        a = pool.do(lambda e: e.tensor_tensor(iwr[1], iww, iwr[0].bitcast(F32), ALU.subtract), a)
        take(bV)
        for i in range(NT):
            for k in range(KT):
                for n, (x, w) in enumerate(((0, 0), (1, 0), (0, 1))):
                    ap = (h2.hi, h2.lo)[x][k][:, i * P:(i + 1) * P]
                    f = lambda e, ap=ap, w=w, i=i, k=k, n=n: e.matmul(
                        bV.ap[:, 16 * i:16 * i + 16], ap, iwr[w][:, 16 * k:16 * k + 16], start=(k == 0 and n == 0),
                        stop=(k == KT - 1 and n == 2))
                    if k == KT - 1 and n == 2:
                        m = pe.do(f)
                    else:
                        pe.quiet(f, a, h2.ready[k], *bV.free)
        m = dve.do(lambda e: e.tensor_scalar(iwt, bV.ap[:, 0:64], 1.0 / 32, None, ALU.mult), m)
        bV.give(m)
        iw_m.append(m)
        sc_m = {1: None, 2: None, 3: None}

        def idx_head(j, Qb, ms):
            while not ik_m or not ms:
                yield
            for hh in range(2):
                head = 2 * j + hh
                rows = slice(64 * hh, 64 * hh + 64)
                for i in (1, 2, 3):
                    n = P * (i + 1)
                    bk = (bS0, bS1)[i % 2]
                    yield from get(bk)
                    m = pe.do(lambda e: e.matmul(bk.ap[:, 0:n], Qb.ap[rows, i * P:(i + 1) * P], ik.ap[rows, 0:n],
                                                 start=True, stop=True), *ms, *ik_m, *bk.free)
                    yield from get(rt)
                    a = act.do(lambda e: e.activation(rt.ap[:, 0:n], bk.ap[:, 0:n], ACT.Relu), m, *rt.free)
                    bk.give(a)
                    s = sc[:, OFF[i]:OFF[i] + n]
                    wcol = iwt[:, 16 * i + head:16 * i + head + 1]
                    if head == 0:
                        m = dve.do(lambda e: e.tensor_scalar(s, rt.ap[:, 0:n], wcol, None, ALU.mult), a, *iw_m, *h2.ready)
                    else:
                        m = dve.do(lambda e: e.scalar_tensor_tensor(out=s, in0=rt.ap[:, 0:n], scalar=wcol, in1=s,
                                                                    op0=ALU.mult, op1=ALU.add), a, sc_m[i])
                    rt.give(m)
                    sc_m[i] = m
                yield
            Qb.give(sc_m[1], sc_m[2], sc_m[3])
            if j == 7:
                ik.give(*sc_m.values())

        for j in range(8):
            Qb = W.Q[j % 2]
            bk, m = full(h2, "w_in2", IQ + j)
            r = evac(bk, m, take(Qb))
            behind.append(idx_head(j, Qb, [r]))

        def topk():
            mx = small[:, 48:56]
            for i in (1, 2, 3):
                n = P * (i + 1)
                s = sc[:, OFF[i]:OFF[i] + n]
                d = sc[:, OFF[i] + n - P:OFF[i] + n]
                m = dve.do(lambda e: e.tensor_tensor(d, d, C("causal"), ALU.add), sc_m[i])
                for r in range(TOPK // 8):
                    m = dve.do(lambda e: e.max(tkm, s), m)
                    m = dve.do(lambda e: e.match_replace(s, tkm, s, -3e38), m)
                    if r % 2:
                        yield
                sc_m[i] = dve.do(lambda e: e.tensor_scalar(s, s, -2e38, NEG, ALU.is_gt, ALU.mult), m)

        tkm = par[:, 96:104]
        tk = topk()
        tk_running = [True]

        def tk_step():
            if tk_running[0]:
                try:
                    next(tk)
                except StopIteration:
                    tk_running[0] = False

        def staged(h, Zb, others, m, last):
            for b in others:
                b.give(last, m)
            r = dve.do(lambda e: e.tensor_tensor(ost[h].ap, bO.ap, Zb.ap, ALU.mult), m, *ost[h].free)
            bO.give(r)
            Zb.give(r)
            o_m[h] = r

        o_m = {}

        def c_head(h, Qb, Kb, Vb, Zb, ms):
            while len(ms) < 2:
                yield
            yield from get(ost[h])
            dk = load(sp, Kb, Kb.ap[:, 0:256], kvs[2 * h], m_kv[h, 0], *Kb.free)
            dv = load(sp, Vb, Vb.ap[:, 0:256], kvs[2 * h + 1], m_kv[h, 1], *Vb.free)

            def finish(m, last):
                staged(h, Zb, (Qb, Kb, Vb), m, last)
                yield
            yield from attention(W, Qb, Kb, Vb, [*ms, dk, dv], [(all_rows, slice(0, 128), all_rows, SC128, None, None, None)],
                                 [[0, 1]] * NT, None, finish)

        for h in range(4):
            ms = []
            bufs = W.Q[h % 2], W.K[h % 2], W.V[h % 2], W.Z[h % 2]
            take_head(W, "w_in2", h2, CQ + h, bufs[0], "norm", ms, gain=C("qc"))
            take_head(W, "w_in2", h2, CG + h, bufs[3], "silu", ms)
            take(bufs[1])
            take(bufs[2])
            behind.append(c_head(h, *bufs, ms))

        bK, bVv = W.K[0], W.V[0]
        kvm = []
        take_head(W, "w_in2", h2, BK, bK, "norm", kvm, gain=C("kb"), over=ones64, n=64)
        take_head(W, "w_in2", h2, BV, bVv, "turn", kvm)
        oc = Acts(O2[0], O2[1], 6, T)
        while len(o_m) < 4:
            pump()
        for k in range(4):
            ost[k].give(oc.put(k, ost[k].ap, o_m[k]))
        o_m.clear()
        window = [[0], [0, 1], [1, 2], [2, 3]]

        def b_pair(j, Qb, Zb, ms):
            while len(ms) < 1 or len(kvm) < 2 or len(zs[j]) < 1:
                yield
            yield from get(ost[j])
            for b in W.ST:
                yield from get(b)
            heads = []
            for half, head in enumerate((j, j + 6)):
                rows = slice(64 * half, 64 * half + 64)
                sbuf = W.ST[half]
                d = load(sp, sbuf, sbuf.ap[:, 0:256], io["strip_b"][head], *sbuf.free)
                strip = lambda i, s=sbuf, d=d: (s.ap[:, 128:256] if i == 0 else s.ap[:, 0:256], d)
                heads.append((rows, rows, rows, SC64, strip, None,
                              (C("sinks", head, 1), par[:, 80 + head:81 + head])))

            def finish(m, last):
                for b in W.ST:
                    b.give(last)
                staged(j, Zb, (Qb,), m, last)
                if j == 5:
                    bK.give(last)
                    bVv.give(m)
                yield
            yield from attention(W, Qb, bK, bVv, [*ms, *kvm, m_ns], heads, window, None, finish)

        zs = [[] for _ in range(6)]
        for j in range(6):
            ms = []
            Qb, Zb = W.Q[j % 2], W.Z[j % 2]
            take_head(W, "w_in2", h2, BQ + j, Qb, "norm", ms, gain=C("qb"), over=ones64, n=64)
            take_head(W, "w_in2", h2, BG + j, Zb, "silu", zs[j])
            behind.append(b_pair(j, Qb, Zb, ms))

        st_m = [None] * KT

        def mix_gate(b, mark, nb, out):
            def use(s, m):
                out.append(pool.do(lambda e: e.tensor_copy(b.ap, s), m))
                return out[0]
            yield from sigma(W2, b.ap, mark, [(1, use)])

        def mix(branch, MX, name, o, nk, gcol):
            for nb in range(KT):
                g = gx[nb % 2]
                bk, m = full(h2, "w_in2", MX + nb)
                r = evac(bk, m, take(g), bias=C("gate_b", gcol + nb, 1))
                out = []
                urgent.append(mix_gate(g, r, nb, out))
                if branch > 0:
                    lb = lb_[nb % 2]
                    d = load(sp, lb, lb.ap, mks[nb], st_m[nb], *lb.free)
                bk, m = product(o, [((name, nb), nk, 0)], list(range(nk)))
                while not out:
                    pump()
                u = ub[nb % 2]
                r = dve.do(lambda e, bk=bk, u=u, g=g: e.tensor_tensor(u.ap, bk.ap, g.ap, ALU.mult), m, out[0], *u.free)
                bk.give(r)
                g.give(r)
                if branch == 1:
                    r = pool.do(lambda e, u=u, lb=lb: e.tensor_tensor(u.ap, u.ap, lb.ap, ALU.add), r, d)
                    lb.free = (r,)
                if branch == 2:
                    r = dve.do(lambda e, u=u, lb=lb, nb=nb: e.tensor_tensor(yb[nb].ap, u.ap, lb.ap, ALU.add), r, d,
                               *y_free)
                    lb.free = (r,)
                    u.free = (r,)
                    mg_m[nb] = r
                else:
                    st_m[nb] = load(sp, u, mks[nb], u.ap, r)
                    u.free = (st_m[nb],)
                tk_step()
                tk_step()
            return m

        mix_last = mix(0, MC, "w_upc", oc, 4, 32)
        while tk_running[0]:
            tk_step()

        ckb = []
        bufs = take(W.K[1]), take(W.V[1])
        cm = []
        for i in range(2):
            bk, m = full(h2, "w_in2", CKV + i)
            cm.append(evac(bk, m, bufs[i]))
        cx = Acts(CK[0], CK[1], 2, T)

        def ck_post():
            yield from norm(W, [b.ap for b in bufs], cm, ones, 256, [C("kv_g", 0, 1), C("kv_g", 1, 1)])
            for i in range(2):
                bufs[i].give(cx.put(i, bufs[i].ap, cm[i]))
            ckb.append(1)

        urgent.append(ck_post())
        while not ckb:
            pump()
        while len(o_m) < 6:
            pump()
        ob = Acts(O2[0], O2[1], 6, T)
        ob.used = (mix_last,)
        for k in range(6):
            ost[k].give(ob.put(k, ost[k].ap, o_m[k], on_dve=k % 2 == 1))
        o_m.clear()

        def a_head(h, Qb, Kb, Vb, Zb, ms):
            while len(ms) < 4:
                yield
            yield from get(ost[h])
            yield from get(W.ST[h % 2])
            sbuf = W.ST[h % 2]
            d = load(sp, sbuf, sbuf.ap, io["strip_a"][h], *sbuf.free)

            def finish(m, last):
                sbuf.give(last)
                staged(h, Zb, (Qb, Kb, Vb), m, last)
                yield
            yield from attention(W, Qb, Kb, Vb, ms, [(
                all_rows, slice(0, 128), all_rows, SC128, lambda i: (sbuf.ap[:, 384 - 128 * i:512], d),
                lambda i: (sc[:, OFF[i]:OFF[i] + P * (i + 1)], sc_m[i]) if i else (None, None), None)],
                causal1, None, finish)

        for h2i in range(3):
            key = ("w_kv", h2i)
            kv_bufs = []
            mss = [[], []]
            for e_ in range(2):
                h = 2 * h2i + e_
                for kind in range(2):
                    off = (2 * e_ + kind) * 256
                    bk, m = product(cx, [(key, 2, off)], [0, 1])
                    key = None
                    b = take((W.K, W.V)[kind][h % 2])
                    r = evac(bk, m, b)
                    urgent.append(head_post(W, ("norm", "turn")[kind], b, r, mss[e_], gain=C("ka")))
            for e_ in range(2):
                h = 2 * h2i + e_
                take_head(W, "w_in2", h2, AQ + h, W.Q[h % 2], "norm", mss[e_], gain=C("qa"))
                take_head(W, "w_in2", h2, AG + h, W.Z[h % 2], "silu", mss[e_])
                behind.append(a_head(h, W.Q[h % 2], W.K[h % 2], W.V[h % 2], W.Z[h % 2], mss[e_]))

        mix_last = mix(1, MB, "w_upb", ob, 6, 16)
        drain()
        oa = Acts(O2[0], O2[1], 6, T)
        oa.used = (mix_last,)
        for k in range(6):
            ost[k].give(oa.put(k, ost[k].ap, o_m[k], on_dve=k % 2 == 1))
        y_free = tuple(x for b in W2.all() for x in b.free)
        mg_m = [None] * KT
        mix_last = mix(2, MA, "w_upa", oa, 6, 0)
        drain()

        mx = Acts(H[0], H[1], KT, T)
        mx.used = (mix_last,)
        for k in range(KT):
            mx.put(k, yb[k].ap, mg_m[k], on_dve=k % 3 == 1)
        out_m = []
        for nb in range(KT):
            lb, u = lb_[nb % 2], ub[nb % 2]
            d = load(sp, lb, lb.ap, x1s[nb], x1_st[nb], *lb.free)
            bk, m = full(mx, "w_o", nb)
            r = dve.do(lambda e, bk=bk, u=u, lb=lb: e.tensor_tensor(u.ap, bk.ap, lb.ap, ALU.add), m, d, *u.free)
            bk.give(r)
            lb.free = (r,)
            s = load(sp, u, io["out"][nb], u.ap, r)
            u.free = (s,)
            out_m.append(s)
        sp.wait(*out_m, *st_m, *x1_st, *m_kv.values())
        assert ring.i == len(items)


def buckets():
    n = np.arange(512)
    nf = np.maximum(n, 1).astype(np.float32)
    large = 16 + (np.log(nf / np.float32(16)) / np.float32(np.log(8.0)) * np.float32(16)).astype(np.int32)
    return np.where(n < 16, n, np.minimum(large, 31))


def tiles(w, kt=8):
    K, N = w.shape
    return np.ascontiguousarray(
        w.reshape(K // (128 * kt), kt, 128, N // 128, 128).transpose(3, 0, 2, 1, 4).reshape(-1, 128, kt * 128))


def kernel(**inputs):
    import concourse.bacc as _bacc
    from concourse.bass_utils import run_bass_kernel_spmd as _run

    I = {k: np.asarray(v) for k, v in inputs.items()}
    f32 = np.float32

    def feat(a, n):
        return a.reshape(n, 128).T

    ar = np.arange(128)
    p, u = ar[:, None], np.arange(512)[None, :]
    cols = {
        "ident": np.eye(128, dtype=f32), "ones": np.ones((128, 128), f32),
        "ones64": np.kron(np.eye(2), np.ones((64, 64))).astype(f32),
        "causal": np.where(p >= ar[None, :], 0, NEG).astype(f32),
        "norm_g": feat(I["norm_g"], 16), "b_ada": feat(I["b_ada"], 48),
        "q_g": I["q_norm_g"].T, "k_g": I["k_norm_g"].T, "hg_g": I["hg_norm_g"].T,
        "lb": np.concatenate([feat(I["lower_bounds"][i], 8) for i in range(2)], 1),
        "norm_g2": feat(I["norm_g_2"], 16), "kv_g": feat(I["kv_norm_g_2"], 2),
        "ik_g": np.concatenate([I["idx_k_ln_g_2"].T] * 2), "ik_b": np.concatenate([I["idx_k_ln_b_2"].T] * 2),
        "qa": I["q_norm_a_2"].T, "ka": I["k_norm_a_2"].T,
        "qb": np.concatenate([I["q_norm_b_2"].T] * 2), "kb": np.concatenate([I["k_norm_b_2"].T] * 2),
        "qc": I["q_norm_c_2"].T, "kc": I["k_norm_c_2"].T, "mem_g": feat(I["mem_norm_g_2"], 16),
        "gate_b": feat(I["gate_bias_2"], 48), "sinks": np.broadcast_to(I["sinks_b_2"], (128, 12)),
        "c": I["c"].reshape(128, 16),
    }
    cst = np.zeros((128, NCST), f32)
    for name, (at, n) in CST.items():
        cst[:, at:at + n] = cols[name]
    s, t = ar[:, None], ar[None, :]
    masks = [s == t] + [(s // (2 * m) == t // (2 * m)) & (s // m % 2 == 0) & (t // m % 2 == 1)
                        for m in (1, 2, 4, 8, 16, 32, 64)]
    masks = np.concatenate(masks, 1).astype(np.int32)

    neg = f32(NEG)
    d = p - (u - 384)
    strip1 = I["rel_bias"][0][:, np.clip(d, -128, 128) + 128]
    strip1 = np.where((p < 64) & (u >= 448), neg, strip1)
    bk = buckets()
    ra, rb = I["rel_bias_2"][:, :6].T, I["rel_bias_2"][:, 6:].T
    strip_a = np.where(d >= 0, ra[:, bk[np.clip(d, 0, 511)]], neg)
    db = p - (u[:, :256] - 128)
    strip_b = np.where((db >= 0) & (db < 128), rb[:, bk[np.clip(db, 0, 511)]], neg)

    w2 = I["w_in_2"][0]
    sizes = (768, 256, 1024, 64, 16, 768, 768, 128, 128, 768, 512, 512, 6144)
    cuts = np.cumsum(np.array(sizes))[:-1].tolist()
    a_q, a_ckv, i_q, i_k, i_w, a_g, b_q, b_k, b_v, b_g, c_q, c_g, mixg = np.split(w2, cuts, axis=1)
    perm = np.concatenate([np.r_[64 * j:64 * j + 64, 64 * (j + 6):64 * (j + 7)] for j in range(6)])
    w_in2 = tiles(np.concatenate([i_q, i_k, i_k, a_ckv, c_q, c_g, b_k, b_v, b_q[:, perm], b_g[:, perm], a_q, a_g,
                                  mixg], axis=1))
    kv = I["w_kv_up_2"][0].reshape(2, 128, 12, 128)
    order = [x for h in range(6) for x in (h, 6 + h)]
    w_kv = kv[:, :, order].transpose(2, 1, 0, 3).reshape(3, 4, 128, 256).transpose(0, 2, 1, 3).reshape(3, 128, 1024)

    arrays = {
        "cst": cst, "masks": masks,
        "w_iw": i_w.reshape(16, 128, 16).transpose(1, 0, 2).reshape(128, 256),
        "xT": I["x"][0].T.reshape(16, 128, 512).transpose(1, 0, 2).reshape(128, 8192),
        "memT": I["mem_2"][0].T.reshape(16, 128, 256).transpose(1, 0, 2).reshape(128, 4096),
        "w_ada": I["w_ada"][0], "w_in": tiles(I["w_in"][0]), "w_out": tiles(I["w_out"][0]),
        "w_mem": tiles(I["w_mem_kv_2"][0]), "w_in2": w_in2, "w_kv": w_kv,
        "w_upa": tiles(I["w_up_a_2"][0], 6), "w_upb": tiles(I["w_up_b_2"][0][perm], 6),
        "w_upc": tiles(I["w_up_c_2"][0], 4), "w_o": tiles(I["w_o_2"][0]),
        "strip1": strip1, "strip_a": strip_a, "strip_b": strip_b,
    }
    arrays = {f"in_{k}": np.ascontiguousarray(v) for k, v in arrays.items()}
    nc = _bacc.Bacc("TRN2", target_bir_lowering=False, num_devices=1)
    io = {k[3:]: nc.dram_tensor(k, v.shape, mybir.dt.from_np(v.dtype), kind="ExternalInput").ap()
          for k, v in arrays.items()}
    io["out"] = nc.dram_tensor("out_0", (16, 128, 512), F32, kind="ExternalOutput").ap()
    for name, shape in (("x1s", (16, 128, 512)), ("mgs", (16, 128, 512)), ("kvs", (8, 128, 256))):
        io[name] = nc.dram_tensor(f"tmp_{name}", shape, F32, kind="Internal").ap()
    program(nc, io)
    r = _run(nc, [arrays], core_ids=[0])
    got = r.results[0]["out_0"]
    return np.ascontiguousarray(got.reshape(2048, 512).T).reshape(1, 512, 2048)
```

```python
from contextlib import ExitStack

import numpy as np

import concourse.bass as bass
from concourse import mybir

F32 = mybir.dt.float32
F32R = mybir.dt.float32r
U8 = mybir.dt.uint8
I32 = mybir.dt.int32
ALU = mybir.AluOpType
ACT = mybir.ActivationFunctionType
AX = mybir.AxisListType.X

P = 128
T = 512
NT = 4
D = 2048
KT = 16
EPS = 1e-6
NEG = -1e30
TOPK = 128
SC128 = float(np.float32(128.0 ** -0.5))
SC64 = 0.125

CST = {}


def _columns():
    at = 0
    for name, n in (("ident", 128), ("ones", 128), ("ones64", 128), ("causal", 128), ("norm_g", 16), ("b_ada", 48),
                    ("q_g", 1), ("k_g", 1), ("hg_g", 1), ("lb", 16), ("norm_g2", 16), ("kv_g", 2), ("ik_g", 1),
                    ("ik_b", 1), ("qa", 1), ("ka", 1), ("qb", 1), ("kb", 1), ("qc", 1), ("kc", 1), ("mem_g", 16),
                    ("gate_b", 48), ("sinks", 12), ("c", 16)):
        CST[name] = (at, n)
        at += n
    return at


NCST = _columns()


class Queue:

    def __init__(self, engine, sem):
        self.e, self.sem, self.n, self.met = engine, sem, 0, {}

    def wait(self, *marks):
        for sem, v in (m for m in marks if m is not None):
            if self.met.get(sem.name, 0) < v:
                self.met[sem.name] = v
                self.e.wait_ge(sem, v)

    def do(self, fn, *marks):
        self.wait(*marks)
        self.n += 1
        fn(self.e).then_inc(self.sem, 1)
        return (self.sem, self.n)

    def quiet(self, fn, *marks):
        self.wait(*marks)
        fn(self.e)

    def dma(self, dst, src, sem):
        self.e.dma_start(dst, src).then_inc(sem, 16)


class Chan:

    def __init__(self, sem):
        self.sem, self.n = sem, 0


class Buf:

    def __init__(self, ap, sem=None):
        self.ap, self.free, self.busy, self.chan = ap, (), False, sem

    def give(self, *marks):
        self.busy = False
        self.free = marks


def program(nc, io):
    with ExitStack() as ctx:
        def sb(name, shape, dt=F32):
            return ctx.enter_context(nc.sbuf_tensor(name, shape, dt))[:, :]

        def sem(name):
            return ctx.enter_context(nc.semaphore(name))

        def chan(name):
            return Chan(sem(name))

        H = [sb("Hhi", [P, KT * T], F32R), sb("Hlo", [P, KT * T], F32R)]
        Y = sb("Y", [P, KT * T])
        TA = sb("TA", [P, 9216])
        NRAW, NSPL = 3, 3
        wraw = [Buf(sb(f"wraw{i}", [P, 1024]), chan(f"s_wraw{i}")) for i in range(NRAW)]
        whi = [sb(f"whi{i}", [P, 1024], F32R) for i in range(NSPL)]
        wlo = [sb(f"wlo{i}", [P, 1024], F32R) for i in range(NSPL)]
        O2 = [sb("Ohi", [P, 6 * T], F32R), sb("Olo", [P, 6 * T], F32R)]
        CK = [sb("CKhi", [P, 2 * T], F32R), sb("CKlo", [P, 2 * T], F32R)]
        cst = sb("cst", [P, NCST])
        mk = sb("mk", [P, 8 * P], U8)
        small = sb("small", [P, 64])
        par = sb("par", [P, 112])
        ngb = sb("ngb", [P, 48])
        iwt = sb("iwt", [P, 64])
        rows = sb("rows", [P, T])

        bank = [Buf(ctx.enter_context(nc.psum_tensor(f"bank{i}", [P, 512], F32))[:, :]) for i in range(8)]
        PJ = bank[0:2]
        bST, bS0, bS1, bT, bO, bV = bank[2:8]

        pe, dve, act, pool, sp = (Queue(e, sem(n)) for e, n in (
            (nc.tensor, "s_pe"), (nc.vector, "s_dve"), (nc.scalar, "s_act"), (nc.gpsimd, "s_pool"), (nc.sync, "s_sp")))
        s_cst = [sem(f"s_cst{i}") for i in range(2)]

        def C(name, i=0, n=None):
            at, w = CST[name]
            return cst[:, at + i:at + (w if n is None else i + n)]

        nc.scalar.preload_act_table_set("natural_log_exp_and_others")

        urgent, behind, slow = [], [], []

        def pump():
            for line in (urgent, behind, slow):
                if line:
                    try:
                        next(line[0])
                    except StopIteration:
                        line.pop(0)

        def drain():
            while urgent or behind or slow:
                pump()

        def take(b):
            while b.busy:
                assert urgent or behind or slow
                pump()
            b.busy = True
            return b

        def until(there):
            while not there():
                assert urgent or behind or slow
                pump()

        def need(marks, *names):
            while any(n not in marks for n in names):
                yield

        def get(b):
            while b.busy:
                yield
            b.busy = True

        def load(q, b, dst, src, *marks):
            b.chan.n += 16
            q.wait(*marks)
            q.dma(dst, src, b.chan.sem)
            return (b.chan.sem, b.chan.n)

        for i, (dst, src) in enumerate(((cst, io["cst"]), (TA[:, 8192:9216].bitcast(I32), io["masks"]))):
            sp.dma(dst, src, s_cst[i])
        m_cst, m_mk = [(s_cst[i], 16) for i in range(2)]
        ident, ones, ones64 = C("ident"), C("ones"), C("ones64")

        m_mk = dve.do(lambda e: e.tensor_copy(mk, TA[:, 8192:9216].bitcast(I32)), m_mk)
        m_eps = dve.do(lambda e: e.memset(par[:, 92:93], EPS))
        eps = par[:, 92:93]

        items = []

        def plan(name, first, count, cols=1024):
            for i in range(first, first + count):
                items.append((io[name][i, :, 0:cols], cols, (name, i)))

        class Ring:
            i = n_split = n_dma = 0
            done = {}
            spl_free = [() for _ in range(NSPL)]
            held = [False] * NSPL

            def dma(self):
                j = self.n_dma
                b = wraw[j % NRAW]
                src, w, _ = items[j]
                b.mark = load(sp, b, b.ap[:, 0:w], src, *b.free)
                self.n_dma += 1

            def split(self):
                j = self.n_split
                b, s = wraw[j % NRAW], j % NSPL
                w = items[j][1]
                hi = act.do(lambda e: e.activation(whi[s][:, 0:w], b.ap[:, 0:w], ACT.Copy), b.mark, *self.spl_free[s])
                lo = pool.do(lambda e: e.tensor_tensor(wlo[s][:, 0:w], b.ap[:, 0:w], whi[s][:, 0:w].bitcast(F32),
                                                       ALU.subtract), hi)
                b.free = (hi, lo)
                self.done[j] = lo
                self.n_split += 1

            def take(self, key):
                i = self.i
                assert items[i][2] == key, (items[i][2], key)
                while self.n_dma < min(len(items), NRAW):
                    self.dma()
                while self.n_split < min(len(items), i + NSPL) and not self.held[self.n_split % NSPL]:
                    self.split()
                    if self.n_dma < len(items):
                        self.dma()
                self.i += 1
                self.held[i % NSPL] = True
                return whi[i % NSPL], wlo[i % NSPL], self.done[i], i % NSPL

            def give(self, s, mark):
                self.held[s] = False
                self.spl_free[s] = (mark,)

        ring = Ring()

        class Acts:

            def __init__(self, hi, lo, n, w):
                self.hi = [hi[:, k * w:(k + 1) * w] for k in range(n)]
                self.lo = [lo[:, k * w:(k + 1) * w] for k in range(n)]
                self.ready = [None] * n
                self.used = ()
                self.w = w

            def put(self, k, src, mark, on_dve=False):
                hi = act.do(lambda e: e.activation(self.hi[k], src, ACT.Copy), mark, *self.used)
                q = dve if on_dve else pool
                self.ready[k] = q.do(lambda e: e.tensor_tensor(self.lo[k], src, self.hi[k].bitcast(F32), ALU.subtract), hi)
                return self.ready[k]

        turn = [0]

        def open_bank():
            turn[0] += 1
            return take(PJ[turn[0] % 2])

        def part(b, x, piece, kts, off=0, first=False, last=False):
            hi, lo, there, _ = piece
            out = b.ap[:, 0:x.w]
            for j, k in enumerate(kts):
                until(lambda: x.ready[k] is not None)
                c = slice(off + j * P, off + (j + 1) * P)
                pe.wait(there, x.ready[k], *(b.free if first and j == 0 else ()))
                pe.quiet(lambda e: e.matmul(out, hi[:, c], x.hi[k], start=first and j == 0, stop=False))
                pe.quiet(lambda e: e.matmul(out, hi[:, c], x.lo[k], start=False, stop=False))
                f = lambda e: e.matmul(out, lo[:, c], x.hi[k], start=False, stop=last and j == len(kts) - 1)
                if j == len(kts) - 1:
                    m = pe.do(f)
                else:
                    pe.quiet(f)
                if j % 4 == 3:
                    pump()
            return m

        def full(x, name, nb):
            b = open_bank()
            for half in range(2):
                piece = ring.take((name, 2 * nb + half))
                m = part(b, x, piece, range(8 * half, 8 * half + 8), first=half == 0, last=half == 1)
                ring.give(piece[3], m)
            return b, m

        def thin(x, name, nb, n):
            b = open_bank()
            piece = ring.take((name, nb))
            m = part(b, x, piece, range(n), first=True, last=True)
            ring.give(piece[3], m)
            pump()
            return b, m

        def evac(b, m, dst, w=T, by=None):
            if by is not None:
                r = dve.do(lambda e: e.tensor_tensor(dst.ap[:, 0:w], b.ap[:, 0:w], by[0], ALU.mult), m, by[1], *dst.free)
            else:
                r = act.do(lambda e: e.activation(dst.ap[:, 0:w], b.ap[:, 0:w], ACT.Copy), m, *dst.free)
            b.give(r)
            return r

        class Work:

            def __init__(self, mem, t1, t2, sems):
                def piece(i, n=T):
                    return mem[:, i:i + n]
                self.Q = [Buf(piece(T * i), sems[i]) for i in range(2)]
                self.K = [Buf(piece(T * (2 + i)), sems[2 + i]) for i in range(2)]
                self.V = [Buf(piece(T * (4 + i)), sems[4 + i]) for i in range(2)]
                self.Z = [Buf(piece(T * (6 + i))) for i in range(2)]
                self.S = [Buf(piece(T * (8 + i))) for i in range(2)]
                self.PT = [Buf(piece(T * (10 + i))) for i in range(2)]
                self.ST = [Buf(piece(T * (12 + i)), sems[6 + i]) for i in range(2)]
                self.SQ, self.R = Buf(piece(T * 14)), Buf(piece(T * 15))
                self.t1, self.t2 = Buf(t1), Buf(t2)

            def all(self):
                return [*self.Q, *self.K, *self.V, *self.Z, *self.S, *self.PT, *self.ST, self.SQ, self.R]

        w_chans = [chan(f"s_w{i}") for i in range(10)]
        W1 = Work(TA, TA[:, 8192:8704], TA[:, 8704:9216], w_chans)
        W2 = Work(Y, TA[:, 8192:8704], TA[:, 8704:9216], w_chans)

        def rsq(W, w, n, src, mark):
            R = W.R.ap[:, 0:w]
            m = act.do(lambda e: e.activation(R, src, ACT.Ln, scale=1.0 / n, bias=eps), mark, m_eps, *W.R.free)
            return act.do(lambda e: e.activation(R, R, ACT.Exp, scale=-0.5), m), m

        def norm(W, raws, marks, over, n, gains, w=T, out=None):
            yield from get(bST)
            for i, (raw, mark) in enumerate(zip(raws, marks)):
                yield from get(W.SQ)
                m = act.do(lambda e: e.activation(W.SQ.ap[:, 0:w], raw, ACT.Square), mark, *W.SQ.free)
                yield
                m = pe.do(lambda e: e.matmul(bST.ap[:, 0:w], over, W.SQ.ap[:, 0:w], start=(i == 0), stop=(i == len(raws) - 1)),
                          m, m_cst, *bST.free)
                W.SQ.give(m)
            yield from get(W.R)
            r, ln = rsq(W, w, n, bST.ap[:, 0:w], m)
            bST.give(ln)
            for i, (raw, g) in enumerate(zip(raws, gains)):
                marks[i] = dve.do(lambda e: e.scalar_tensor_tensor(out=raw, in0=raw, scalar=g, in1=W.R.ap[:, 0:w],
                                                                   op0=ALU.mult, op1=ALU.mult), r)
            W.R.give(marks[-1])

        def sigma(W, x, mark, signs, bias=(0.0, 0.0)):
            yield from get(W.t1)
            t1, t2 = W.t1.ap[:, 0:x.shape[1]], W.t2.ap[:, 0:x.shape[1]]
            m = act.do(lambda e: e.activation(t1, x, ACT.Abs, bias=bias[0]), mark, *W.t1.free)
            m = act.do(lambda e: e.activation(t1, t1, ACT.Exp, scale=-1.0), m)
            m = act.do(lambda e: e.activation(t1, t1, ACT.Ln, bias=1.0), m)
            for sign, use in signs:
                yield from get(W.t2)
                if sign > 0:
                    a = dve.do(lambda e: e.scalar_tensor_tensor(out=t2, in0=x, scalar=bias[1], in1=t1, op0=ALU.min,
                                                                op1=ALU.subtract), m, *W.t2.free)
                    a = act.do(lambda e: e.activation(t2, t2, ACT.Exp, bias=bias[0]), a)
                else:
                    a = dve.do(lambda e: e.scalar_tensor_tensor(out=t2, in0=x, scalar=0.0, in1=t1, op0=ALU.max,
                                                                op1=ALU.add), m, *W.t2.free)
                    a = act.do(lambda e: e.activation(t2, t2, ACT.Exp, scale=-1.0), a)
                W.t2.give(use(t2, a))
                last = a
            W.t1.give(last, a)

        def silu(W, x, mark, out):
            def use(s, m):
                out[0] = pool.do(lambda e: e.tensor_tensor(x, x, s, ALU.mult), m)
                return out[0]
            yield from sigma(W, x, mark, [(1, use)])

        def turned(W, b, mark, out, n=NT):
            yield from get(bV)
            for i in range(n):
                m = pe.do(lambda e, i=i: e.transpose(bV.ap[:, i * P:(i + 1) * P], b.ap[:, i * P:(i + 1) * P], ident),
                          mark, m_cst, *bV.free)
            out[0] = dve.do(lambda e: e.tensor_copy(b.ap[:, 0:n * P], bV.ap[:, 0:n * P]), m)
            bV.give(out[0])
            yield

        col = [0]

        def scol():
            col[0] = (col[0] + 1) % 64
            return small[:, col[0]:col[0] + 1]

        def softmax_rows(W, sbuf, n, scale, strip, marks, extra=None, sink=None):
            bk, S = sbuf
            src, s = bk.ap[:, 0:n], S.ap[:, 0:n]
            if strip is not None:
                m = dve.do(lambda e: e.scalar_tensor_tensor(out=s, in0=src, scalar=scale, in1=strip, op0=ALU.mult,
                                                            op1=ALU.add), *marks, *S.free)
            else:
                m = dve.do(lambda e: e.tensor_scalar(s, src, scale, None, ALU.mult), *marks, *S.free)
            bk.give(m)
            if extra is not None:
                m = dve.do(lambda e: e.tensor_tensor(s, s, extra, ALU.add), m)
            nm, l, rl = scol(), scol(), scol()
            m = dve.do(lambda e: e.tensor_reduce(nm, s, AX, ALU.max, negate=True), m)
            if sink is not None:
                m = dve.do(lambda e: e.tensor_scalar(nm, nm, sink[1], None, ALU.min), m)
                es = scol()
                x = act.do(lambda e: e.activation(es, sink[0], ACT.Exp, bias=nm), m)
            m = act.do(lambda e: e.activation(s, s, ACT.Exp, bias=nm, accum_out=l), m)
            if sink is not None:
                m = dve.do(lambda e: e.tensor_tensor(l, l, es, ALU.add), m, x)
            m = dve.do(lambda e: e.reciprocal(rl, l), m)
            return dve.do(lambda e: e.tensor_scalar(s, s, rl, None, ALU.mult), m)

        def attention(W, Qb, Kb, Vb, ms, more, heads, blocks, rate=1):
            yield from need(ms, "q", "k")
            yield
            yield from get(bO)
            work = [(hd, i) for hd in heads for i in range(NT)]
            probs, ptm, sm = {}, {}, {}
            m_last = None
            for n in range(len(work) + 3):
                if 0 <= n - 2 < len(work):
                    w = n - 2
                    bl = blocks[work[w][1]]
                    S, PT = W.S[w % 2], W.PT[w % 2]
                    yield from get(bT)
                    yield from get(PT)
                    for j in range(len(bl)):
                        m = pe.do(lambda e: e.transpose(bT.ap[:, j * P:(j + 1) * P], S.ap[:, j * P:(j + 1) * P], ident),
                                  probs[w], *bT.free)
                    S.give(m)
                    ptm[w] = act.do(lambda e: e.activation(PT.ap[:, 0:P * len(bl)], bT.ap[:, 0:P * len(bl)], ACT.Copy),
                                    m, *PT.free)
                    bT.give(ptm[w])
                if n < len(work):
                    (rws, _, _, scale, strip, extra, sink), i = work[n]
                    N = P * len(blocks[i])
                    bk, S = (bS0, bS1)[n % 2], W.S[n % 2]
                    yield from get(bk)
                    yield from get(S)
                    k0 = blocks[i][0] * P
                    m = pe.do(lambda e: e.matmul(bk.ap[:, 0:N], Qb.ap[rws, i * P:(i + 1) * P], Kb.ap[rws, k0:k0 + N],
                                                 start=True, stop=True), ms["q"], ms["k"], *more, *bk.free)
                    m_scores = m
                    st = strip(i) if strip else (None, None)
                    ex = extra(i) if extra else (None, None)
                    probs[n] = softmax_rows(W, (bk, S), N, scale, st[0], [m, st[1], ex[1]], ex[0], sink)
                    m_soft = probs[n]
                if n >= 3:
                    w = n - 3
                    (_, vcols, orows, _, _, _, _), i = work[w]
                    bl, PT = blocks[i], W.PT[w % 2]
                    if w == 0:
                        yield from need(ms, "v")
                    for j, kb in enumerate(bl):
                        m_last = pe.do(lambda e: e.matmul(
                            bO.ap[orows, i * P:(i + 1) * P], Vb.ap[:, kb * P + vcols.start:kb * P + vcols.stop],
                            PT.ap[:, j * P:(j + 1) * P], start=(j == 0), stop=(j == len(bl) - 1)),
                            ptm[w], ms["v"], *more, *(bO.free if w == 0 else ()))
                    PT.give(m_last)
                if n % rate == rate - 1:
                    yield
            return m_last, m_soft, m_scores

        x1s, mks, kvs = io["x1s"], io["mgs"], io["kvs"]

        IQ, IK, CKV, CQ, CG, BK, BV, BQ, BG, AQ, AG, MA, MB, MC = 0, 8, 9, 11, 15, 19, 20, 21, 27, 33, 39, 45, 61, 77
        SHARE = (3, 3, 3, 3, 2, 2)
        for h in range(4):
            plan("w_mem", 2 * h, 2)
            plan("w_mem", 2 * (4 + h), 2)
        for h in range(8):
            for j in (5, 4, 6, 7):
                plan("w_in", 2 * (8 * j + h), 2)
        for h in range(8):
            for j in range(4):
                plan("w_in", 2 * (8 * j + h), 2)
        plan("w_out", 0, 32)
        for tile in (IK, *range(IQ, IQ + 8), *(c + h for h in range(4) for c in (CQ, CG)), CKV, CKV + 1, BK, BV):
            plan("w_in2", 2 * tile, 2)
        nb = 0
        for j in range(6):
            plan("w_in2", 2 * (BQ + j), 2)
            plan("w_in2", 2 * (BG + j), 2)
            for nb in range(nb, nb + SHARE[j]):
                plan("w_in2", 2 * (MC + nb), 2)
                plan("w_upc", nb, 1, 512)
            nb += 1
        nb = 0
        for j in range(6):
            plan("w_kv", j, 1, 512)
            plan("w_in2", 2 * (AQ + j), 2)
            plan("w_in2", 2 * (AG + j), 2)
            for nb in range(nb, nb + SHARE[j]):
                plan("w_in2", 2 * (MB + nb), 2)
                plan("w_upb", nb, 1, 768)
            nb += 1
        for nb in range(16):
            plan("w_in2", 2 * (MA + nb), 2)
            plan("w_upa", nb, 1, 768)
        plan("w_o", 0, 32)

        s_mem, s_x = [sem(f"s_mem{i}") for i in range(4)], [sem(f"s_x{i}") for i in range(4)]
        for i in range(4):
            sp.dma(Y[:, i * 1024:(i + 1) * 1024], io["memT"][:, i * 1024:(i + 1) * 1024], s_mem[i])
        act.wait(m_cst)
        dve.wait(m_cst)

        def small_sigmoid(x, out, tmp, mark=None):
            m = act.do(lambda e: e.activation(tmp, x, ACT.Abs), mark)
            m = act.do(lambda e: e.activation(tmp, tmp, ACT.Exp, scale=-1.0), m)
            m = act.do(lambda e: e.activation(tmp, tmp, ACT.Ln, bias=1.0), m)
            m = dve.do(lambda e: e.scalar_tensor_tensor(out=out, in0=x, scalar=0.0, in1=tmp, op0=ALU.min,
                                                        op1=ALU.subtract), m)
            return act.do(lambda e: e.activation(out, out, ACT.Exp), m)

        m = small_sigmoid(C("c"), par[:, 64:80], small[:, 0:16])
        m_c = dve.do(lambda e: e.tensor_tensor(par[:, 64:80], par[:, 64:80], C("c"), ALU.mult), m)
        m = dve.do(lambda e: e.tensor_tensor(small[:, 24:32], C("lb", 0, 8), C("lb", 8, 8), ALU.subtract))
        m = small_sigmoid(small[:, 24:32], par[:, 56:64], small[:, 32:40], m)
        m_lb = dve.do(lambda e: e.tensor_scalar(par[:, 48:56], par[:, 56:64], -1.0, 1.0, ALU.mult, ALU.add), m)
        m_ns = dve.do(lambda e: e.tensor_scalar(par[:, 80:92], C("sinks"), -1.0, None, ALU.mult))
        m_ng = dve.do(lambda e: e.tensor_scalar(ngb, C("gate_b"), -1.0, None, ALU.mult))

        ada = io["w_ada"].rearrange("(p j) n -> p j n", j=16)

        def ada_chunk(cc, acc, slots, *marks):
            m = None
            for j in range(16):
                s = slots[j % len(slots)]
                d = load(sp, s, s.ap, ada[:, j, cc * 1024:(cc + 1) * 1024], *s.free)
                cj = par[:, 64 + j:65 + j]
                if j == 0:
                    m = dve.do(lambda e: e.tensor_scalar(acc.ap, s.ap, cj, None, ALU.mult), d, m_c, *acc.free)
                else:
                    m = dve.do(lambda e: e.scalar_tensor_tensor(out=acc.ap, in0=s.ap, scalar=cj, in1=acc.ap,
                                                                op0=ALU.mult, op1=ALU.add), d, m)
                s.free = (m,)
                if j % 2:
                    yield
            for half in range(2):
                a = acc.ap[:, half * T:(half + 1) * T]
                yield from get(bO)
                r = pe.do(lambda e: e.matmul(bO.ap, ones, a, start=True, stop=True), m, m_cst, *bO.free)
                a3 = a.rearrange("p (i t) -> p i t", i=NT)
                r = dve.do(lambda e: e.tensor_tensor(a3, bO.ap.rearrange("p (i t) -> p i t", i=NT),
                                                     ident.unsqueeze(1).to_broadcast([P, NT, P]), ALU.mult), r)
                bO.give(r)
                c0 = 8 * cc + 4 * half
                r = dve.do(lambda e: e.tensor_reduce(par[:, c0:c0 + 4], a3, AX, ALU.add), r)
                r = dve.do(lambda e: e.tensor_tensor(par[:, c0:c0 + 4], par[:, c0:c0 + 4], C("b_ada", c0, 4), ALU.add), r)
            acc.free = (r,)
            ada_m[cc] = r

        ada_m = {}
        a_chans = [chan(f"s_ada{i}") for i in range(6)]
        a_slots = [Buf(TA[:, 2048 + 1024 * i:3072 + 1024 * i], a_chans[i]) for i in range(6)]
        a_acc = [Buf(TA[:, 1024 * i:1024 * i + 1024]) for i in range(2)]

        mem = Acts(H[1][:, 0:4096], H[1][:, 4096:8192], KT, 256)
        rr = TA[:, 8192:8448]
        sqb = [Buf(rows[:, 0:256]), Buf(rows[:, 256:512])]
        for k in range(KT):
            b = sqb[k % 2]
            m = act.do(lambda e: e.activation(b.ap, Y[:, k * 256:(k + 1) * 256], ACT.Square), (s_mem[k // 4], 16), *b.free)
            m = pe.do(lambda e: e.matmul(bST.ap[:, 0:256], ones, b.ap, start=(k == 0), stop=(k == KT - 1)), m, m_cst)
            b.free = (m,)
        m = act.do(lambda e: e.activation(rr, bST.ap[:, 0:256], ACT.Ln, scale=1.0 / D, bias=eps), m, m_eps, m_mk)
        bST.give(m)
        m_r = act.do(lambda e: e.activation(rr, rr, ACT.Exp, scale=-0.5), m)
        for i in (2, 3):
            sp.dma(Y[:, i * 2048:(i + 1) * 2048], io["xT"][:, i * 2048:(i + 1) * 2048], s_x[i])
        for k in range(KT):
            t = Y[:, k * 256:(k + 1) * 256]
            m = dve.do(lambda e: e.scalar_tensor_tensor(out=t, in0=t, scalar=C("mem_g", k, 1), in1=rr,
                                                        op0=ALU.mult, op1=ALU.mult), m_r)
            mem.put(k, t, m, on_dve=k % 3 != 0)
        for i in (0, 1):
            sp.wait(*mem.ready)
            sp.dma(Y[:, i * 2048:(i + 1) * 2048], io["xT"][:, i * 2048:(i + 1) * 2048], s_x[i])

        class WM:
            SQ, R = Buf(TA[:, 8448:8704]), Buf(TA[:, 8192:8448])
        w_mem = [Buf(TA[:, 8704 + 256 * i:8960 + 256 * i], w_chans[i]) for i in range(2)]
        for b in (*w_mem, WM.SQ, WM.R):
            b.free = (m, m_mk)
        m_kv = {}

        def mem_post(h, kind, b, mark):
            mm = [mark]
            if kind == 0:
                yield from norm(WM, [b.ap], mm, ones, 128, [C("kc")], w=256)
            else:
                yield from turned(WM, b, mark, mm, n=2)
            m_kv[h, kind] = load(sp, b, kvs[2 * h + kind], b.ap, mm[0])
            b.give(m_kv[h, kind])
            yield

        def x_norm():
            yield from get(bS0)
            m = None
            order = [*range(8, 16), *range(8)]
            for n, k in enumerate(order):
                m = act.do(lambda e: e.activation(rows, Y[:, k * T:(k + 1) * T], ACT.Square), (s_x[k // 4], 16), m,
                           *sqb[0].free, *sqb[1].free)
                yield
                m = pe.do(lambda e: e.matmul(bS0.ap, ones, rows, start=(n == 0), stop=(n == KT - 1)), m, *bS0.free)
            m = act.do(lambda e: e.activation(rows, bS0.ap, ACT.Ln, scale=1.0 / D, bias=eps), m)
            bS0.give(m)
            m = act.do(lambda e: e.activation(rows, rows, ACT.Exp, scale=-0.5), m)
            for k in range(KT):
                t = Y[:, k * T:(k + 1) * T]
                x_m[k] = dve.do(lambda e: e.tensor_tensor(t, t, rows, ALU.mult), m)
                if k % 2:
                    yield

        x_m = {}
        hx = Acts(H[0], H[1], KT, T)

        def h_prep(half):
            yield from need(x_m, *range(8 * half, 8 * half + 8))
            while not mem_done:
                yield
            hx.used = tuple(mem_done)
            c = slice(16 + 8 * half, 24 + 8 * half)
            m = dve.do(lambda e: e.tensor_scalar(par[:, c], par[:, c], 1.0, None, ALU.add), ada_m[2 + half], ada_m[half])
            m = dve.do(lambda e: e.tensor_tensor(par[:, c], par[:, c], C("norm_g", 8 * half, 8), ALU.mult), m)
            for k in range(8 * half, 8 * half + 8):
                t = Y[:, k * T:(k + 1) * T]
                r = dve.do(lambda e: e.tensor_scalar(t, t, par[:, 16 + k:17 + k], par[:, k:k + 1], ALU.mult, ALU.add),
                           m, x_m[k])
                hx.put(k, t, r, on_dve=k % 3 == 1)

        def conditioning():
            yield from ada_chunk(2, a_acc[0], a_slots)
            yield from ada_chunk(0, a_acc[1], a_slots)
            yield from h_prep(0)
            yield from ada_chunk(3, a_acc[0], a_slots)
            yield from ada_chunk(1, a_acc[1], a_slots)
            yield from h_prep(1)
            for b in (*g_slots, g_acc):
                b.free = tuple(hx.ready)
            for b in W1.all() + [W1.t1, W1.t2]:
                b.free = (*a_acc[0].free, *a_acc[1].free, *w_mem[0].free, *w_mem[1].free, *WM.SQ.free, *WM.R.free)
                b.busy = False
            for cc in (4, 5):
                yield from ada_chunk(cc, g_acc, g_slots)

        g_slots = [Buf(Y[:, 1024 * i:1024 * i + 1024], a_chans[i]) for i in range(3)]
        g_acc = Buf(Y[:, 3072:4096])
        mem_done = []
        for b in W1.all() + [W1.t1, W1.t2]:
            b.busy = True
        slow.append(conditioning())
        behind.append(x_norm())
        for h in range(4):
            for kind in range(2):
                bk, m = full(mem, "w_mem", h + 4 * kind)
                b = take(w_mem[kind])
                r = evac(bk, m, b, w=256)
                urgent.append(mem_post(h, kind, b, r))
        mem_done.append(m)

        yb = [Buf(Y[:, k * T:(k + 1) * T]) for k in range(KT)]
        y_m = [None] * KT
        causal1 = [list(range(i + 1)) for i in range(NT)]
        all_rows = slice(0, 128)

        def head_post(W, kind, b, mark, ms, name, gain=None, over=None, n=128):
            mm = [mark]
            if kind == "norm":
                yield from norm(W, [b.ap], mm, over or ones, n, [gain])
            elif kind == "turn":
                yield from turned(W, b, mark, mm)
            else:
                yield from silu(W, b.ap, mark, mm)
            ms[name] = mm[0]

        def take_head(W, wname, x, nb, b, kind, ms, name, by=None, **kw):
            bk, m = full(x, wname, nb)
            r = evac(bk, m, take(b), by=by)
            urgent.append(head_post(W, kind, b, r, ms, name, **kw))

        AD, OF1, OF2 = TA[:, 4096:4608], TA[:, 4608:4864], TA[:, 4864:5376]
        TOT = TA[:, 5376:5888]

        def hg_decay(h, b, mark, ms, F):
            def pos(s, m):
                ms["f"] = dve.do(lambda e: e.tensor_scalar(F.ap, s, par[:, 48 + h:49 + h], par[:, 56 + h:57 + h],
                                                           ALU.mult, ALU.add), m, m_lb, *F.free)
                return ms["f"]

            def neg(s, m):
                ms["k"] = dve.do(lambda e: e.tensor_scalar(b.ap, s, par[:, 48 + h:49 + h], None, ALU.mult), m)
                return ms["k"]
            yield from sigma(W1, b.ap, mark, [(1, pos), (-1, neg)])

        def hg_head(h, Qb, Kb, Vb, Zb, Fb, ms):
            W = W1
            yield from need(ms, "q", "k", "f")
            yield
            yield
            for b in (*W.S, *W.PT):
                yield from get(b)
            free = [x for b in (*W.S, *W.PT) for x in b.free]
            q, k = Qb.ap, Kb.ap
            up = [ms["q"], ms["k"], ms["f"]]
            if h == 0:
                free = [dve.do(lambda e: e.memset(AD, 0.0), *free)]
            tot, tot_m, done = Fb.ap, None, None
            for step, m in enumerate([0, 1, 2, 4, 8, 16, 32, 64]):
                bk = (bS0, bS1)[step % 2]
                yield from get(bk)
                for i in range(NT):
                    r = pe.do(lambda e: e.matmul(bk.ap[:, i * P:(i + 1) * P], k[:, i * P:(i + 1) * P],
                                                 q[:, i * P:(i + 1) * P], start=True, stop=True), *up, *bk.free)
                if m == 0:
                    up = [dve.do(lambda e: e.tensor_tensor(q, q, Fb.ap, ALU.mult), r)]
                else:
                    nb = T // (2 * m)
                    qv = q.rearrange("p (b two m) -> p b two m", two=2, m=m)
                    kv = k.rearrange("p (b two m) -> p b two m", two=2, m=m)
                    tv = tot.rearrange("p (b two) -> p b two", two=2)
                    tl = tv[:, :, 0:1].to_broadcast([P, nb, m])
                    tr = tv[:, :, 1:2].to_broadcast([P, nb, m])
                    u1 = dve.do(lambda e: e.tensor_tensor(qv[:, :, 1, :], qv[:, :, 1, :], tl, ALU.mult), r, tot_m)
                    u2 = dve.do(lambda e: e.tensor_tensor(kv[:, :, 0, :], kv[:, :, 0, :], tr, ALU.mult), r, tot_m)
                    new = TOT[:, T - 2 * nb:T - nb]
                    tot_m = dve.do(lambda e: e.tensor_tensor(new, tv[:, :, 0], tv[:, :, 1], ALU.mult), tot_m, *free)
                    tot = new
                    up = [u1, u2]
                msk = mk[:, step * P:(step + 1) * P].unsqueeze(1).to_broadcast([P, NT, P])
                done = dve.do(lambda e: e.copy_predicated(AD.rearrange("p (i t) -> p i t", i=NT), msk,
                                                          bk.ap.rearrange("p (i t) -> p i t", i=NT)), r, m_mk, done, *free)
                bk.give(done)
                yield
            yield from get(bS0)
            for i in range(2):
                r = pe.do(lambda e: e.matmul(bS0.ap[:, i * P:(i + 1) * P], k[:, 2 * i * P:(2 * i + 1) * P],
                                             q[:, (2 * i + 1) * P:(2 * i + 2) * P], start=True, stop=True), *up, *bS0.free)
            qv = q.rearrange("p (b two m) -> p b two m", two=2, m=P)
            kv = k.rearrange("p (b two m) -> p b two m", two=2, m=P)
            tv = tot.rearrange("p (b two) -> p b two", two=2)
            u1 = dve.do(lambda e: e.tensor_tensor(qv[:, :, 1, :], qv[:, :, 1, :], tv[:, :, 0:1].to_broadcast([P, 2, P]),
                                                  ALU.mult), r, tot_m)
            u2 = dve.do(lambda e: e.tensor_tensor(kv[:, :, 0, :], kv[:, :, 0, :], tv[:, :, 1:2].to_broadcast([P, 2, P]),
                                                  ALU.mult), r, tot_m)
            c1 = act.do(lambda e: e.activation(OF1, bS0.ap[:, 0:256], ACT.Copy), r, *free)
            bS0.give(c1)
            Fb.give(u2)
            yield
            yield from get(bS1)
            for i in range(2):
                r = pe.do(lambda e: e.matmul(bS1.ap[:, i * 256:(i + 1) * 256], k[:, i * P:(i + 1) * P], q[:, 256:512],
                                             start=True, stop=True), u1, u2, *bS1.free)
            c2 = act.do(lambda e: e.activation(OF2, bS1.ap, ACT.Copy), r, *free)
            bS1.give(c2)
            Qb.give(r)
            Kb.give(r)
            yield from need(ms, "v")
            yield
            yield from get(bO)
            pairs = [[(0, AD[:, 0:128])],
                     [(1, AD[:, 128:256]), (0, OF1[:, 0:128])],
                     [(2, AD[:, 256:384]), (0, OF2[:, 0:128]), (1, OF2[:, 256:384])],
                     [(3, AD[:, 384:512]), (2, OF1[:, 128:256]), (0, OF2[:, 128:256]), (1, OF2[:, 384:512])]]
            for i, ps in enumerate(pairs):
                for j, (kb, a) in enumerate(ps):
                    r = pe.do(lambda e: e.matmul(bO.ap[:, i * P:(i + 1) * P], Vb.ap[:, kb * P:(kb + 1) * P], a,
                                                 start=(j == 0), stop=(j == len(ps) - 1)), done, c1, c2, ms["v"], *bO.free)
            for b in (*W.S, *W.PT):
                b.give(r, tot_m)
            Vb.give(r)
            yield from get(W.SQ)
            m = act.do(lambda e: e.activation(W.SQ.ap, bO.ap, ACT.Square), r, *W.SQ.free)
            yield
            yield from get(bST)
            m = pe.do(lambda e: e.matmul(bST.ap, ones, W.SQ.ap, start=True, stop=True), m, *bST.free)
            W.SQ.give(m)
            yield from get(W.R)
            r, ln = rsq(W, T, 128, bST.ap, m)
            bST.give(ln)
            y = yb[8 + h].ap
            m = dve.do(lambda e: e.scalar_tensor_tensor(out=y, in0=bO.ap, scalar=C("hg_g"), in1=W.R.ap, op0=ALU.mult,
                                                        op1=ALU.mult), r, *hx.ready)
            bO.give(m)
            W.R.give(m)
            yield from need(ms, "z")
            y_m[8 + h] = dve.do(lambda e: e.tensor_tensor(y, y, Zb.ap, ALU.mult), m, ms["z"])
            Zb.give(y_m[8 + h])

        for h in range(8):
            W, ms = W1, {}
            bufs = W.Q[h % 2], W.K[h % 2], W.V[h % 2], W.Z[h % 2], W.ST[h % 2]
            bk, m = full(hx, "w_in", 40 + h)
            take(bufs[4])
            r = evac(bk, m, take(bufs[1]))
            urgent.append(hg_decay(h, bufs[1], r, ms, bufs[4]))
            take_head(W, "w_in", hx, 32 + h, bufs[0], "silu", ms, "q")
            behind.append(hg_head(h, *bufs, ms))
            take_head(W, "w_in", hx, 48 + h, bufs[2], "turn", ms, "v")
            take_head(W, "w_in", hx, 56 + h, bufs[3], "silu", ms, "z")

        def att_head(h, Qb, Kb, Vb, Zb, ms):
            W = W1
            yield from get(W.ST[h % 2])
            sbuf = W.ST[h % 2]
            d = load(sp, sbuf, sbuf.ap, io["strip1"][h], *sbuf.free)
            m, soft, scores = yield from attention(
                W, Qb, Kb, Vb, ms, (), [(all_rows, slice(0, 128), all_rows, SC128,
                                         lambda i: (sbuf.ap[:, 384 - 128 * i:512], d), None, None)], causal1)
            Qb.give(scores)
            Kb.give(scores)
            sbuf.give(soft)
            Vb.give(m)
            yield from need(ms, "z")
            y_m[h] = dve.do(lambda e: e.tensor_tensor(yb[h].ap, bO.ap, Zb.ap, ALU.mult), m, ms["z"], ada_m[4], ada_m[5])
            bO.give(y_m[h])
            Zb.give(y_m[h])

        for h in range(8):
            W, ms = W1, {}
            bufs = W.Q[h % 2], W.K[h % 2], W.V[h % 2], W.Z[h % 2]
            take_head(W, "w_in", hx, h, bufs[0], "norm", ms, "q", gain=C("q_g"))
            take_head(W, "w_in", hx, 8 + h, bufs[1], "norm", ms, "k", gain=C("k_g"))
            behind.append(att_head(h, *bufs, ms))
            take_head(W, "w_in", hx, 16 + h, bufs[2], "turn", ms, "v")
            bk, m = full(hx, "w_in", 24 + h)
            r = evac(bk, m, take(bufs[3]))
            urgent.append(head_post(W, "silu", bufs[3], r, ms, "z"))
        last_in = m

        yx = Acts(H[0], H[1], KT, T)
        yx.used = (last_in,)
        YO = [*range(8, 16), *range(8)]

        def y_prep():
            for n, k in enumerate(YO):
                while y_m[k] is None:
                    yield
                yx.put(k, yb[k].ap, y_m[k], on_dve=n % 3 == 1)

        slow.append(y_prep())
        R2 = rows
        s_x1 = sem("s_x1st")
        x1_m = [None] * KT
        hb = [Buf(TA[:, i * T:(i + 1) * T]) for i in range(4)]
        sqt = Buf(TA[:, 4 * T:5 * T])
        m_st = None

        def x1_block(nb, bk, m):
            nonlocal m_st
            b = xw[nb % 2]
            d = load(sp, b, b.ap, io["xT"][:, nb * T:(nb + 1) * T], *b.free)
            t = yb[nb].ap
            r = dve.do(lambda e: e.scalar_tensor_tensor(out=t, in0=bk.ap, scalar=par[:, 32 + nb:33 + nb], in1=b.ap,
                                                        op0=ALU.mult, op1=ALU.add), m, d, *yx.ready)
            bk.give(r)
            b.free = (r,)
            x1_m[nb] = r
            sp.wait(r)
            sp.dma(x1s[nb], t, s_x1)
            r = act.do(lambda e: e.activation(sqt.ap, t, ACT.Square), r, *sqt.free)
            m_st = pe.do(lambda e: e.matmul(bST.ap, ones, sqt.ap, start=(nb == 0), stop=(nb == KT - 1)), r, *bST.free)
            sqt.free = (m_st,)

        held = []
        for nb in range(2):
            bk = open_bank()
            p0 = ring.take(("w_out", 2 * nb))
            m = part(bk, yx, p0, YO[0:8], first=True)
            ring.give(p0[3], m)
            p1 = ring.take(("w_out", 2 * nb + 1))
            part(bk, yx, p1, YO[8:15])
            held.append((bk, p1))
        until(lambda: yx.ready[7] is not None)
        drain()
        w_free = tuple(x for b in W1.all() for x in b.free)
        xw = [Buf(TA[:, (5 + i) * T:(6 + i) * T], w_chans[8 + i]) for i in range(2)]
        for b in (*xw, *hb, sqt):
            b.free = w_free
        for nb, (bk, p1) in enumerate(held):
            m = part(bk, yx, p1, YO[15:16], off=7 * P, last=True)
            ring.give(p1[3], m)
            x1_block(nb, bk, m)
        for nb in range(2, KT):
            bk = open_bank()
            for half in range(2):
                p1 = ring.take(("w_out", 2 * nb + half))
                m = part(bk, yx, p1, YO[8 * half:8 * half + 8], first=half == 0, last=half == 1)
                ring.give(p1[3], m)
            x1_block(nb, bk, m)
        h2 = Acts(H[0], H[1], KT, T)
        h2.used = (m,)
        for k in range(KT):
            b = hb[k % 4]
            x = dve.do(lambda e: e.tensor_scalar(b.ap, yb[k].ap, C("norm_g2", k, 1), None, ALU.mult), x1_m[k], *b.free)
            b.free = (h2.put(k, b.ap, x, on_dve=k % 2 == 1),)
            if k == 3:
                m = act.do(lambda e: e.activation(R2, bST.ap, ACT.Ln, scale=1.0 / D, bias=eps), m_st)
                bST.give(m)
                m_R2 = act.do(lambda e: e.activation(R2, R2, ACT.Exp, scale=-0.5), m)
        by = (R2, m_R2)
        m_x1s = (s_x1, 16 * KT)

        W = W2
        for b in W2.all():
            b.free = (x, m_x1s)
        W2.t1.free = W2.t2.free = (*W1.t1.free, *W1.t2.free)
        ost = [Buf(TA[:, i * T:(i + 1) * T]) for i in range(6)]
        sc = TA[:, 3072:4224]
        gx = [Buf(TA[:, 4224 + i * T:4224 + (i + 1) * T]) for i in range(2)]
        ub = [Buf(TA[:, 5248 + i * T:5248 + (i + 1) * T], chan(f"s_u{i}")) for i in range(2)]
        lb_ = [Buf(TA[:, 6272 + i * T:6272 + (i + 1) * T], chan(f"s_l{i}")) for i in range(2)]
        rt = [Buf(TA[:, 7296:7808]), None]
        rt[1] = Buf(TA[:, 7808:8192])
        ta_free = (*h2.ready, *xw[0].free, *xw[1].free, *sqt.free, *w_free)
        for b in (*ost, *gx, *ub, *lb_, *rt):
            b.free = ta_free
        OFF = {1: 0, 2: 256, 3: 640}

        ik = W.K[0]
        bk, m = full(h2, "w_in2", IK)
        r_ik = evac(bk, m, take(ik), by=by)
        im = {}

        def ik_post():
            lo = slice(0, 64)
            yield from get(bV)
            for i in range(NT):
                m = pe.do(lambda e: e.transpose(bV.ap[:, 16 * i:16 * i + 16], ik.ap[64:80, i * P:(i + 1) * P],
                                                ident[64:80, 64:80]), r_ik, *bV.free)
            m = dve.do(lambda e: e.tensor_scalar(iwt, bV.ap[:, 0:64], 1.0 / 32, None, ALU.mult), m)
            bV.give(m)
            im["w"] = m
            yield from get(bST)
            m = pe.do(lambda e: e.matmul(bST.ap[lo, :], ones64[lo, lo], ik.ap[lo, :], start=True, stop=True),
                      r_ik, *bST.free)
            m = dve.do(lambda e: e.scalar_tensor_tensor(out=ik.ap[lo, :], in0=bST.ap[lo, :], scalar=-1.0 / 64,
                                                        in1=ik.ap[lo, :], op0=ALU.mult, op1=ALU.add), m)
            bST.give(m)
            yield
            yield from get(bST)
            yield from get(W.SQ)
            m = act.do(lambda e: e.activation(W.SQ.ap[lo, :], ik.ap[lo, :], ACT.Square), m, *W.SQ.free)
            m = pe.do(lambda e: e.matmul(bST.ap[lo, :], ones64[lo, lo], W.SQ.ap[lo, :], start=True, stop=True), m)
            W.SQ.give(m)
            yield from get(W.R)
            R = W.R.ap[lo, :]
            m = act.do(lambda e: e.activation(R, bST.ap[lo, :], ACT.Ln, scale=1.0 / 64, bias=eps[lo, :]), m, *W.R.free)
            bST.give(m)
            m = act.do(lambda e: e.activation(R, R, ACT.Exp, scale=-0.5), m)
            m = dve.do(lambda e: e.scalar_tensor_tensor(out=ik.ap[lo, :], in0=ik.ap[lo, :], scalar=C("ik_g")[lo, :],
                                                        in1=R, op0=ALU.mult, op1=ALU.mult), m)
            W.R.give(m)
            m = dve.do(lambda e: e.tensor_scalar(ik.ap[lo, :], ik.ap[lo, :], C("ik_b")[lo, :], None, ALU.add), m)
            im["k"] = dve.do(lambda e: e.tensor_copy(ik.ap[64:128, :], ik.ap[lo, :]), m, im["w"])

        urgent.append(ik_post())
        sc_m = {1: ta_free, 2: ta_free, 3: ta_free}

        def idx_head(j, Qb, ms):
            yield from need(im, "k", "w")
            yield
            n_rt = 0
            for hh in range(2):
                head = 2 * j + hh
                rws = slice(64 * hh, 64 * hh + 64)
                for i in (3, 2, 1):
                    n = P * (i + 1)
                    bk = (bS0, bS1)[i % 2]
                    yield from get(bk)
                    m = pe.do(lambda e: e.matmul(bk.ap[:, 0:n], Qb.ap[rws, i * P:(i + 1) * P], ik.ap[rws, 0:n],
                                                 start=True, stop=True), *ms, im["k"], *bk.free)
                    t = rt[0] if i != 2 else rt[1]
                    yield from get(t)
                    a = act.do(lambda e: e.activation(t.ap[:, 0:n], bk.ap[:, 0:n], ACT.Relu), m, *t.free)
                    bk.give(a)
                    s = sc[:, OFF[i]:OFF[i] + n]
                    wcol = iwt[:, 16 * i + head:16 * i + head + 1]
                    if head == 0:
                        m = dve.do(lambda e: e.tensor_scalar(s, t.ap[:, 0:n], wcol, None, ALU.mult), a, im["w"], *sc_m[i])
                    else:
                        m = dve.do(lambda e: e.scalar_tensor_tensor(out=s, in0=t.ap[:, 0:n], scalar=wcol, in1=s,
                                                                    op0=ALU.mult, op1=ALU.add), a, *sc_m[i])
                    t.give(m)
                    sc_m[i] = (m,)
                    if i == 2:
                        yield
                yield
            last = [x[0] for x in sc_m.values()]
            Qb.give(*last)
            if j == 7:
                ik.give(*last)
                im["done"] = None

        for j in range(8):
            Qb = W.Q[j % 2]
            bk, m = full(h2, "w_in2", IQ + j)
            r = evac(bk, m, take(Qb), by=by)
            behind.append(idx_head(j, Qb, [r]))

        tkm = par[:, 96:104]

        def topk():
            yield from need(im, "done")
            for i in (1, 2, 3):
                n = P * (i + 1)
                s = sc[:, OFF[i]:OFF[i] + n]
                d = sc[:, OFF[i] + n - P:OFF[i] + n]
                m = dve.do(lambda e: e.tensor_tensor(d, d, C("causal"), ALU.add), *sc_m[i])
                for r in range(TOPK // 8):
                    m = dve.do(lambda e: e.max(tkm, s), m)
                    m = dve.do(lambda e: e.match_replace(s, tkm, s, -3e38), m)
                    yield
                sc_m[i] = (dve.do(lambda e: e.tensor_scalar(s, s, -2e38, NEG, ALU.is_gt, ALU.mult), m),)

        slow.append(topk())

        o_m = {}

        def staged(h, Zb, ms, m, *gives):
            for b, mark in gives:
                b.give(mark)
            yield from need(ms, "z")
            r = dve.do(lambda e: e.tensor_tensor(ost[h].ap, bO.ap, Zb.ap, ALU.mult), m, ms["z"], *ost[h].free)
            bO.give(r)
            Zb.give(r)
            o_m[h] = r

        def c_head(h, Qb, Kb, Vb, Zb, ms):
            ms["k"] = load(sp, Kb, Kb.ap[:, 0:256], kvs[2 * h], m_kv[h, 0], *Kb.free)
            ms["v"] = load(sp, Vb, Vb.ap[:, 0:256], kvs[2 * h + 1], m_kv[h, 1], *Vb.free)
            yield from get(ost[h])
            m, soft, scores = yield from attention(
                W, Qb, Kb, Vb, ms, (), [(all_rows, slice(0, 128), all_rows, SC128, None, None, None)], [[0, 1]] * NT)
            yield from staged(h, Zb, ms, m, (Qb, scores), (Kb, scores), (Vb, m))

        for h in range(4):
            ms = {}
            bufs = W.Q[h % 2], W.K[h % 2], W.V[h % 2], W.Z[h % 2]
            take_head(W, "w_in2", h2, CQ + h, bufs[0], "norm", ms, "q", by=by, gain=C("qc"))
            take(bufs[1])
            take(bufs[2])
            behind.append(c_head(h, *bufs, ms))
            take_head(W, "w_in2", h2, CG + h, bufs[3], "silu", ms, "z", by=by)

        cx = Acts(CK[0], CK[1], 2, T)
        bufs = [take(W.K[0]), take(W.V[0])]
        cm = []
        for i in range(2):
            bk, m = full(h2, "w_in2", CKV + i)
            cm.append(evac(bk, m, bufs[i], by=by))

        def ck_post(bufs):
            yield from norm(W, [b.ap for b in bufs], cm, ones, 256, [C("kv_g", 0, 1), C("kv_g", 1, 1)])
            for i in range(2):
                bufs[i].give(cx.put(i, bufs[i].ap, cm[i]))

        urgent.append(ck_post(bufs))

        bK, bVv = W.K[1], W.V[1]
        kvm = {}
        take_head(W, "w_in2", h2, BK, bK, "norm", kvm, "k", by=by, gain=C("kb"), over=ones64, n=64)
        take_head(W, "w_in2", h2, BV, bVv, "turn", kvm, "v", by=by)
        until(lambda: len(o_m) == 4)
        oc = Acts(O2[0], O2[1], 6, T)
        for k in range(4):
            ost[k].give(oc.put(k, ost[k].ap, o_m[k], on_dve=k % 2 == 1))
        o_m.clear()
        window = [[0], [0, 1], [1, 2], [2, 3]]

        def b_pair(j, Qb, Zb, ms):
            yield from get(ost[j])
            heads = []
            for half, head in enumerate((j, j + 6)):
                yield from get(W.ST[half])
                rws = slice(64 * half, 64 * half + 64)
                sbuf = W.ST[half]
                d = load(sp, sbuf, sbuf.ap[:, 0:256], io["strip_b"][head], *sbuf.free)
                strip = lambda i, s=sbuf, d=d: (s.ap[:, 128:256] if i == 0 else s.ap[:, 0:256], d)
                heads.append((rws, rws, rws, SC64, strip, None,
                              (C("sinks", head, 1), par[:, 80 + head:81 + head])))
            yield from need(kvm, "k", "v")
            ms["k"], ms["v"] = kvm["k"], kvm["v"]
            m, soft, scores = yield from attention(W, Qb, bK, bVv, ms, (m_ns,), heads, window)
            gives = [(Qb, scores), (W.ST[0], soft), (W.ST[1], soft)]
            if j == 5:
                gives += [(bK, scores), (bVv, m)]
            yield from staged(j, Zb, ms, m, *gives)

        st_m = [None] * KT
        mg_m = [None] * KT
        mixed = [None]

        def mix_gate(b, mark, nb, gcol, out):
            def use(s, m):
                out.append(pool.do(lambda e: e.tensor_copy(b.ap, s), m))
                return out[0]
            yield from sigma(W2, b.ap, mark, [(1, use)],
                             bias=(C("gate_b", gcol + nb, 1), ngb[:, gcol + nb:gcol + nb + 1]))

        def mix(branch, MX, name, o, nk, gcol, y_free=()):
            for nb in range(KT):
                g = take(gx[nb % 2])
                bk, m = full(h2, "w_in2", MX + nb)
                r = evac(bk, m, g, by=by)
                out = []
                urgent.append(mix_gate(g, r, nb, gcol, out))
                lb, u = lb_[nb % 2], ub[nb % 2]
                if branch > 0:
                    d = load(sp, lb, lb.ap, mks[nb], st_m[nb], *lb.free)
                bk, m = thin(o, name, nb, nk)
                until(lambda: out)
                r = dve.do(lambda e: e.tensor_tensor(u.ap, bk.ap, g.ap, ALU.mult), m, out[0], *u.free)
                bk.give(r)
                g.give(r)
                if branch == 2:
                    r = dve.do(lambda e: e.tensor_tensor(yb[nb].ap, u.ap, lb.ap, ALU.add), r, d, *y_free)
                    lb.free = u.free = (r,)
                    mg_m[nb] = r
                else:
                    if branch == 1:
                        r = pool.do(lambda e: e.tensor_tensor(u.ap, u.ap, lb.ap, ALU.add), r, d)
                        lb.free = (r,)
                    st_m[nb] = load(sp, u, mks[nb], u.ap, r)
                    u.free = (st_m[nb],)
                mixed[0] = m
                yield

        mix_c = mix(0, MC, "w_upc", oc, 4, 32)
        for j in range(6):
            ms = {}
            Qb, Zb = W.Q[j % 2], W.Z[j % 2]
            take_head(W, "w_in2", h2, BQ + j, Qb, "norm", ms, "q", by=by, gain=C("qb"), over=ones64, n=64)
            behind.append(b_pair(j, Qb, Zb, ms))
            take_head(W, "w_in2", h2, BG + j, Zb, "silu", ms, "z", by=by)
            for _ in range(SHARE[j]):
                next(mix_c)
        until(lambda: len(o_m) == 6)
        ob = Acts(O2[0], O2[1], 6, T)
        ob.used = (mixed[0],)
        for k in range(6):
            ost[k].give(ob.put(k, ost[k].ap, o_m[k], on_dve=k % 2 == 1))
        o_m.clear()
        until(lambda: not slow)

        def a_head(h, Qb, Kb, Vb, Zb, ms):
            yield from get(ost[h])
            yield from get(W.ST[h % 2])
            sbuf = W.ST[h % 2]
            d = load(sp, sbuf, sbuf.ap, io["strip_a"][h], *sbuf.free)
            m, soft, scores = yield from attention(W, Qb, Kb, Vb, ms, (), [(
                all_rows, slice(0, 128), all_rows, SC128, lambda i: (sbuf.ap[:, 384 - 128 * i:512], d),
                lambda i: (sc[:, OFF[i]:OFF[i] + P * (i + 1)], sc_m[i][0]) if i else (None, None), None)], causal1)
            yield from staged(h, Zb, ms, m, (Qb, scores), (Kb, scores), (Vb, m), (sbuf, soft))

        mix_b = mix(1, MB, "w_upb", ob, 6, 16)
        for h in range(6):
            ms = {}
            bufs = W.Q[h % 2], W.K[h % 2], W.V[h % 2], W.Z[h % 2]
            piece = ring.take(("w_kv", h))
            for kind in range(2):
                bk = open_bank()
                m = part(bk, cx, piece, range(2), off=256 * kind, first=True, last=True)
                r = evac(bk, m, take(bufs[1 + kind]))
                urgent.append(head_post(W, ("norm", "turn")[kind], bufs[1 + kind], r, ms, "kv"[kind], gain=C("ka")))
            ring.give(piece[3], m)
            take_head(W, "w_in2", h2, AQ + h, bufs[0], "norm", ms, "q", by=by, gain=C("qa"))
            behind.append(a_head(h, *bufs, ms))
            take_head(W, "w_in2", h2, AG + h, bufs[3], "silu", ms, "z", by=by)
            for _ in range(SHARE[h]):
                next(mix_b)
        until(lambda: len(o_m) == 6)
        drain()
        oa = Acts(O2[0], O2[1], 6, T)
        oa.used = (mixed[0],)
        for k in range(6):
            ost[k].give(oa.put(k, ost[k].ap, o_m[k], on_dve=k % 2 == 1))
        for _ in mix(2, MA, "w_upa", oa, 6, 0, tuple(x for b in W2.all() for x in b.free)):
            pass
        mix_last = mixed[0]

        mx = Acts(H[0], H[1], KT, T)
        mx.used = (mix_last,)
        for k in range(KT):
            mx.put(k, yb[k].ap, mg_m[k], on_dve=k % 3 == 1)
        out_m = []
        for nb in range(KT):
            lb, u = lb_[nb % 2], ub[nb % 2]
            d = load(sp, lb, lb.ap, x1s[nb], m_x1s, *lb.free)
            bk, m = full(mx, "w_o", nb)
            r = dve.do(lambda e, bk=bk, u=u, lb=lb: e.tensor_tensor(u.ap, bk.ap, lb.ap, ALU.add), m, d, *u.free)
            bk.give(r)
            lb.free = (r,)
            s = load(sp, u, io["out"][nb], u.ap, r)
            u.free = (s,)
            out_m.append(s)
        sp.wait(*out_m, *st_m, m_x1s, *m_kv.values())
        assert ring.i == len(items)


def buckets():
    n = np.arange(512)
    nf = np.maximum(n, 1).astype(np.float32)
    large = 16 + (np.log(nf / np.float32(16)) / np.float32(np.log(8.0)) * np.float32(16)).astype(np.int32)
    return np.where(n < 16, n, np.minimum(large, 31))


def tiles(w, kt=8):
    K, N = w.shape
    return np.ascontiguousarray(
        w.reshape(K // (128 * kt), kt, 128, N // 128, 128).transpose(3, 0, 2, 1, 4).reshape(-1, 128, kt * 128))


def kernel(**inputs):
    import concourse.bacc as _bacc
    from concourse.bass_utils import run_bass_kernel_spmd as _run

    I = {k: np.asarray(v) for k, v in inputs.items()}
    f32 = np.float32

    def feat(a, n):
        return a.reshape(n, 128).T

    ar = np.arange(128)
    p, u = ar[:, None], np.arange(512)[None, :]
    cols = {
        "ident": np.eye(128, dtype=f32), "ones": np.ones((128, 128), f32),
        "ones64": np.kron(np.eye(2), np.ones((64, 64))).astype(f32),
        "causal": np.where(p >= ar[None, :], 0, NEG).astype(f32),
        "norm_g": feat(I["norm_g"], 16), "b_ada": feat(I["b_ada"], 48),
        "q_g": I["q_norm_g"].T, "k_g": I["k_norm_g"].T, "hg_g": I["hg_norm_g"].T,
        "lb": np.concatenate([feat(I["lower_bounds"][i], 8) for i in range(2)], 1),
        "norm_g2": feat(I["norm_g_2"], 16), "kv_g": feat(I["kv_norm_g_2"], 2),
        "ik_g": np.concatenate([I["idx_k_ln_g_2"].T] * 2), "ik_b": np.concatenate([I["idx_k_ln_b_2"].T] * 2),
        "qa": I["q_norm_a_2"].T, "ka": I["k_norm_a_2"].T,
        "qb": np.concatenate([I["q_norm_b_2"].T] * 2), "kb": np.concatenate([I["k_norm_b_2"].T] * 2),
        "qc": I["q_norm_c_2"].T, "kc": I["k_norm_c_2"].T, "mem_g": feat(I["mem_norm_g_2"], 16),
        "gate_b": feat(I["gate_bias_2"], 48), "sinks": np.broadcast_to(I["sinks_b_2"], (128, 12)),
        "c": I["c"].reshape(128, 16),
    }
    cst = np.zeros((128, NCST), f32)
    for name, (at, n) in CST.items():
        cst[:, at:at + n] = cols[name]
    s, t = ar[:, None], ar[None, :]
    masks = [s == t] + [(s // (2 * m) == t // (2 * m)) & (s // m % 2 == 0) & (t // m % 2 == 1)
                        for m in (1, 2, 4, 8, 16, 32, 64)]
    masks = np.concatenate(masks, 1).astype(np.int32)

    neg = f32(NEG)
    d = p - (u - 384)
    strip1 = I["rel_bias"][0][:, np.clip(d, -128, 128) + 128]
    strip1 = np.where((p < 64) & (u >= 448), neg, strip1)
    bk = buckets()
    ra, rb = I["rel_bias_2"][:, :6].T, I["rel_bias_2"][:, 6:].T
    strip_a = np.where(d >= 0, ra[:, bk[np.clip(d, 0, 511)]], neg)
    db = p - (u[:, :256] - 128)
    strip_b = np.where((db >= 0) & (db < 128), rb[:, bk[np.clip(db, 0, 511)]], neg)

    w2 = I["w_in_2"][0]
    sizes = (768, 256, 1024, 64, 16, 768, 768, 128, 128, 768, 512, 512, 6144)
    cuts = np.cumsum(np.array(sizes))[:-1].tolist()
    a_q, a_ckv, i_q, i_k, i_w, a_g, b_q, b_k, b_v, b_g, c_q, c_g, mixg = np.split(w2, cuts, axis=1)
    perm = np.concatenate([np.r_[64 * j:64 * j + 64, 64 * (j + 6):64 * (j + 7)] for j in range(6)])
    w_in2 = tiles(np.concatenate([i_q, i_k, i_w, np.zeros((2048, 48), f32), a_ckv, c_q, c_g, b_k, b_v, b_q[:, perm], b_g[:, perm], a_q, a_g,
                                  mixg], axis=1))
    kv = I["w_kv_up_2"][0].reshape(2, 128, 12, 128)
    order = [x for h in range(6) for x in (h, 6 + h)]
    w_kv = kv[:, :, order].transpose(2, 1, 0, 3).reshape(6, 2, 128, 256).transpose(0, 2, 1, 3).reshape(6, 128, 512)

    arrays = {
        "cst": cst, "masks": masks,
        "xT": I["x"][0].T.reshape(16, 128, 512).transpose(1, 0, 2).reshape(128, 8192),
        "memT": I["mem_2"][0].T.reshape(16, 128, 256).transpose(1, 0, 2).reshape(128, 4096),
        "w_ada": I["w_ada"][0], "w_in": tiles(I["w_in"][0]), "w_out": tiles(np.roll(I["w_out"][0], 1024, axis=0)),
        "w_mem": tiles(I["w_mem_kv_2"][0]), "w_in2": w_in2, "w_kv": w_kv,
        "w_upa": tiles(I["w_up_a_2"][0], 6), "w_upb": tiles(I["w_up_b_2"][0][perm], 6),
        "w_upc": tiles(I["w_up_c_2"][0], 4), "w_o": tiles(I["w_o_2"][0]),
        "strip1": strip1, "strip_a": strip_a, "strip_b": strip_b,
    }
    arrays = {f"in_{k}": np.ascontiguousarray(v) for k, v in arrays.items()}
    nc = _bacc.Bacc("TRN2", target_bir_lowering=False, num_devices=1)
    io = {k[3:]: nc.dram_tensor(k, v.shape, mybir.dt.from_np(v.dtype), kind="ExternalInput").ap()
          for k, v in arrays.items()}
    io["out"] = nc.dram_tensor("out_0", (16, 128, 512), F32, kind="ExternalOutput").ap()
    for name, shape in (("x1s", (16, 128, 512)), ("mgs", (16, 128, 512)), ("kvs", (8, 128, 256))):
        io[name] = nc.dram_tensor(f"tmp_{name}", shape, F32, kind="Internal").ap()
    program(nc, io)
    r = _run(nc, [arrays], core_ids=[0])
    got = r.results[0]["out_0"]
    return np.ascontiguousarray(got.reshape(2048, 512).T).reshape(1, 512, 2048)
```

```python
from contextlib import ExitStack

import numpy as np

import concourse.bass as bass
from concourse import mybir

F32 = mybir.dt.float32
F32R = mybir.dt.float32r
U8 = mybir.dt.uint8
I32 = mybir.dt.int32
ALU = mybir.AluOpType
ACT = mybir.ActivationFunctionType
AX = mybir.AxisListType.X

P = 128
T = 512
NT = 4
D = 2048
KT = 16
EPS = 1e-6
NEG = -1e30
TOPK = 128
SC128 = float(np.float32(128.0 ** -0.5))
SC64 = 0.125

CST = {}


def _columns():
    at = 0
    for name, n in (("ident", 128), ("ones", 128), ("ones64", 128), ("causal", 128), ("norm_g", 16), ("b_ada", 48),
                    ("q_g", 1), ("k_g", 1), ("hg_g", 1), ("lb", 16), ("norm_g2", 16), ("kv_g", 2), ("ik_g", 1),
                    ("ik_b", 1), ("qa", 1), ("ka", 1), ("qb", 1), ("kb", 1), ("qc", 1), ("kc", 1), ("mem_g", 16),
                    ("gate_b", 48), ("sinks", 12), ("c", 16)):
        CST[name] = (at, n)
        at += n
    return at


NCST = _columns()


class Queue:

    def __init__(self, engine, sem):
        self.e, self.sem, self.n, self.met = engine, sem, 0, {}

    def wait(self, *marks):
        for sem, v in (m for m in marks if m is not None):
            if self.met.get(sem.name, 0) < v:
                self.met[sem.name] = v
                self.e.wait_ge(sem, v)

    def do(self, fn, *marks):
        self.wait(*marks)
        self.n += 1
        fn(self.e).then_inc(self.sem, 1)
        return (self.sem, self.n)

    def quiet(self, fn, *marks):
        self.wait(*marks)
        fn(self.e)

    def dma(self, dst, src, sem):
        self.e.dma_start(dst, src).then_inc(sem, 16)


class Chan:

    def __init__(self, sem):
        self.sem, self.n = sem, 0


class Buf:

    def __init__(self, ap, sem=None):
        self.ap, self.free, self.busy, self.chan = ap, (), False, sem

    def give(self, *marks):
        self.busy = False
        self.free = marks


def program(nc, io):
    with ExitStack() as ctx:
        def sb(name, shape, dt=F32):
            return ctx.enter_context(nc.sbuf_tensor(name, shape, dt))[:, :]

        def sem(name):
            return ctx.enter_context(nc.semaphore(name))

        def chan(name):
            return Chan(sem(name))

        H = [sb("Hhi", [P, KT * T], F32R), sb("Hlo", [P, KT * T], F32R)]
        Y = sb("Y", [P, KT * T])
        TA = sb("TA", [P, 9216])
        NRAW, NSPL = 3, 3
        wraw = [Buf(sb(f"wraw{i}", [P, 1024]), chan(f"s_wraw{i}")) for i in range(NRAW)]
        whi = [sb(f"whi{i}", [P, 1024], F32R) for i in range(NSPL)]
        wlo = [sb(f"wlo{i}", [P, 1024], F32R) for i in range(NSPL)]
        with nc.sbuf_tensor("first", [P, 8192], F32) as first:
            first = first[:, :]
        O2 = [sb("Ohi", [P, 6 * T], F32R), sb("Olo", [P, 6 * T], F32R)]
        CK = [sb("CKhi", [P, 2 * T], F32R), sb("CKlo", [P, 2 * T], F32R)]
        cst = sb("cst", [P, NCST])
        mk = sb("mk", [P, 8 * P], U8)
        small = sb("small", [P, 64])
        par = sb("par", [P, 112])
        ngb = sb("ngb", [P, 48])
        iwt = sb("iwt", [P, 64])
        rows = sb("rows", [P, T])

        bank = [Buf(ctx.enter_context(nc.psum_tensor(f"bank{i}", [P, 512], F32))[:, :]) for i in range(8)]
        PJ = bank[0:2]
        bST, bS0, bS1, bT, bO, bV = bank[2:8]

        pe, dve, act, pool, sp = (Queue(e, sem(n)) for e, n in (
            (nc.tensor, "s_pe"), (nc.vector, "s_dve"), (nc.scalar, "s_act"), (nc.gpsimd, "s_pool"), (nc.sync, "s_sp")))
        s_cst = [sem(f"s_cst{i}") for i in range(2)]

        def C(name, i=0, n=None):
            at, w = CST[name]
            return cst[:, at + i:at + (w if n is None else i + n)]

        nc.scalar.preload_act_table_set("natural_log_exp_and_others")

        urgent, behind, slow = [], [], []

        def pump():
            for line in (urgent, behind, slow):
                if line:
                    try:
                        next(line[0])
                    except StopIteration:
                        line.pop(0)

        def drain():
            while urgent or behind or slow:
                pump()

        def take(b):
            while b.busy:
                assert urgent or behind or slow
                pump()
            b.busy = True
            return b

        def until(there):
            while not there():
                assert urgent or behind or slow
                pump()

        def need(marks, *names):
            while any(n not in marks for n in names):
                yield

        def get(b):
            while b.busy:
                yield
            b.busy = True

        def load(q, b, dst, src, *marks):
            b.chan.n += 16
            q.wait(*marks)
            q.dma(dst, src, b.chan.sem)
            return (b.chan.sem, b.chan.n)

        for i, (dst, src) in enumerate(((cst, io["cst"]), (TA[:, 8192:9216].bitcast(I32), io["masks"]))):
            sp.dma(dst, src, s_cst[i])
        m_cst, m_mk = [(s_cst[i], 16) for i in range(2)]
        ident, ones, ones64 = C("ident"), C("ones"), C("ones64")

        m_mk = dve.do(lambda e: e.tensor_copy(mk, TA[:, 8192:9216].bitcast(I32)), m_mk)
        m_eps = dve.do(lambda e: e.memset(par[:, 92:93], EPS))
        eps = par[:, 92:93]

        items = []

        def plan(name, first, count, cols=1024):
            for i in range(first, first + count):
                items.append((io[name][i, :, 0:cols], cols, (name, i)))

        class Ring:
            i = n_split = n_dma = 0
            done = {}
            spl_free = [() for _ in range(NSPL)]
            held = [False] * NSPL

            early = True

            def dma(self, upto):
                while self.n_dma < min(len(items), upto - (1 if self.early else 0)):
                    j = self.n_dma
                    b = wraw[j % NRAW]
                    src, w, _ = items[j]
                    b.mark = load(act if self.early else sp, b, b.ap[:, 0:w], src, *b.free)
                    self.n_dma += 1

            def split(self):
                j = self.n_split
                b, s = wraw[j % NRAW], j % NSPL
                w = items[j][1]
                hi = act.do(lambda e: e.activation(whi[s][:, 0:w], b.ap[:, 0:w], ACT.Copy), b.mark, *self.spl_free[s])
                lo = pool.do(lambda e: e.tensor_tensor(wlo[s][:, 0:w], b.ap[:, 0:w], whi[s][:, 0:w].bitcast(F32),
                                                       ALU.subtract), hi)
                b.free = (hi, lo)
                self.done[j] = lo
                self.n_split += 1

            def take(self, key):
                i = self.i
                assert items[i][2] == key, (items[i][2], key)
                self.dma(self.n_split + NRAW)
                self.ahead()
                self.i += 1
                self.held[i % NSPL] = True
                return whi[i % NSPL], wlo[i % NSPL], self.done[i], i % NSPL

            def ahead(self):
                while self.n_split < min(len(items), self.i + NSPL) and not self.held[self.n_split % NSPL]:
                    self.split()
                    self.dma(self.n_split + NRAW)

            def give(self, s, mark):
                self.held[s] = False
                self.spl_free[s] = (mark,)

        ring = Ring()

        class Acts:

            def __init__(self, hi, lo, n, w):
                self.hi = [hi[:, k * w:(k + 1) * w] for k in range(n)]
                self.lo = [lo[:, k * w:(k + 1) * w] for k in range(n)]
                self.ready = [None] * n
                self.used = ()
                self.w = w

            def put(self, k, src, mark, on_dve=False):
                hi = act.do(lambda e: e.activation(self.hi[k], src, ACT.Copy), mark, *self.used)
                q = dve if on_dve else pool
                self.ready[k] = q.do(lambda e: e.tensor_tensor(self.lo[k], src, self.hi[k].bitcast(F32), ALU.subtract), hi)
                return self.ready[k]

        turn = [0]

        def open_bank():
            turn[0] += 1
            return take(PJ[turn[0] % 2])

        def part(b, x, piece, kts, off=0, first=False, last=False):
            hi, lo, there, _ = piece
            out = b.ap[:, 0:x.w]
            for j, k in enumerate(kts):
                until(lambda: x.ready[k] is not None)
                c = slice(off + j * P, off + (j + 1) * P)
                pe.wait(there, x.ready[k], *(b.free if first and j == 0 else ()))
                pe.quiet(lambda e: e.matmul(out, hi[:, c], x.hi[k], start=first and j == 0, stop=False))
                pe.quiet(lambda e: e.matmul(out, hi[:, c], x.lo[k], start=False, stop=False))
                f = lambda e: e.matmul(out, lo[:, c], x.hi[k], start=False, stop=last and j == len(kts) - 1)
                if j == len(kts) - 1:
                    m = pe.do(f)
                else:
                    pe.quiet(f)
                if j % 4 == 3:
                    pump()
            return m

        def full(x, name, nb, halves=(0, 1), between=None, ks=range(16)):
            b = open_bank()
            for n, half in enumerate(halves):
                piece = ring.take((name, 2 * nb + half))
                m = part(b, x, piece, ks[8 * half:8 * half + 8], first=n == 0, last=n == 1)
                ring.give(piece[3], m)
                if between and n == 0:
                    ring.ahead()
                    between(m)
            return b, m

        def thin(x, name, nb, n):
            b = open_bank()
            piece = ring.take((name, nb))
            m = part(b, x, piece, range(n), first=True, last=True)
            ring.give(piece[3], m)
            pump()
            return b, m

        def evac(b, m, dst, w=T, by=None):
            if by is not None:
                r = dve.do(lambda e: e.tensor_tensor(dst.ap[:, 0:w], b.ap[:, 0:w], by[0], ALU.mult), m, by[1], *dst.free)
            else:
                r = act.do(lambda e: e.activation(dst.ap[:, 0:w], b.ap[:, 0:w], ACT.Copy), m, *dst.free)
            b.give(r)
            return r

        class Work:

            def __init__(self, mem, t1, t2, sems, more=[]):
                def piece(i, n=T):
                    return mem[:, i:i + n]
                self.Q = [Buf(piece(T * i), sems[i]) for i in range(2)]
                self.K = [Buf(piece(T * (2 + i)), sems[2 + i]) for i in range(2)]
                self.V = [Buf(piece(T * (4 + i)), sems[4 + i]) for i in range(2)]
                self.Z = [Buf(piece(T * (6 + i))) for i in range(2)]
                self.S = [Buf(piece(T * (8 + i))) for i in range(2)] + more
                self.PT = [Buf(piece(T * (10 + i))) for i in range(2)]
                self.ST = [Buf(piece(T * (12 + i)), sems[6 + i]) for i in range(2)]
                self.SQ, self.R = Buf(piece(T * 14)), Buf(piece(T * 15))
                self.t1, self.t2 = Buf(t1), Buf(t2)

            def all(self):
                return [*self.Q, *self.K, *self.V, *self.Z, *self.S, *self.PT, *self.ST, self.SQ, self.R]

        w_chans = [chan(f"s_w{i}") for i in range(10)]
        W1 = Work(TA, TA[:, 8192:8704], TA[:, 8704:9216], w_chans)
        W2 = Work(Y, TA[:, 8192:8704], TA[:, 8704:9216], w_chans, [Buf(TA[:, 7296:7808])])

        def rsq(W, w, n, src, mark):
            R = W.R.ap[:, 0:w]
            m = act.do(lambda e: e.activation(R, src, ACT.Ln, scale=1.0 / n, bias=eps), mark, m_eps, *W.R.free)
            return act.do(lambda e: e.activation(R, R, ACT.Exp, scale=-0.5), m), m

        def norm(W, raws, marks, over, n, gains, w=T, out=None):
            yield from get(bST)
            for i, (raw, mark) in enumerate(zip(raws, marks)):
                yield from get(W.SQ)
                m = act.do(lambda e: e.activation(W.SQ.ap[:, 0:w], raw, ACT.Square), mark, *W.SQ.free)
                yield
                m = pe.do(lambda e: e.matmul(bST.ap[:, 0:w], over, W.SQ.ap[:, 0:w], start=(i == 0), stop=(i == len(raws) - 1)),
                          m, m_cst, *bST.free)
                W.SQ.give(m)
            yield from get(W.R)
            r, ln = rsq(W, w, n, bST.ap[:, 0:w], m)
            bST.give(ln)
            for i, (raw, g) in enumerate(zip(raws, gains)):
                marks[i] = dve.do(lambda e: e.scalar_tensor_tensor(out=raw, in0=raw, scalar=g, in1=W.R.ap[:, 0:w],
                                                                   op0=ALU.mult, op1=ALU.mult), r)
            W.R.give(marks[-1])

        def sigma(W, x, mark, signs, bias=(0.0, 0.0)):
            yield from get(W.t1)
            t1, t2 = W.t1.ap[:, 0:x.shape[1]], W.t2.ap[:, 0:x.shape[1]]
            m = act.do(lambda e: e.activation(t1, x, ACT.Abs, bias=bias[0]), mark, *W.t1.free)
            m = act.do(lambda e: e.activation(t1, t1, ACT.Exp, scale=-1.0), m)
            m = act.do(lambda e: e.activation(t1, t1, ACT.Ln, bias=1.0), m)
            yield
            for sign, use in signs:
                yield from get(W.t2)
                if sign > 0:
                    a = dve.do(lambda e: e.scalar_tensor_tensor(out=t2, in0=x, scalar=bias[1], in1=t1, op0=ALU.min,
                                                                op1=ALU.subtract), m, *W.t2.free)
                    yield
                    a = act.do(lambda e: e.activation(t2, t2, ACT.Exp, bias=bias[0]), a)
                else:
                    a = dve.do(lambda e: e.scalar_tensor_tensor(out=t2, in0=x, scalar=0.0, in1=t1, op0=ALU.max,
                                                                op1=ALU.add), m, *W.t2.free)
                    a = act.do(lambda e: e.activation(t2, t2, ACT.Exp, scale=-1.0), a)
                W.t2.give(use(t2, a))
                last = a
            W.t1.give(last, a)

        def silu(W, x, mark, out):
            def use(s, m):
                out[0] = pool.do(lambda e: e.tensor_tensor(x, x, s, ALU.mult), m)
                return out[0]
            yield from sigma(W, x, mark, [(1, use)])

        def turned(W, b, mark, out, n=NT):
            yield from get(bV)
            for i in range(n):
                m = pe.do(lambda e, i=i: e.transpose(bV.ap[:, i * P:(i + 1) * P], b.ap[:, i * P:(i + 1) * P], ident),
                          mark, m_cst, *bV.free)
            out[0] = dve.do(lambda e: e.tensor_copy(b.ap[:, 0:n * P], bV.ap[:, 0:n * P]), m)
            bV.give(out[0])
            yield

        col = [0]

        def scol():
            col[0] = (col[0] + 1) % 64
            return small[:, col[0]:col[0] + 1]

        def softmax_rows(W, sbuf, n, scale, strip, marks, extra=None, sink=None):
            bk, S = sbuf
            src, s = bk.ap[:, 0:n], S.ap[:, 0:n]
            if strip is not None:
                m = dve.do(lambda e: e.scalar_tensor_tensor(out=s, in0=src, scalar=scale, in1=strip, op0=ALU.mult,
                                                            op1=ALU.add), *marks, *S.free)
            else:
                m = dve.do(lambda e: e.tensor_scalar(s, src, scale, None, ALU.mult), *marks, *S.free)
            bk.give(m)
            if extra is not None:
                m = dve.do(lambda e: e.tensor_tensor(s, s, extra, ALU.add), m)
            nm, l, rl = scol(), scol(), scol()
            m = dve.do(lambda e: e.tensor_reduce(nm, s, AX, ALU.max, negate=True), m)
            if sink is not None:
                m = dve.do(lambda e: e.tensor_scalar(nm, nm, sink[1], None, ALU.min), m)
                es = scol()
                x = act.do(lambda e: e.activation(es, sink[0], ACT.Exp, bias=nm), m)
            m = act.do(lambda e: e.activation(s, s, ACT.Exp, bias=nm, accum_out=l), m)
            if sink is not None:
                m = dve.do(lambda e: e.tensor_tensor(l, l, es, ALU.add), m, x)
            m = dve.do(lambda e: e.reciprocal(rl, l), m)
            return dve.do(lambda e: e.tensor_scalar(s, s, rl, None, ALU.mult), m)

        def attention(W, Qb, Kb, Vb, ms, more, heads, blocks, rate=1):
            yield from need(ms, "q", "k")
            yield
            yield from get(bO)
            work = [(hd, i) for hd in heads for i in range(NT)]
            probs, ptm, sm = {}, {}, {}
            m_last = None
            lag = len(W.S)
            for n in range(len(work) + lag + 1):
                if 0 <= n - lag < len(work):
                    w = n - lag
                    bl = blocks[work[w][1]]
                    S, PT = W.S[w % lag], W.PT[w % 2]
                    yield from get(bT)
                    yield from get(PT)
                    for j in range(len(bl)):
                        m = pe.do(lambda e: e.transpose(bT.ap[:, j * P:(j + 1) * P], S.ap[:, j * P:(j + 1) * P], ident),
                                  probs[w], *bT.free)
                    S.give(m)
                    ptm[w] = act.do(lambda e: e.activation(PT.ap[:, 0:P * len(bl)], bT.ap[:, 0:P * len(bl)], ACT.Copy),
                                    m, *PT.free)
                    bT.give(ptm[w])
                if n < len(work):
                    (rws, _, _, scale, strip, extra, sink), i = work[n]
                    N = P * len(blocks[i])
                    bk, S = (bS0, bS1)[n % 2], W.S[n % lag]
                    yield from get(bk)
                    yield from get(S)
                    k0 = blocks[i][0] * P
                    m = pe.do(lambda e: e.matmul(bk.ap[:, 0:N], Qb.ap[rws, i * P:(i + 1) * P], Kb.ap[rws, k0:k0 + N],
                                                 start=True, stop=True), ms["q"], ms["k"], *more, *bk.free)
                    m_scores = m
                    st = strip(i) if strip else (None, None)
                    ex = extra(i) if extra else (None, None)
                    probs[n] = softmax_rows(W, (bk, S), N, scale, st[0], [m, st[1], ex[1]], ex[0], sink)
                    m_soft = probs[n]
                if n > lag:
                    w = n - lag - 1
                    (_, vcols, orows, _, _, _, _), i = work[w]
                    bl, PT = blocks[i], W.PT[w % 2]
                    if w == 0:
                        yield from need(ms, "v")
                    for j, kb in enumerate(bl):
                        m_last = pe.do(lambda e: e.matmul(
                            bO.ap[orows, i * P:(i + 1) * P], Vb.ap[:, kb * P + vcols.start:kb * P + vcols.stop],
                            PT.ap[:, j * P:(j + 1) * P], start=(j == 0), stop=(j == len(bl) - 1)),
                            ptm[w], ms["v"], *more, *(bO.free if w == 0 else ()))
                    PT.give(m_last)
                if n % rate == rate - 1:
                    yield
            return m_last, m_soft, m_scores

        x1s, mks = io["x1s"], io["mgs"]

        IQ, IK, CKV, CQ, CG, BK, BV, BQ, BG, AQ, AG, MA, MB, MC = 0, 8, 9, 11, 15, 19, 20, 21, 27, 33, 39, 45, 61, 77
        SHARE = (3, 3, 3, 3, 2, 2)
        for h in range(4):
            plan("w_mem", 2 * h, 2)
            plan("w_mem", 2 * (4 + h), 2)
        BEGUN = (40, 32, 48, 56, 41, 33)
        for tile in BEGUN:
            plan("w_in", 2 * tile, 1)
        for h in range(8):
            for j in (5, 4, 6, 7):
                tile = 8 * j + h
                if tile in BEGUN:
                    plan("w_in", 2 * tile + 1, 1)
                else:
                    plan("w_in", 2 * tile, 2)
        for h in range(8):
            for j in range(4 - h // 7):
                plan("w_in", 2 * (8 * j + h), 2)
        plan("w_in", 63, 1)
        plan("w_in", 62, 1)
        for i in (0, 2, 4, 1, 3, 5):
            plan("w_out", i, 1)
        plan("w_out", 6, 24)
        plan("w_out", 31, 1)
        plan("w_out", 30, 1)
        for tile in (IK, *range(IQ, IQ + 8), *(c + h for h in range(4) for c in (CQ, CG)), CKV, CKV + 1, BK, BV):
            plan("w_in2", 2 * tile, 2)

        def plan_mix(MX, name, cols, nb):
            if nb == 0:
                plan("w_in2", 2 * MX, 2)
            if nb < KT - 1:
                plan("w_in2", 2 * (MX + nb + 1), 2)
            plan(name, nb, 1, cols)

        at = 0
        for j in range(6):
            plan("w_in2", 2 * (BQ + j), 2)
            plan("w_in2", 2 * (BG + j), 2)
            for at in range(at, at + SHARE[j]):
                plan_mix(MC, "w_upc", 512, at)
            at += 1
        at = 0
        for j in range(6):
            plan("w_in2", 2 * (AQ + j), 2)
            plan("w_kv", j, 1, 512)
            plan("w_in2", 2 * (AG + j), 2)
            for at in range(at, at + SHARE[j]):
                plan_mix(MB, "w_upb", 768, at)
            at += 1
        for nb in range(KT):
            plan_mix(MA, "w_upa", 768, nb)
        plan("w_o", 0, 32)

        s_mem, s_x = [sem(f"s_mem{i}") for i in range(4)], [sem(f"s_x{i}") for i in range(4)]
        memt = [first[:, (k // 8) * 3072 + k % 8 * 256:(k // 8) * 3072 + k % 8 * 256 + 256] for k in range(KT)]
        for i in range(4):
            at = i // 2 * 3072 + i % 2 * 1024
            sp.dma(first[:, at:at + 1024], io["memT"][:, i * 1024:(i + 1) * 1024], s_mem[i])
        ring.dma(NRAW + 1)
        act.wait(m_cst)
        dve.wait(m_cst)

        def small_sigmoid(x, out, tmp, mark=None):
            m = act.do(lambda e: e.activation(tmp, x, ACT.Abs), mark)
            m = act.do(lambda e: e.activation(tmp, tmp, ACT.Exp, scale=-1.0), m)
            m = act.do(lambda e: e.activation(tmp, tmp, ACT.Ln, bias=1.0), m)
            m = dve.do(lambda e: e.scalar_tensor_tensor(out=out, in0=x, scalar=0.0, in1=tmp, op0=ALU.min,
                                                        op1=ALU.subtract), m)
            return act.do(lambda e: e.activation(out, out, ACT.Exp), m)

        m = small_sigmoid(C("c"), par[:, 64:80], small[:, 0:16])
        m_c = dve.do(lambda e: e.tensor_tensor(par[:, 64:80], par[:, 64:80], C("c"), ALU.mult), m)
        m = dve.do(lambda e: e.tensor_tensor(small[:, 24:32], C("lb", 0, 8), C("lb", 8, 8), ALU.subtract))
        m = small_sigmoid(small[:, 24:32], par[:, 56:64], small[:, 32:40], m)
        m_lb = dve.do(lambda e: e.tensor_scalar(par[:, 48:56], par[:, 56:64], -1.0, 1.0, ALU.mult, ALU.add), m)
        m_ns = dve.do(lambda e: e.tensor_scalar(par[:, 80:92], C("sinks"), -1.0, None, ALU.mult))
        dve.do(lambda e: e.tensor_tensor(par[:, 104:105], C("qc"), C("kc"), ALU.mult))
        m_ng = dve.do(lambda e: e.tensor_scalar(ngb, C("gate_b"), -1.0, None, ALU.mult))

        ada = io["w_ada"].rearrange("(p j) n -> p j n", j=16)

        def ada_sum(cc, acc, slots, rate):
            m = None
            ahead = []
            for j in range(-2, 16):
                if j < 14:
                    s = slots[ada_n[0] % len(slots)]
                    ada_n[0] += 1
                    ahead.append((s, load(sp, s, s.ap, ada[:, j + 2, cc * 1024:(cc + 1) * 1024], *s.free)))
                if j < 0:
                    continue
                s, d = ahead.pop(0)
                cj = par[:, 64 + j:65 + j]
                if j == 0:
                    m = dve.do(lambda e: e.tensor_scalar(acc.ap, s.ap, cj, None, ALU.mult), d, m_c, *acc.free)
                else:
                    m = dve.do(lambda e: e.scalar_tensor_tensor(out=acc.ap, in0=s.ap, scalar=cj, in1=acc.ap,
                                                                op0=ALU.mult, op1=ALU.add), d, m)
                s.free = (m,)
                if j % rate == rate - 1:
                    yield
            acc.made = m

        def ada_post(*chunks):
            halves = [(cc, acc, half) for cc, acc in chunks for half in range(2)]
            sums = []
            for n, (cc, acc, half) in enumerate(halves):
                bk = (bO, bV)[n % 2]
                sums.append((bk, cc, acc, half))
                if n < 2:
                    yield from get(bk)
            r = {}

            def total(n):
                bk, cc, acc, half = sums[n]
                r[n] = pe.do(lambda e: e.matmul(bk.ap, ones, acc.ap[:, half * T:(half + 1) * T], start=True, stop=True),
                             acc.made, m_cst, *bk.free)
            total(0)
            total(1)
            for n, (bk, cc, acc, half) in enumerate(sums):
                a3 = acc.ap[:, half * T:(half + 1) * T].rearrange("p (i t) -> p i t", i=NT)
                m = dve.do(lambda e: e.tensor_tensor(a3, bk.ap.rearrange("p (i t) -> p i t", i=NT),
                                                     ident.unsqueeze(1).to_broadcast([P, NT, P]), ALU.mult), r[n])
                bk.free = (m,)
                if n + 2 < len(sums):
                    total(n + 2)
                c0 = 8 * cc + 4 * half
                m = dve.do(lambda e: e.tensor_reduce(par[:, c0:c0 + 4], a3, AX, ALU.add), m)
                m = dve.do(lambda e: e.tensor_tensor(par[:, c0:c0 + 4], par[:, c0:c0 + 4], C("b_ada", c0, 4), ALU.add), m)
                acc.free = (m,)
                ada_m[cc] = m
            bO.give(*bO.free)
            bV.give(*bV.free)

        ada_m, ada_n = {}, [0]
        a_chans = [chan(f"s_ada{i}") for i in range(4)]
        a_slots = [Buf(TA[:, 4096 + 1024 * i:5120 + 1024 * i], a_chans[i]) for i in range(4)]
        a_acc = [Buf(TA[:, 1024 * i:1024 * i + 1024]) for i in range(4)]

        mem = Acts(H[1][:, 0:4096], H[1][:, 4096:8192], KT, 256)
        sqb = [Buf(first[:, 6144 + i * T:6144 + (i + 1) * T]) for i in range(4)]
        rr = rows[:, 0:256]
        puts = []

        def mem_put():
            k, t, x = puts.pop(0)
            mem.put(k, t, x, on_dve=k % 4 != 0)

        for k in range(KT):
            b, t = sqb[k % 4], memt[k]
            m = act.do(lambda e: e.activation(b.ap[:, 0:256], t, ACT.Square), (s_mem[k // 4], 16), *b.free)
            x = dve.do(lambda e: e.tensor_scalar(t, t, C("mem_g", k, 1), None, ALU.mult), m)
            m = pe.do(lambda e: e.matmul(bST.ap[:, 0:256], ones, b.ap[:, 0:256], start=(k == 0), stop=(k == KT - 1)),
                      m, m_cst)
            b.free = (m,)
            puts.append((k, t, x))
            if k > 1:
                mem_put()
            if k in (8, 10, 12):
                ring.split()
        mem_put()
        mem_put()
        m = act.do(lambda e: e.activation(rr, bST.ap[:, 0:256], ACT.Ln, scale=1.0 / D, bias=eps), m, m_eps)
        bST.give(m)
        mem_by = (rr, act.do(lambda e: e.activation(rr, rr, ACT.Exp, scale=-0.5), m))

        class WM:
            SQ, R = Buf(TA[:, 8448:8704]), Buf(TA[:, 8192:8448])
        WM.SQ.free = WM.R.free = (m_mk,)
        kvb = [Buf(first[:, i // 4 * 3072 + 2048 + i % 4 * 256:i // 4 * 3072 + 2304 + i % 4 * 256]) for i in range(8)]
        m_kv = {}

        def mem_post(h, kind, b, mark):
            m = pool.do(lambda e: e.tensor_tensor(b.ap, b.ap, mem_by[0], ALU.mult), mark, mem_by[1])
            if kind == 0:
                yield from get(WM.SQ)
                m = act.do(lambda e: e.activation(WM.SQ.ap, b.ap, ACT.Square), m, *WM.SQ.free)
                yield
                yield from get(bST)
                m = pe.do(lambda e: e.matmul(bST.ap[:, 0:256], ones, WM.SQ.ap, start=True, stop=True), m, *bST.free)
                WM.SQ.give(m)
                r, ln = rsq(WM, 256, 128, bST.ap[:, 0:256], m)
                bST.give(ln)
                m = pool.do(lambda e: e.tensor_tensor(b.ap, b.ap, WM.R.ap, ALU.mult), r)
                WM.R.give(m)
            else:
                yield
                yield from get(bV)
                for i in range(2):
                    m = pe.do(lambda e, i=i: e.transpose(bV.ap[:, i * P:(i + 1) * P], b.ap[:, i * P:(i + 1) * P], ident),
                              m, *bV.free)
                m = act.do(lambda e: e.activation(b.ap, bV.ap[:, 0:256], ACT.Copy), m)
                bV.give(m)
            m_kv[h, kind] = m
            yield

        def x_norm():
            yield from get(bS0)
            for k in range(KT):
                b = sqb[k % 4]
                a = act.do(lambda e: e.activation(b.ap, Y[:, k * T:(k + 1) * T], ACT.Square), (s_x[k // 4], 16), *b.free)
                yield
                m = pe.do(lambda e: e.matmul(bS0.ap, ones, b.ap, start=(k == 0), stop=(k == KT - 1)), a, *bS0.free)
                b.free = (m,)
            xr = sqb[0].ap
            m = act.do(lambda e: e.activation(xr, bS0.ap, ACT.Ln, scale=1.0 / D, bias=eps), m)
            bS0.give(m)
            m = act.do(lambda e: e.activation(xr, xr, ACT.Exp, scale=-0.5), m)
            for k in range(KT):
                t = Y[:, k * T:(k + 1) * T]
                x_m[k] = (dve if k % 2 else pool).do(lambda e: e.tensor_tensor(t, t, xr, ALU.mult), m)
                if k >= 8 and k % 2:
                    yield

        x_m = {}
        hx = Acts(H[0], H[1], KT, T)

        def h_prep(half):
            yield from need(x_m, *range(8 * half, 8 * half + 8))
            c = slice(16 + 8 * half, 24 + 8 * half)
            m = dve.do(lambda e: e.tensor_scalar(par[:, c], par[:, c], 1.0, None, ALU.add), ada_m[2 + half], ada_m[half])
            m = dve.do(lambda e: e.tensor_tensor(par[:, c], par[:, c], C("norm_g", 8 * half, 8), ALU.mult), m)
            r = {}
            for k in range(8 * half, 8 * half + 8):
                t = Y[:, k * T:(k + 1) * T]
                r[k] = dve.do(lambda e: e.tensor_scalar(t, t, par[:, 16 + k:17 + k], par[:, k:k + 1], ALU.mult, ALU.add),
                              m, x_m[k])
                if half == 1:
                    hx.put(k, t, r[k], on_dve=k % 2 == 1)
            while not mem_done:
                yield
            hx.used = tuple(mem_done)
            if half == 0:
                for k in range(8):
                    hx.put(k, Y[:, k * T:(k + 1) * T], r[k])

        def conditioning():
            yield from ada_sum(2, a_acc[0], a_slots, 2)
            yield from ada_sum(0, a_acc[1], a_slots, 2)
            third = ada_sum(3, a_acc[2], a_slots, 1)
            for _ in range(6):
                next(third)
                yield
            yield from ada_post((2, a_acc[0]), (0, a_acc[1]))
            behind.append(h_prep(0))
            yield from third
            yield from ada_sum(1, a_acc[3], a_slots, 1)
            ring.early = False
            yield from ada_post((3, a_acc[2]), (1, a_acc[3]))
            yield from h_prep(1)
            while None in hx.ready:
                yield
            for b in (*g_slots, g_acc):
                b.free = tuple(hx.ready)
            for b in W1.all() + [W1.t1, W1.t2]:
                b.free = (*a_acc[0].free, *a_acc[1].free, *a_acc[2].free, *a_acc[3].free, *WM.SQ.free, *WM.R.free)
                b.busy = False
            for cc in (4, 5):
                yield from ada_sum(cc, g_acc, g_slots, 1)
                for _ in range(6):
                    yield
                yield from ada_post((cc, g_acc))

        g_slots = [Buf(Y[:, 1024 * i:1024 * i + 1024], a_chans[i]) for i in range(3)]
        g_acc = Buf(Y[:, 3072:4096])
        mem_done = []
        for b in W1.all() + [W1.t1, W1.t2]:
            b.busy = True
        for i in range(4):
            sp.dma(Y[:, i * 2048:(i + 1) * 2048], io["xT"][:, i * 2048:(i + 1) * 2048], s_x[i])
        behind.append(x_norm())
        slow.append(conditioning())
        for h in range(4):
            for kind in range(2):
                bk, m = full(mem, "w_mem", h + 4 * kind)
                b = kvb[2 * h + kind]
                r = evac(bk, m, b, w=256)
                urgent.append(mem_post(h, kind, b, r))
        mem_done.append(m)

        yb = [Buf(Y[:, k * T:(k + 1) * T]) for k in range(KT)]
        y_m = [None] * KT
        causal1 = [list(range(i + 1)) for i in range(NT)]
        all_rows = slice(0, 128)

        def head_post(W, kind, b, mark, ms, name, gain=None, over=None, n=128):
            mm = [mark]
            if kind == "norm":
                yield from norm(W, [b.ap], mm, over or ones, n, [gain])
            elif kind == "turn":
                yield from turned(W, b, mark, mm)
            else:
                yield from silu(W, b.ap, mark, mm)
            ms[name] = mm[0]

        def take_head(W, wname, x, nb, b, kind, ms, name, by=None, **kw):
            bk, m = full(x, wname, nb)
            r = evac(bk, m, take(b), by=by)
            urgent.append(head_post(W, kind, b, r, ms, name, **kw))

        AD, OF1, OF2 = TA[:, 4096:4608], TA[:, 4608:4864], TA[:, 4864:5376]
        TOT = TA[:, 5376:5888]

        def hg_decay(h, b, mark, ms, F):
            def pos(s, m):
                ms["f"] = dve.do(lambda e: e.tensor_scalar(F.ap, s, par[:, 48 + h:49 + h], par[:, 56 + h:57 + h],
                                                           ALU.mult, ALU.add), m, m_lb, *F.free)
                return ms["f"]

            def neg(s, m):
                ms["k"] = dve.do(lambda e: e.tensor_scalar(b.ap, s, par[:, 48 + h:49 + h], None, ALU.mult), m)
                return ms["k"]
            yield from sigma(W1, b.ap, mark, [(1, pos), (-1, neg)])

        def hg_head(h, Qb, Kb, Vb, Zb, Fb, ms):
            W = W1
            yield from need(ms, "q", "k", "f")
            yield
            yield
            for b in (*W.S, *W.PT):
                yield from get(b)
            free = [x for b in (*W.S, *W.PT) for x in b.free]
            q, k = Qb.ap, Kb.ap
            up = [ms["q"], ms["k"], ms["f"]]
            if h == 0:
                free = [dve.do(lambda e: e.memset(AD, 0.0), *free)]
            tot, tot_m, done = Fb.ap, None, None
            for step, m in enumerate([0, 1, 2, 4, 8, 16, 32, 64]):
                bk = (bS0, bS1)[step % 2]
                yield from get(bk)
                for i in range(NT):
                    r = pe.do(lambda e: e.matmul(bk.ap[:, i * P:(i + 1) * P], k[:, i * P:(i + 1) * P],
                                                 q[:, i * P:(i + 1) * P], start=True, stop=True), *up, *bk.free)
                if m == 0:
                    up = [dve.do(lambda e: e.tensor_tensor(q, q, Fb.ap, ALU.mult), r)]
                else:
                    nb = T // (2 * m)
                    qv = q.rearrange("p (b two m) -> p b two m", two=2, m=m)
                    kv = k.rearrange("p (b two m) -> p b two m", two=2, m=m)
                    tv = tot.rearrange("p (b two) -> p b two", two=2)
                    tl = tv[:, :, 0:1].to_broadcast([P, nb, m])
                    tr = tv[:, :, 1:2].to_broadcast([P, nb, m])
                    u1 = dve.do(lambda e: e.tensor_tensor(qv[:, :, 1, :], qv[:, :, 1, :], tl, ALU.mult), r, tot_m)
                    u2 = dve.do(lambda e: e.tensor_tensor(kv[:, :, 0, :], kv[:, :, 0, :], tr, ALU.mult), r, tot_m)
                    new = TOT[:, T - 2 * nb:T - nb]
                    tot_m = dve.do(lambda e: e.tensor_tensor(new, tv[:, :, 0], tv[:, :, 1], ALU.mult), tot_m, *free)
                    tot = new
                    up = [u1, u2]
                msk = mk[:, step * P:(step + 1) * P].unsqueeze(1).to_broadcast([P, NT, P])
                done = dve.do(lambda e: e.copy_predicated(AD.rearrange("p (i t) -> p i t", i=NT), msk,
                                                          bk.ap.rearrange("p (i t) -> p i t", i=NT)), r, m_mk, done, *free)
                bk.give(done)
                yield
            yield from get(bS0)
            for i in range(2):
                r = pe.do(lambda e: e.matmul(bS0.ap[:, i * P:(i + 1) * P], k[:, 2 * i * P:(2 * i + 1) * P],
                                             q[:, (2 * i + 1) * P:(2 * i + 2) * P], start=True, stop=True), *up, *bS0.free)
            qv = q.rearrange("p (b two m) -> p b two m", two=2, m=P)
            kv = k.rearrange("p (b two m) -> p b two m", two=2, m=P)
            tv = tot.rearrange("p (b two) -> p b two", two=2)
            u1 = dve.do(lambda e: e.tensor_tensor(qv[:, :, 1, :], qv[:, :, 1, :], tv[:, :, 0:1].to_broadcast([P, 2, P]),
                                                  ALU.mult), r, tot_m)
            u2 = dve.do(lambda e: e.tensor_tensor(kv[:, :, 0, :], kv[:, :, 0, :], tv[:, :, 1:2].to_broadcast([P, 2, P]),
                                                  ALU.mult), r, tot_m)
            c1 = act.do(lambda e: e.activation(OF1, bS0.ap[:, 0:256], ACT.Copy), r, *free)
            bS0.give(c1)
            Fb.give(u2)
            yield
            yield from get(bS1)
            for i in range(2):
                r = pe.do(lambda e: e.matmul(bS1.ap[:, i * 256:(i + 1) * 256], k[:, i * P:(i + 1) * P], q[:, 256:512],
                                             start=True, stop=True), u1, u2, *bS1.free)
            c2 = act.do(lambda e: e.activation(OF2, bS1.ap, ACT.Copy), r, *free)
            bS1.give(c2)
            Qb.give(r)
            Kb.give(r)
            yield from need(ms, "v")
            yield
            yield from get(bO)
            pairs = [[(0, AD[:, 0:128])],
                     [(1, AD[:, 128:256]), (0, OF1[:, 0:128])],
                     [(2, AD[:, 256:384]), (0, OF2[:, 0:128]), (1, OF2[:, 256:384])],
                     [(3, AD[:, 384:512]), (2, OF1[:, 128:256]), (0, OF2[:, 128:256]), (1, OF2[:, 384:512])]]
            for i, ps in enumerate(pairs):
                for j, (kb, a) in enumerate(ps):
                    r = pe.do(lambda e: e.matmul(bO.ap[:, i * P:(i + 1) * P], Vb.ap[:, kb * P:(kb + 1) * P], a,
                                                 start=(j == 0), stop=(j == len(ps) - 1)), done, c1, c2, ms["v"], *bO.free)
            for b in (*W.S, *W.PT):
                b.give(r, tot_m)
            Vb.give(r)
            yield from get(W.SQ)
            m = act.do(lambda e: e.activation(W.SQ.ap, bO.ap, ACT.Square), r, *W.SQ.free)
            yield
            yield from get(bST)
            m = pe.do(lambda e: e.matmul(bST.ap, ones, W.SQ.ap, start=True, stop=True), m, *bST.free)
            W.SQ.give(m)
            yield from get(W.R)
            r, ln = rsq(W, T, 128, bST.ap, m)
            bST.give(ln)
            y = yb[8 + h].ap
            m = dve.do(lambda e: e.scalar_tensor_tensor(out=y, in0=bO.ap, scalar=C("hg_g"), in1=W.R.ap, op0=ALU.mult,
                                                        op1=ALU.mult), r, *hx.ready)
            bO.give(m)
            W.R.give(m)
            yield from need(ms, "z")
            y_m[8 + h] = dve.do(lambda e: e.tensor_tensor(y, y, Zb.ap, ALU.mult), m, ms["z"])
            Zb.give(y_m[8 + h])

        begun = {}
        for tile, bank_of in zip(BEGUN, (None, None, bS0, bS1, bT, bST)):
            bk = take(bank_of) if bank_of else open_bank()
            piece = ring.take(("w_in", 2 * tile))
            m = part(bk, hx, piece, range(8), first=True)
            ring.give(piece[3], m)
            begun[tile] = bk

        def in_tile(nb):
            if nb not in begun:
                return full(hx, "w_in", nb)
            bk = begun[nb]
            piece = ring.take(("w_in", 2 * nb + 1))
            m = part(bk, hx, piece, range(8, 16), last=True)
            ring.give(piece[3], m)
            return bk, m

        for h in range(8):
            W, ms = W1, {}
            bufs = W.Q[h % 2], W.K[h % 2], W.V[h % 2], W.Z[h % 2], W.ST[h % 2]
            bk, m = in_tile(40 + h)
            take(bufs[4])
            r = evac(bk, m, take(bufs[1]))
            urgent.append(hg_decay(h, bufs[1], r, ms, bufs[4]))
            bk, m = in_tile(32 + h)
            r = evac(bk, m, take(bufs[0]))
            urgent.append(head_post(W, "silu", bufs[0], r, ms, "q"))
            behind.append(hg_head(h, *bufs, ms))
            for tile, buf, kind, name in ((48 + h, bufs[2], "turn", "v"), (56 + h, bufs[3], "silu", "z")):
                bk, m = in_tile(tile)
                r = evac(bk, m, take(buf))
                urgent.append(head_post(W, kind, buf, r, ms, name))

        def att_head(h, Qb, Kb, Vb, Zb, ms):
            W = W1
            yield from get(W.ST[h % 2])
            sbuf = W.ST[h % 2]
            d = load(sp, sbuf, sbuf.ap, io["strip1"][h], *sbuf.free)
            m, soft, scores = yield from attention(
                W, Qb, Kb, Vb, ms, (), [(all_rows, slice(0, 128), all_rows, SC128,
                                         lambda i: (sbuf.ap[:, 384 - 128 * i:512], d), None, None)], causal1)
            Qb.give(scores)
            Kb.give(scores)
            sbuf.give(soft)
            Vb.give(m)
            yield from need(ms, "z")
            y_m[h] = dve.do(lambda e: e.tensor_tensor(yb[h].ap, bO.ap, Zb.ap, ALU.mult), m, ms["z"], ada_m[4], ada_m[5])
            bO.give(y_m[h])
            Zb.give(y_m[h])

        yx = Acts(H[0], H[1], KT, T)
        YO = [*range(8, 16), *range(8)]

        def y_early(m):
            yx.used = (m,)
            for n, k in enumerate(YO[:8]):
                yx.put(k, yb[k].ap, y_m[k], on_dve=n % 3 == 1)

        for h in range(8):
            W, ms = W1, {}
            bufs = W.Q[h % 2], W.K[h % 2], W.V[h % 2], W.Z[h % 2]
            take_head(W, "w_in", hx, h, bufs[0], "norm", ms, "q", gain=C("q_g"))
            take_head(W, "w_in", hx, 8 + h, bufs[1], "norm", ms, "k", gain=C("k_g"))
            behind.append(att_head(h, *bufs, ms))
            take_head(W, "w_in", hx, 16 + h, bufs[2], "turn", ms, "v")
            if h < 7:
                bk, m = full(hx, "w_in", 24 + h)
            else:
                bk, m = full(hx, "w_in", 24 + h, (1, 0), y_early)
            r = evac(bk, m, take(bufs[3]))
            urgent.append(head_post(W, "silu", bufs[3], r, ms, "z"))
        last_in = m

        def y_prep():
            for n, k in enumerate(YO[8:]):
                while y_m[k] is None:
                    yield
                yx.used = (last_in,)
                yx.put(k, yb[k].ap, y_m[k], on_dve=n % 3 == 1)

        slow.append(y_prep())
        R2 = rows
        s_x1 = sem("s_x1st")
        x1_m = [None] * KT
        hb = [Buf(TA[:, i * T:(i + 1) * T]) for i in range(4)]
        sqt, sqa = Buf(TA[:, 4 * T:5 * T]), Buf(TA[:, 7 * T:8 * T])
        m_st = None

        x_d = {}

        def x_load(nb):
            b = xw[nb % 2]
            x_d[nb] = load(sp, b, b.ap, io["xT"][:, nb * T:(nb + 1) * T], *b.free)

        def x1_block(nb, bk, m):
            nonlocal m_st
            b = xw[nb % 2]
            d = x_d[nb]
            t = yb[nb].ap
            r = dve.do(lambda e: e.scalar_tensor_tensor(out=t, in0=bk.ap, scalar=par[:, 32 + nb:33 + nb], in1=b.ap,
                                                        op0=ALU.mult, op1=ALU.add), m, d, *yx.ready)
            bk.give(r)
            b.free = (r,)
            x1_m[nb] = r
            sp.wait(r)
            sp.dma(x1s[nb], t, s_x1)
            if nb == 0:
                m_st = act.do(lambda e: e.activation(sqa.ap, t, ACT.Square), r, *sqa.free)
            else:
                r = act.do(lambda e: e.activation(sqt.ap, t, ACT.Square), r, *sqt.free)
                m_st = dve.do(lambda e: e.tensor_tensor(sqa.ap, sqa.ap, sqt.ap, ALU.add), r, m_st)
                sqt.free = (m_st,)

        held = []
        for nb in range(3):
            bk = take(bV) if nb == 2 else open_bank()
            p0 = ring.take(("w_out", 2 * nb))
            m = part(bk, yx, p0, YO[0:8], first=True)
            ring.give(p0[3], m)
            held.append(bk)
        for nb in range(3):
            p1 = ring.take(("w_out", 2 * nb + 1))
            part(held[nb], yx, p1, YO[8:15])
            held[nb] = held[nb], p1
        until(lambda: yx.ready[7] is not None)
        drain()
        w_free = tuple(x for b in W1.all() for x in b.free)
        xw = [Buf(TA[:, (5 + i) * T:(6 + i) * T], w_chans[8 + i]) for i in range(2)]
        for b in (*xw, *hb, sqt, sqa):
            b.free = w_free
        x_load(0)
        x_load(1)
        for nb, (bk, p1) in enumerate(held):
            m = part(bk, yx, p1, YO[15:16], off=7 * P, last=True)
            ring.give(p1[3], m)
            ring.ahead()
            if nb > 1:
                x_load(nb)
            x1_block(nb, bk, m)
        h2 = Acts(H[0], H[1], KT, T)

        def h2_put(k):
            b = hb[k % 4]
            x = dve.do(lambda e: e.tensor_scalar(b.ap, yb[k].ap, C("norm_g2", k, 1), None, ALU.mult), x1_m[k], *b.free)
            b.free = (h2.put(k, b.ap, x, on_dve=k % 2 == 1),)
            return x

        def h2_early(m):
            h2.used = (m,)
            for k in range(8):
                h2_put(k)

        for nb in range(3, KT):
            x_load(nb)
            bk, m = full(yx, "w_out", nb, *(((1, 0), h2_early) if nb == KT - 1 else ()), ks=YO)
            ring.ahead()
            x1_block(nb, bk, m)
        h2.used = (m,)
        for k in range(8, KT):
            x = h2_put(k)

        def stats():
            m = pe.do(lambda e: e.matmul(bST.ap, ones, sqa.ap, start=True, stop=True), m_st, *bST.free)
            sqa.free = (m,)
            m = act.do(lambda e: e.activation(R2, bST.ap, ACT.Ln, scale=1.0 / D, bias=eps), m)
            bST.give(m)
            return act.do(lambda e: e.activation(R2, R2, ACT.Exp, scale=-0.5), m)
        m_x1s = (s_x1, 16 * KT)

        W = W2
        for b in W2.all():
            b.free = (x, m_x1s)
        W2.t1.free = W2.t2.free = (*W1.t1.free, *W1.t2.free)
        ost = [Buf(TA[:, i * T:(i + 1) * T]) for i in range(6)]
        sc = TA[:, 3072:4224]
        gx = [Buf(TA[:, 4224 + i * T:4224 + (i + 1) * T]) for i in range(2)]
        ub = [Buf(TA[:, 5248 + i * T:5248 + (i + 1) * T], chan(f"s_u{i}")) for i in range(2)]
        lb_ = [Buf(TA[:, 6272 + i * T:6272 + (i + 1) * T], chan(f"s_l{i}")) for i in range(2)]
        rt = [W2.S[2], Buf(TA[:, 7808:8192])]
        bk, m_ik = full(h2, "w_in2", IK)
        by = (R2, stats())
        ta_free = (*h2.ready, *xw[0].free, *xw[1].free, *sqt.free, *sqa.free, *w_free)
        for b in (*ost, *gx, *ub, *lb_, *rt):
            b.free = ta_free
        OFF = {1: 0, 2: 256, 3: 640}

        ik = W.K[0]
        r_ik = evac(bk, m_ik, take(ik), by=by)
        im = {}

        def ik_post():
            lo = slice(0, 64)
            yield from get(bV)
            for i in range(NT):
                m = pe.do(lambda e: e.transpose(bV.ap[:, 16 * i:16 * i + 16], ik.ap[64:80, i * P:(i + 1) * P],
                                                ident[64:80, 64:80]), r_ik, *bV.free)
            m = dve.do(lambda e: e.tensor_scalar(iwt, bV.ap[:, 0:64], 1.0 / 32, None, ALU.mult), m)
            bV.give(m)
            im["w"] = m
            yield from get(bST)
            m = pe.do(lambda e: e.matmul(bST.ap[lo, :], ones64[lo, lo], ik.ap[lo, :], start=True, stop=True),
                      r_ik, *bST.free)
            m = dve.do(lambda e: e.scalar_tensor_tensor(out=ik.ap[lo, :], in0=bST.ap[lo, :], scalar=-1.0 / 64,
                                                        in1=ik.ap[lo, :], op0=ALU.mult, op1=ALU.add), m)
            bST.give(m)
            yield
            yield from get(bST)
            yield from get(W.SQ)
            m = act.do(lambda e: e.activation(W.SQ.ap[lo, :], ik.ap[lo, :], ACT.Square), m, *W.SQ.free)
            m = pe.do(lambda e: e.matmul(bST.ap[lo, :], ones64[lo, lo], W.SQ.ap[lo, :], start=True, stop=True), m)
            W.SQ.give(m)
            yield from get(W.R)
            R = W.R.ap[lo, :]
            m = act.do(lambda e: e.activation(R, bST.ap[lo, :], ACT.Ln, scale=1.0 / 64, bias=eps[lo, :]), m, *W.R.free)
            bST.give(m)
            m = act.do(lambda e: e.activation(R, R, ACT.Exp, scale=-0.5), m)
            m = dve.do(lambda e: e.scalar_tensor_tensor(out=ik.ap[lo, :], in0=ik.ap[lo, :], scalar=C("ik_g")[lo, :],
                                                        in1=R, op0=ALU.mult, op1=ALU.mult), m)
            W.R.give(m)
            m = dve.do(lambda e: e.tensor_scalar(ik.ap[lo, :], ik.ap[lo, :], C("ik_b")[lo, :], None, ALU.add), m)
            im["k"] = dve.do(lambda e: e.tensor_copy(ik.ap[64:128, :], ik.ap[lo, :]), m, im["w"])

        urgent.append(ik_post())
        sc_m = {1: ta_free, 2: ta_free, 3: ta_free}

        def idx_head(j, Qb, ms):
            yield from need(im, "k", "w")
            yield
            n_rt = 0
            for hh in range(2):
                head = 2 * j + hh
                rws = slice(64 * hh, 64 * hh + 64)
                for i in (3, 2, 1):
                    n = P * (i + 1)
                    bk = (bS0, bS1)[i % 2]
                    yield from get(bk)
                    m = pe.do(lambda e: e.matmul(bk.ap[:, 0:n], Qb.ap[rws, i * P:(i + 1) * P], ik.ap[rws, 0:n],
                                                 start=True, stop=True), *ms, im["k"], *bk.free)
                    t = rt[0] if i != 2 else rt[1]
                    yield from get(t)
                    a = act.do(lambda e: e.activation(t.ap[:, 0:n], bk.ap[:, 0:n], ACT.Relu), m, *t.free)
                    bk.give(a)
                    s = sc[:, OFF[i]:OFF[i] + n]
                    wcol = iwt[:, 16 * i + head:16 * i + head + 1]
                    if head == 0:
                        m = dve.do(lambda e: e.tensor_scalar(s, t.ap[:, 0:n], wcol, None, ALU.mult), a, im["w"], *sc_m[i])
                    else:
                        m = dve.do(lambda e: e.scalar_tensor_tensor(out=s, in0=t.ap[:, 0:n], scalar=wcol, in1=s,
                                                                    op0=ALU.mult, op1=ALU.add), a, *sc_m[i])
                    t.give(m)
                    sc_m[i] = (m,)
                    if i == 2:
                        yield
                yield
            last = [x[0] for x in sc_m.values()]
            Qb.give(*last)
            if j == 7:
                ik.give(*last)
                im["done"] = None

        for j in range(8):
            Qb = W.Q[j % 2]
            bk, m = full(h2, "w_in2", IQ + j)
            r = evac(bk, m, take(Qb), by=by)
            behind.append(idx_head(j, Qb, [r]))

        tkm = par[:, 96:104]

        def topk():
            yield from need(im, "done")
            for i in (1, 2, 3):
                n = P * (i + 1)
                s = sc[:, OFF[i]:OFF[i] + n]
                d = sc[:, OFF[i] + n - P:OFF[i] + n]
                m = dve.do(lambda e: e.tensor_tensor(d, d, C("causal"), ALU.add), *sc_m[i])
                for r in range(TOPK // 8):
                    m = dve.do(lambda e: e.max(tkm, s), m)
                    m = dve.do(lambda e: e.match_replace(s, tkm, s, -3e38), m)
                    yield
                sc_m[i] = (dve.do(lambda e: e.tensor_scalar(s, s, -2e38, NEG, ALU.is_gt, ALU.mult), m),)

        slow.append(topk())

        o_m = {}

        def staged(h, Zb, ms, m, *gives):
            for b, mark in gives:
                b.give(mark)
            yield from need(ms, "z")
            r = dve.do(lambda e: e.tensor_tensor(ost[h].ap, bO.ap, Zb.ap, ALU.mult), m, ms["z"], *ost[h].free)
            bO.give(r)
            Zb.give(r)
            o_m[h] = r

        def c_head(h, Qb, Kb, Vb, Zb, ms):
            ms["k"], ms["v"] = m_kv[h, 0], m_kv[h, 1]
            yield from get(ost[h])
            m, soft, scores = yield from attention(
                W, Qb, Kb, Vb, ms, (), [(all_rows, slice(0, 128), all_rows, SC128, None, None, None)], [[0, 1]] * NT)
            yield from staged(h, Zb, ms, m, (Qb, scores))

        for h in range(4):
            ms = {}
            bufs = W.Q[h % 2], kvb[2 * h], kvb[2 * h + 1], W.Z[h % 2]
            take_head(W, "w_in2", h2, CQ + h, bufs[0], "norm", ms, "q", by=by, gain=par[:, 104:105])
            behind.append(c_head(h, *bufs, ms))
            take_head(W, "w_in2", h2, CG + h, bufs[3], "silu", ms, "z", by=by)

        cx = Acts(CK[0], CK[1], 2, T)
        bufs = [take(W.K[0]), take(W.V[0])]
        cm = []
        for i in range(2):
            bk, m = full(h2, "w_in2", CKV + i)
            cm.append(evac(bk, m, bufs[i], by=by))

        def ck_post(bufs):
            yield from norm(W, [b.ap for b in bufs], cm, ones, 256, [C("kv_g", 0, 1), C("kv_g", 1, 1)])
            for i in range(2):
                bufs[i].give(cx.put(i, bufs[i].ap, cm[i]))

        urgent.append(ck_post(bufs))

        bK, bVv = W.K[1], W.V[1]
        kvm = {}
        take_head(W, "w_in2", h2, BK, bK, "norm", kvm, "k", by=by, gain=C("kb"), over=ones64, n=64)
        take_head(W, "w_in2", h2, BV, bVv, "turn", kvm, "v", by=by)
        until(lambda: len(o_m) == 4)
        oc = Acts(O2[0], O2[1], 6, T)
        for k in range(4):
            ost[k].give(oc.put(k, ost[k].ap, o_m[k], on_dve=k % 2 == 1))
        o_m.clear()
        window = [[0], [0, 1], [1, 2], [2, 3]]

        def b_pair(j, Qb, Zb, ms):
            yield from get(ost[j])
            heads = []
            for half, head in enumerate((j, j + 6)):
                yield from get(W.ST[half])
                rws = slice(64 * half, 64 * half + 64)
                sbuf = W.ST[half]
                d = load(sp, sbuf, sbuf.ap[:, 0:256], io["strip_b"][head], *sbuf.free)
                strip = lambda i, s=sbuf, d=d: (s.ap[:, 128:256] if i == 0 else s.ap[:, 0:256], d)
                heads.append((rws, rws, rws, SC64, strip, None,
                              (C("sinks", head, 1), par[:, 80 + head:81 + head])))
            yield from need(kvm, "k", "v")
            ms["k"], ms["v"] = kvm["k"], kvm["v"]
            m, soft, scores = yield from attention(W, Qb, bK, bVv, ms, (m_ns,), heads, window)
            gives = [(Qb, scores), (W.ST[0], soft), (W.ST[1], soft)]
            if j == 5:
                gives += [(bK, scores), (bVv, m)]
            yield from staged(j, Zb, ms, m, *gives)

        st_m = [None] * KT
        mg_m = [None] * KT
        mixed = [None]

        def mix_gate(b, mark, nb, gcol, out):
            def use(s, m):
                out.append(pool.do(lambda e: e.tensor_copy(b.ap, s), m))
                return out[0]
            yield from sigma(W2, b.ap, mark, [(1, use)],
                             bias=(C("gate_b", gcol + nb, 1), ngb[:, gcol + nb:gcol + nb + 1]))

        def mix(branch, MX, name, o, nk, gcol, y_free=()):
            outs = {}

            def gate(nb):
                g = take(gx[nb % 2])
                last = branch == 2 and nb == KT - 1
                bk, m = full(h2, "w_in2", MX + nb, between=mx_early if last else None)
                if last:
                    mx.used = (m,)
                r = evac(bk, m, g, by=by)
                outs[nb] = []
                urgent.append(mix_gate(g, r, nb, gcol, outs[nb]))

            for nb in range(KT):
                if nb == 0:
                    gate(0)
                if nb < KT - 1:
                    gate(nb + 1)
                g, out = gx[nb % 2], outs[nb]
                lb, u = lb_[nb % 2], ub[nb % 2]
                if branch > 0:
                    d = load(sp, lb, lb.ap, mks[nb], st_m[nb], *lb.free)
                bk, m = thin(o, name, nb, nk)
                until(lambda: out)
                r = dve.do(lambda e: e.tensor_tensor(u.ap, bk.ap, g.ap, ALU.mult), m, out[0], *u.free)
                bk.give(r)
                g.give(r)
                if branch == 2:
                    r = dve.do(lambda e: e.tensor_tensor(yb[nb].ap, u.ap, lb.ap, ALU.add), r, d, *y_free)
                    lb.free = u.free = (r,)
                    mg_m[nb] = r
                else:
                    if branch == 1:
                        r = pool.do(lambda e: e.tensor_tensor(u.ap, u.ap, lb.ap, ALU.add), r, d)
                        lb.free = (r,)
                    st_m[nb] = load(sp, u, mks[nb], u.ap, r)
                    u.free = (st_m[nb],)
                mixed[0] = m
                yield

        mx = Acts(H[0], H[1], KT, T)

        def mx_early(m):
            mx.used = (m,)
            for k in range(8):
                mx.put(k, yb[k].ap, mg_m[k], on_dve=k % 3 == 1)

        mix_c = mix(0, MC, "w_upc", oc, 4, 32)
        for j in range(6):
            ms = {}
            Qb, Zb = W.Q[j % 2], W.Z[j % 2]
            take_head(W, "w_in2", h2, BQ + j, Qb, "norm", ms, "q", by=by, gain=C("qb"), over=ones64, n=64)
            behind.append(b_pair(j, Qb, Zb, ms))
            take_head(W, "w_in2", h2, BG + j, Zb, "silu", ms, "z", by=by)
            for _ in range(SHARE[j]):
                next(mix_c)
        until(lambda: len(o_m) == 6)
        ob = Acts(O2[0], O2[1], 6, T)
        ob.used = (mixed[0],)
        for k in range(6):
            ost[k].give(ob.put(k, ost[k].ap, o_m[k], on_dve=k % 2 == 1))
        o_m.clear()
        until(lambda: not slow)

        def a_head(h, Qb, Kb, Vb, Zb, ms):
            yield from get(ost[h])
            yield from get(W.ST[h % 2])
            sbuf = W.ST[h % 2]
            d = load(sp, sbuf, sbuf.ap, io["strip_a"][h], *sbuf.free)
            m, soft, scores = yield from attention(W, Qb, Kb, Vb, ms, (), [(
                all_rows, slice(0, 128), all_rows, SC128, lambda i: (sbuf.ap[:, 384 - 128 * i:512], d),
                lambda i: (sc[:, OFF[i]:OFF[i] + P * (i + 1)], sc_m[i][0]) if i else (None, None), None)], causal1)
            yield from staged(h, Zb, ms, m, (Qb, scores), (Kb, scores), (Vb, m), (sbuf, soft))

        mix_b = mix(1, MB, "w_upb", ob, 6, 16)
        for h in range(6):
            ms = {}
            bufs = W.Q[h % 2], W.K[h % 2], W.V[h % 2], W.Z[h % 2]
            take_head(W, "w_in2", h2, AQ + h, bufs[0], "norm", ms, "q", by=by, gain=C("qa"))
            piece = ring.take(("w_kv", h))
            for kind in range(2):
                bk = open_bank()
                m = part(bk, cx, piece, range(2), off=256 * kind, first=True, last=True)
                r = evac(bk, m, take(bufs[1 + kind]))
                urgent.append(head_post(W, ("norm", "turn")[kind], bufs[1 + kind], r, ms, "kv"[kind], gain=C("ka")))
            ring.give(piece[3], m)
            behind.append(a_head(h, *bufs, ms))
            take_head(W, "w_in2", h2, AG + h, bufs[3], "silu", ms, "z", by=by)
            for _ in range(SHARE[h]):
                next(mix_b)
        until(lambda: len(o_m) == 6)
        drain()
        oa = Acts(O2[0], O2[1], 6, T)
        oa.used = (mixed[0],)
        for k in range(6):
            ost[k].give(oa.put(k, ost[k].ap, o_m[k], on_dve=k % 2 == 1))
        y_free = tuple(x for b in W2.all() for x in b.free)
        for _ in mix(2, MA, "w_upa", oa, 6, 0, y_free):
            pass
        for k in range(8, KT):
            mx.put(k, yb[k].ap, mg_m[k], on_dve=k % 3 == 1)
        out_m = []
        for nb in range(KT):
            lb, u = lb_[nb % 2], ub[nb % 2]
            d = load(sp, lb, lb.ap, x1s[nb], m_x1s, *lb.free)
            bk, m = full(mx, "w_o", nb)
            r = dve.do(lambda e, bk=bk, u=u, lb=lb: e.tensor_tensor(u.ap, bk.ap, lb.ap, ALU.add), m, d, *u.free)
            bk.give(r)
            lb.free = (r,)
            s = load(sp, u, io["out"][nb], u.ap, r)
            u.free = (s,)
            out_m.append(s)
        sp.wait(*out_m, *st_m, m_x1s)
        assert ring.i == len(items)


def buckets():
    n = np.arange(512)
    nf = np.maximum(n, 1).astype(np.float32)
    large = 16 + (np.log(nf / np.float32(16)) / np.float32(np.log(8.0)) * np.float32(16)).astype(np.int32)
    return np.where(n < 16, n, np.minimum(large, 31))


def tiles(w, kt=8):
    K, N = w.shape
    return np.ascontiguousarray(
        w.reshape(K // (128 * kt), kt, 128, N // 128, 128).transpose(3, 0, 2, 1, 4).reshape(-1, 128, kt * 128))


def kernel(**inputs):
    import concourse.bacc as _bacc
    from concourse.bass_utils import run_bass_kernel_spmd as _run

    I = {k: np.asarray(v) for k, v in inputs.items()}
    f32 = np.float32

    def feat(a, n):
        return a.reshape(n, 128).T

    ar = np.arange(128)
    p, u = ar[:, None], np.arange(512)[None, :]
    cols = {
        "ident": np.eye(128, dtype=f32), "ones": np.ones((128, 128), f32),
        "ones64": np.kron(np.eye(2), np.ones((64, 64))).astype(f32),
        "causal": np.where(p >= ar[None, :], 0, NEG).astype(f32),
        "norm_g": feat(I["norm_g"], 16), "b_ada": feat(I["b_ada"], 48),
        "q_g": I["q_norm_g"].T, "k_g": I["k_norm_g"].T, "hg_g": I["hg_norm_g"].T,
        "lb": np.concatenate([feat(I["lower_bounds"][i], 8) for i in range(2)], 1),
        "norm_g2": feat(I["norm_g_2"], 16), "kv_g": feat(I["kv_norm_g_2"], 2),
        "ik_g": np.concatenate([I["idx_k_ln_g_2"].T] * 2), "ik_b": np.concatenate([I["idx_k_ln_b_2"].T] * 2),
        "qa": I["q_norm_a_2"].T, "ka": I["k_norm_a_2"].T,
        "qb": np.concatenate([I["q_norm_b_2"].T] * 2), "kb": np.concatenate([I["k_norm_b_2"].T] * 2),
        "qc": I["q_norm_c_2"].T, "kc": I["k_norm_c_2"].T, "mem_g": feat(I["mem_norm_g_2"], 16),
        "gate_b": feat(I["gate_bias_2"], 48), "sinks": np.broadcast_to(I["sinks_b_2"], (128, 12)),
        "c": I["c"].reshape(128, 16),
    }
    cst = np.zeros((128, NCST), f32)
    for name, (at, n) in CST.items():
        cst[:, at:at + n] = cols[name]
    s, t = ar[:, None], ar[None, :]
    masks = [s == t] + [(s // (2 * m) == t // (2 * m)) & (s // m % 2 == 0) & (t // m % 2 == 1)
                        for m in (1, 2, 4, 8, 16, 32, 64)]
    masks = np.concatenate(masks, 1).astype(np.int32)

    neg = f32(NEG)
    d = p - (u - 384)
    strip1 = I["rel_bias"][0][:, np.clip(d, -128, 128) + 128]
    strip1 = np.where((p < 64) & (u >= 448), neg, strip1)
    bk = buckets()
    ra, rb = I["rel_bias_2"][:, :6].T, I["rel_bias_2"][:, 6:].T
    strip_a = np.where(d >= 0, ra[:, bk[np.clip(d, 0, 511)]], neg)
    db = p - (u[:, :256] - 128)
    strip_b = np.where((db >= 0) & (db < 128), rb[:, bk[np.clip(db, 0, 511)]], neg)

    w2 = I["w_in_2"][0]
    sizes = (768, 256, 1024, 64, 16, 768, 768, 128, 128, 768, 512, 512, 6144)
    cuts = np.cumsum(np.array(sizes))[:-1].tolist()
    a_q, a_ckv, i_q, i_k, i_w, a_g, b_q, b_k, b_v, b_g, c_q, c_g, mixg = np.split(w2, cuts, axis=1)
    perm = np.concatenate([np.r_[64 * j:64 * j + 64, 64 * (j + 6):64 * (j + 7)] for j in range(6)])
    w_in2 = tiles(np.concatenate([i_q, i_k, i_w, np.zeros((2048, 48), f32), a_ckv, c_q, c_g, b_k, b_v, b_q[:, perm], b_g[:, perm], a_q, a_g,
                                  mixg], axis=1))
    kv = I["w_kv_up_2"][0].reshape(2, 128, 12, 128)
    order = [x for h in range(6) for x in (h, 6 + h)]
    w_kv = kv[:, :, order].transpose(2, 1, 0, 3).reshape(6, 2, 128, 256).transpose(0, 2, 1, 3).reshape(6, 128, 512)

    arrays = {
        "cst": cst, "masks": masks,
        "xT": I["x"][0].T.reshape(16, 128, 512).transpose(1, 0, 2).reshape(128, 8192),
        "memT": I["mem_2"][0].T.reshape(16, 128, 256).transpose(1, 0, 2).reshape(128, 4096),
        "w_ada": I["w_ada"][0], "w_in": tiles(I["w_in"][0]), "w_out": tiles(np.roll(I["w_out"][0], 1024, axis=0)),
        "w_mem": tiles(I["w_mem_kv_2"][0]), "w_in2": w_in2, "w_kv": w_kv,
        "w_upa": tiles(I["w_up_a_2"][0], 6), "w_upb": tiles(I["w_up_b_2"][0][perm], 6),
        "w_upc": tiles(I["w_up_c_2"][0], 4), "w_o": tiles(I["w_o_2"][0]),
        "strip1": strip1, "strip_a": strip_a, "strip_b": strip_b,
    }
    arrays = {f"in_{k}": np.ascontiguousarray(v) for k, v in arrays.items()}
    nc = _bacc.Bacc("TRN2", target_bir_lowering=False, num_devices=1)
    io = {k[3:]: nc.dram_tensor(k, v.shape, mybir.dt.from_np(v.dtype), kind="ExternalInput").ap()
          for k, v in arrays.items()}
    io["out"] = nc.dram_tensor("out_0", (16, 128, 512), F32, kind="ExternalOutput").ap()
    for name, shape in (("x1s", (16, 128, 512)), ("mgs", (16, 128, 512))):
        io[name] = nc.dram_tensor(f"tmp_{name}", shape, F32, kind="Internal").ap()
    program(nc, io)
    r = _run(nc, [arrays], core_ids=[0])
    got = r.results[0]["out_0"]
    return np.ascontiguousarray(got.reshape(2048, 512).T).reshape(1, 512, 2048)
```
